# Optimizing a Trainium2 kernel written in Bass

```python
import jax, jax.numpy as jnp
from jax import lax
import numpy as np

D_MODEL = 1024
BATCH = 1
SEQ = 512
DEPTH = 1

RMS_EPS = 1e-6
N_MOD = 6
POOL_WINDOWS = (2, 4, 8, 16)
POOL_WIDTH = D_MODEL // 2
POOL_GROUP = POOL_WIDTH // len(POOL_WINDOWS)
MLA_HEADS = 8
QK_NOPE = D_MODEL // 16
QK_ROPE = D_MODEL // 32
V_HEAD = D_MODEL // 16
Q_LORA = D_MODEL // 4
KV_LORA = D_MODEL // 8
ROPE_THETA = 10000.0
Q_BLOCK = 128
MLA_WIDTH = MLA_HEADS * V_HEAD
IN_WIDTH = POOL_WIDTH + Q_LORA + KV_LORA + QK_ROPE + 2 * D_MODEL
PEER_HEADS = 8
PEER_KEYS = 128
PEER_EXPERTS = PEER_KEYS * PEER_KEYS
PEER_QUERY = 256
PEER_TOPK = 16
PEER_CHUNK = 128

kernel_name = "hybrid_pool_mla_peer_block"

def rmsnorm(x, gain):
    xf = x.astype(jnp.float32)
    y = xf * lax.rsqrt(jnp.mean(xf * xf, axis=-1, keepdims=True) + RMS_EPS)
    return (y * gain.astype(jnp.float32)).astype(x.dtype)

def rope_tables(seq, dtype):
    pos = jnp.arange(seq, dtype=jnp.float32)
    inv = 1.0 / (ROPE_THETA ** (jnp.arange(0, QK_ROPE, 2, dtype=jnp.float32) / QK_ROPE))
    ang = pos[:, None] * inv[None, :]
    ang = jnp.concatenate([ang, ang], axis=-1)
    return jnp.cos(ang).astype(dtype), jnp.sin(ang).astype(dtype)

def apply_rope(x, cos, sin):
    half = x.shape[-1] // 2
    rot = jnp.concatenate([-x[..., half:], x[..., :half]], axis=-1)
    return x * cos + rot * sin

def multiscale_pool(xp, w_group, scale):
    b, s, _ = xp.shape
    ng = len(POOL_WINDOWS)
    xg = xp.reshape(b, s, ng, POOL_GROUP).astype(jnp.float32)
    csp = jnp.concatenate([jnp.zeros((b, 1, ng, POOL_GROUP), jnp.float32),
                           jnp.cumsum(xg, axis=1)], axis=1)
    t = jnp.arange(s)
    pooled = []
    for g, w in enumerate(POOL_WINDOWS):
        upper = csp[:, 1:, g]
        lower = jnp.concatenate([jnp.zeros((b, w - 1, POOL_GROUP), jnp.float32),
                                 csp[:, :s - w + 1, g]], axis=1)
        count = jnp.minimum(t + 1, w).astype(jnp.float32)[None, :, None]
        pooled.append((upper - lower) / count)
    mixed = (jnp.stack(pooled, axis=2) - xg).astype(xp.dtype)
    mixed = jnp.einsum('bsgc,gcd->bsgd', mixed, w_group)
    return mixed.reshape(b, s, POOL_WIDTH) * scale

def causal_block_attention(q_nope, q_rope, k_nope, k_rope, v):
    s = q_nope.shape[1]
    sm_scale = (QK_NOPE + QK_ROPE) ** -0.5
    outs = []
    for i in range(s // Q_BLOCK):
        q0, q1 = i * Q_BLOCK, (i + 1) * Q_BLOCK
        sc = (jnp.einsum('bqhd,bkhd->bhqk', q_nope[:, q0:q1], k_nope[:, :q1])
              + jnp.einsum('bqhd,bkd->bhqk', q_rope[:, q0:q1], k_rope[:, :q1]))
        sc = sc.astype(jnp.float32) * sm_scale
        qpos = q0 + jnp.arange(Q_BLOCK)[:, None]
        kpos = jnp.arange(q1)[None, :]
        sc = jnp.where(kpos <= qpos, sc, -jnp.inf)
        p = jax.nn.softmax(sc, axis=-1).astype(v.dtype)
        outs.append(jnp.einsum('bhqk,bkhd->bqhd', p, v[:, :q1]))
    return jnp.concatenate(outs, axis=1)

def latent_attention(q_lat, kv_lat, k_rope, g_q_lat, w_q_up, g_kv_lat, w_kv_up):
    b, s, _ = q_lat.shape
    cos, sin = rope_tables(s, q_lat.dtype)
    q = (rmsnorm(q_lat, g_q_lat) @ w_q_up).reshape(b, s, MLA_HEADS, QK_NOPE + QK_ROPE)
    kv = (rmsnorm(kv_lat, g_kv_lat) @ w_kv_up).reshape(b, s, MLA_HEADS, QK_NOPE + V_HEAD)
    q_nope = q[..., :QK_NOPE]
    q_rope = apply_rope(q[..., QK_NOPE:], cos[:, None, :], sin[:, None, :])
    k_nope, v = kv[..., :QK_NOPE], kv[..., QK_NOPE:]
    k_rope = apply_rope(k_rope, cos, sin)
    o = causal_block_attention(q_nope, q_rope, k_nope, k_rope, v)
    return o.reshape(b, s, MLA_WIDTH)

def peer(xn, w_query, sub_keys1, sub_keys2, expert_u, expert_v):
    b, s, d = xn.shape
    half = PEER_QUERY // 2
    q = (xn @ w_query).reshape(b, s, PEER_HEADS, PEER_QUERY)
    s1 = jnp.einsum('bshd,hkd->bshk', q[..., :half], sub_keys1)
    s2 = jnp.einsum('bshd,hkd->bshk', q[..., half:], sub_keys2)
    v1, i1 = lax.top_k(s1, PEER_TOPK)
    v2, i2 = lax.top_k(s2, PEER_TOPK)
    cand = (v1[..., :, None] + v2[..., None, :]).reshape(b, s, PEER_HEADS, PEER_TOPK * PEER_TOPK)
    sc, ci = lax.top_k(cand, PEER_TOPK)
    eidx = (jnp.take_along_axis(i1, ci // PEER_TOPK, axis=-1) * PEER_KEYS
            + jnp.take_along_axis(i2, ci % PEER_TOPK, axis=-1))
    gate = jax.nn.softmax(sc.astype(jnp.float32), axis=-1).astype(xn.dtype)
    n_chunks = (b * s) // PEER_CHUNK
    xs = xn.reshape(n_chunks, PEER_CHUNK, d)
    es = eidx.reshape(n_chunks, PEER_CHUNK, PEER_HEADS, PEER_TOPK)
    gs = gate.reshape(n_chunks, PEER_CHUNK, PEER_HEADS, PEER_TOPK)

    def chunk(args):
        xc, ec, gc = args
        act = jnp.einsum('cd,chkd->chk', xc, expert_u[ec])
        w = gc * jax.nn.gelu(act)
        return jnp.einsum('chk,chkd->cd', w, expert_v[ec])

    y = lax.map(chunk, (xs, es, gs))
    return y.reshape(b, s, d)

def setup_inputs(seed: int = 0) -> dict:
    key = jax.random.key(seed)
    ks = jax.random.split(key, 24)
    L, D = DEPTH, D_MODEL

    def nrm(k, shape, scale):
        return jax.random.normal(k, shape, jnp.float32) * scale

    def gain(k, shape):
        return 1.0 + nrm(k, shape, 0.01)

    return {
        "x": nrm(ks[0], (BATCH, SEQ, D), 1.0),
        "c": nrm(ks[1], (BATCH, D), 1.0),
        "w_ada": nrm(ks[2], (L, D, N_MOD * D), 0.5 * D ** -0.5),
        "b_ada": nrm(ks[3], (L, N_MOD * D), 0.01),
        "g_pre1": gain(ks[4], (L, D)),
        "g_post1": gain(ks[5], (L, D)),
        "w_in": nrm(ks[6], (L, D, IN_WIDTH), D ** -0.5),
        "w_pool_group": nrm(ks[7], (L, len(POOL_WINDOWS), POOL_GROUP, POOL_GROUP), POOL_GROUP ** -0.5),
        "pool_scale": 1.0 + nrm(ks[8], (L, POOL_WIDTH), 0.1),
        "w_pool_o": nrm(ks[9], (L, POOL_WIDTH, D), POOL_WIDTH ** -0.5),
        "g_q_lat": gain(ks[10], (L, Q_LORA)),
        "w_q_up": nrm(ks[11], (L, Q_LORA, MLA_HEADS * (QK_NOPE + QK_ROPE)), Q_LORA ** -0.5),
        "g_kv_lat": gain(ks[12], (L, KV_LORA)),
        "w_kv_up": nrm(ks[13], (L, KV_LORA, MLA_HEADS * (QK_NOPE + V_HEAD)), KV_LORA ** -0.5),
        "w_mla_o": nrm(ks[14], (L, MLA_WIDTH, D), MLA_WIDTH ** -0.5),
        "w_out": nrm(ks[15], (L, D, D), D ** -0.5),
        "g_pre2": gain(ks[16], (L, D)),
        "g_post2": gain(ks[17], (L, D)),
        "w_query": nrm(ks[18], (L, D, PEER_HEADS * PEER_QUERY), D ** -0.5),
        "sub_keys1": nrm(ks[19], (L, PEER_HEADS, PEER_KEYS, PEER_QUERY // 2), (PEER_QUERY // 2) ** -0.5),
        "sub_keys2": nrm(ks[20], (L, PEER_HEADS, PEER_KEYS, PEER_QUERY // 2), (PEER_QUERY // 2) ** -0.5),
        "expert_u": nrm(ks[21], (L, PEER_EXPERTS, D), D ** -0.5),
        "expert_v": nrm(ks[22], (L, PEER_EXPERTS, D), 0.1),
    }

def reference(x, c, w_ada, b_ada, g_pre1, g_post1, w_in, w_pool_group, pool_scale, w_pool_o,
              g_q_lat, w_q_up, g_kv_lat, w_kv_up, w_mla_o, w_out, g_pre2, g_post2,
              w_query, sub_keys1, sub_keys2, expert_u, expert_v):
    h = x
    split_at = np.cumsum([POOL_WIDTH, Q_LORA, KV_LORA, QK_ROPE, D_MODEL]).tolist()
    for l in range(DEPTH):
        mod = jax.nn.silu(c) @ w_ada[l] + b_ada[l]
        shift1, scale1, gate1, shift2, scale2, gate2 = jnp.split(mod[:, None, :], N_MOD, axis=-1)

        xn = rmsnorm(h, g_pre1[l]) * (1.0 + scale1) + shift1
        proj = xn @ w_in[l]
        x_pool, q_lat, kv_lat, k_rope, gate_a, gate_b = jnp.split(proj, split_at, axis=-1)
        y_pool = multiscale_pool(x_pool, w_pool_group[l], pool_scale[l]) @ w_pool_o[l]
        y_mla = latent_attention(q_lat, kv_lat, k_rope, g_q_lat[l], w_q_up[l],
                                 g_kv_lat[l], w_kv_up[l]) @ w_mla_o[l]
        merged = jax.nn.sigmoid(gate_a) * y_pool + jax.nn.sigmoid(gate_b) * y_mla
        h = h + gate1 * rmsnorm(merged @ w_out[l], g_post1[l])

        xn2 = rmsnorm(h, g_pre2[l]) * (1.0 + scale2) + shift2
        y2 = peer(xn2, w_query[l], sub_keys1[l], sub_keys2[l], expert_u[l], expert_v[l])
        h = h + gate2 * rmsnorm(y2, g_post2[l])
    return h


_drawn_inputs = setup_inputs


def setup_inputs(seed=0):
    import zlib

    import numpy as np

    out = dict(_drawn_inputs(seed))
    spreads = {}
    factors = {'g_pre1': 3.284, 'g_post1': 3.279, 'g_q_lat': 8.0, 'g_kv_lat': 6.67, 'g_post2': 8.0}
    for name, (base, spread) in spreads.items():
        noise = np.random.default_rng([zlib.crc32(name.encode()), seed]).standard_normal(out[name].shape)
        drawn = base * np.exp(spread * noise) if base else spread * noise
        out[name] = __import__('jax').numpy.asarray(drawn.astype(out[name].dtype))
    for name, factor in factors.items():
        out[name] = (out[name] * factor).astype(out[name].dtype)
    return out
```

```python
from contextlib import ExitStack

import concourse.bass as bass
from concourse import mybir

F32 = mybir.dt.float32
F32R = mybir.dt.float32r
BF16 = mybir.dt.bfloat16
U32 = mybir.dt.uint32
ALU = mybir.AluOpType
ACT = mybir.ActivationFunctionType
AX_X = mybir.AxisListType.X

P = 128
SEQ, D = 512, 1024
NT, ND = SEQ // P, D // P
HALF = 512
POOL_G = 4
Q_LORA, KV_LORA, ROPE = 256, 128, 32
LAT = Q_LORA + KV_LORA + ROPE
HEADS, NOPE, VH = 8, 64, 64
QK = NOPE + ROPE
SM_SCALE = float(QK) ** -0.5
EPS = 1e-6
RH, TOPK, KEYS = 8, 16, 128
SIDES = 2 * RH
NEG = -3.0e38

KH = 2
ADA_FIRST, ADA_REST = 4, 8
B_IN = KH * ADA_FIRST
B_ADA2 = B_IN + KH * 2
B_MERGE = B_ADA2 + KH * ADA_REST
B_OUT = B_MERGE + 2 * 6
B_QUERY = B_OUT + 2 * KH
N_BLOCKS = B_QUERY + 4 * KH
RING = 4
SHIFT1, SCALE1, GATE1, SHIFT2, SCALE2, GATE2 = range(6)
ADA_ORDER = [SCALE1, SHIFT1, GATE1, SHIFT2, SCALE2, GATE2]

PAIRS = KEYS // 2
QUADS = 4
TURNS = P // (4 * QUADS)
UNITS = NT * HEADS
YJ = NT * 2
YB = 4


def build(nc, x, c_col, b_ada, g_pre1, g_post1, g_pre2, g_post2, g_q, g_kv, wstream, w_q_up, w_kv_up,
          w_group, pool_scale, keys, pool_band, rope_cos, rope_sin, ident_in, mask_in, iota_in,
          expert_u, expert_v, out):
    g_scratch = nc.dram_tensor("g_scratch", (KEYS, KEYS, SEQ), F32, kind="Internal").ap()
    base = (nc.sbuf_base + 31) // 32 * 32

    ctx = ExitStack()
    with ctx:
        def sem(name):
            return ctx.enter_context(nc.semaphore(name))

        def at(name, kb, shape, dt=F32):
            return nc.alloc_sbuf_tensor_at(name, shape, dt, offset=base + int(kb * 1024))

        bank = [ctx.enter_context(nc.psum_tensor(f"bank{i}", [P, HALF], F32)) for i in range(8)]

        h = at("h", 0, [P, NT, D])
        mod = at("mod", 16, [P, 6, D])
        ident = at("ident", 40, [P, P])
        iota = at("iota", 40.5, [P, P])
        stat = at("stat", 41, [P, 96])
        SS1, SSL, SSZ, SSH, SSY = 0, 8, 16, 24, 32
        iota_b = at("iota_b", 41.5, [P, P], BF16)
        xh = at("xh", 42, [P, ND, SEQ], F32R)
        xl = at("xl", 58, [P, ND, SEQ], F32R)
        qs = at("qs", 42, [P, 2, HEADS, QK])
        kc = at("kc", 48, [P, 2, HEADS, QK])
        latT = at("latT", 54, [P, 3, SEQ])
        rtmp = at("rtmp", 60, [P, 2, HEADS, ROPE])
        pr = at("pr", 42, [P, 2, HALF])
        prT = at("prT", 46, [P, 2, 4, P])
        mx = at("mx", 50, [P, 2, SEQ])
        sg = at("sg", 42, [P, 2, NT, HALF])
        lat = at("lat", 62, [P, NT, LAT])
        ccb = at("ccb", 68.5, [P, ND, P])
        csm = at("csm", 72.5, [P, 2, ND])
        nmax = at("nmax", 72.75, [P, UNITS])
        rsum = at("rsum", 72.875, [P, UNITS])
        rinv = at("rinv", 73, [P, UNITS])
        psc = at("psc", 73.125, [P, POOL_G])
        mask = at("mask", 73.5, [P, P])
        ring = at("ring", 74, [P, RING, 4, HALF])
        xT = at("xT", 106, [P, ND, SEQ])
        key_sb = at("key_sb", 122, [P, SIDES, KEYS])
        ga = at("ga", 130, [P, 2, D])
        gq = at("gq", 138, [P, Q_LORA])
        gkv = at("gkv", 139, [P, KV_LORA])
        rcos = at("rcos", 139.5, [P, NT, ROPE])
        rsin = at("rsin", 140, [P, NT, ROPE])
        wkvu = at("wkvu", 140.5, [P, HEADS * (NOPE + VH)])
        wqu = at("wqu", 144.5, [P, 2, HEADS * QK])
        oT = at("oT", 144.5, [P, 4, SEQ])
        ypT = at("ypT", 152.5, [P, POOL_G, SEQ])
        band = at("band", 160.5, [P, 3, POOL_G, P])
        wgr = at("wgr", 166.5, [P, POOL_G, P])
        xpool = at("xpool", 168.5, [P, NT, HALF])
        QT = at("QT", 160.5, [QK, HEADS, SEQ])
        KT = at("KT", 176.5, [QK, HEADS, SEQ])
        squares = at("squares", 176.5, [P, 4, D])
        xrow = at("xrow", 192.5, [P, 2, D])
        vv = at("vv", 192.5, [P, NT, HEADS, VH])
        osb = at("osb", 200.5, [P, HEADS, VH])
        zz = at("zz", 160.5, [P, NT, D])
        mT = at("mT", 176.5, [P, ND, SEQ])
        squares2 = at("squares2", 176.5, [P, 4, D])
        qT = at("qT", 130, [P, 4, SEQ])
        scores = at("scores", 138, [P, NT, SIDES, KEYS])
        top_v = at("top_v", 170, [P, SIDES, TOPK])
        top_i = at("top_i", 171, [P, SIDES, TOPK], U32)
        top_if = at("top_if", 172, [P, SIDES, TOPK])
        cand = at("cand", 173, [P, RH, TOPK, TOPK])
        best_v = at("best_v", 181, [P, RH, TOPK])
        best_c = at("best_c", 181.5, [P, RH, TOPK], U32)
        best_ab = at("best_ab", 182, [P, 2, RH, TOPK], U32)
        best_abf = at("best_abf", 183, [P, 2, RH, TOPK])
        picks = at("picks", 184, [P, 3, RH * TOPK])
        gexp = at("gexp", 185.5, [P, 2, RH, TOPK])
        gsum = at("gsum", 186.5, [P, 2, RH])
        rest = at("rest", 187, [P, 2, P])
        part_b = at("part_b", 188, [P, 2, P], BF16)
        picksT = at("picksT", 189, [P, 5, SEQ])
        hot = at("hot", 16, [P, QUADS, 4, 4, P], BF16)
        gate_t = at("gate_t", 74, [P, KEYS, P])
        raw_u = at("raw_u", 74, [P, 2, 2, D])
        raw_v = at("raw_v", 90, [P, 2, 2, D])
        u_part = at("u_part", 106, [P, 2, 2, ND, P], F32R)
        v_part = at("v_part", 122, [P, 2, 2, 2, D], F32R)
        w_part = at("w_part", 154, [P, 2, 2, 2, SEQ], F32R)
        w_full = at("w_full", 170, [P, 2, SEQ])
        gel = at("gel", 174, [P, 2, SEQ])
        g_in = at("g_in", 178, [P, 2, 2, SEQ])
        yacc = at("yacc", 186, [P, NT, D])
        squares3 = at("squares3", 74, [P, 4, D])

        s_c = sem("c_loaded")
        s_x = sem("x_loaded")
        s_g1 = sem("gains1_loaded")
        s_g2 = sem("gains2_loaded")
        s_tab = sem("tables_loaded")
        s_pool_in = sem("pool_tables_loaded")
        s_key = sem("keys_loaded")
        s_ring = [sem(f"block_loaded{i}") for i in range(RING)]
        s_half = sem("half_used")
        s_sig_c = sem("sigmoid_c")
        s_ccb = sem("silu_c_spread")
        s_ada = sem("ada_chunk")
        s_mod = sem("mod_chunk")
        s_fold = sem("gains_folded")
        s_sq = sem("squares_summed")
        s_var = sem("variance")
        s_std = sem("std")
        s_xn = sem("x_normed")
        s_xtr = sem("x_transposed")
        s_xT = sem("xT_ready")
        s_xp = sem("xpool_psum")
        s_xps = sem("xpool_ready")
        s_lp = sem("lat_psum")
        s_lat = sem("lat_ready")
        s_mxp = sem("pooled_psum")
        s_mx = sem("pooled_ready")
        s_yp = sem("grouped_psum")
        s_ypT = sem("ypT_ready")
        s_ln = sem("lat_normed")
        s_ltr = sem("lat_transposed")
        s_latT = sem("latT_ready")
        s_qup = sem("q_up_psum")
        s_kvup = sem("kv_up_psum")
        s_qs = sem("q_rows")
        s_kc = sem("k_rows_read")
        s_rot = sem("rows_rotated")
        s_qtr = sem("q_transposed")
        s_ktr = sem("k_transposed")
        s_QT = sem("QT_ready")
        s_KT = sem("KT_ready")
        s_sc = sem("att_scores")
        s_max = sem("att_max")
        s_exp = sem("att_exp")
        s_ptr = sem("att_p_transposed")
        s_prT = sem("att_prT_ready")
        s_pv = sem("att_pv")
        s_o = sem("att_o_rows")
        s_otr = sem("att_o_transposed")
        s_oT = sem("oT_ready")
        s_gp = sem("gates_psum")
        s_sg = sem("sigmoids_ready")
        s_ya = sem("mixer_a_psum")
        s_yb = sem("mixer_b_psum")
        s_yad = sem("mixer_a_read")
        s_mg = sem("merged")
        s_mtr = sem("merged_transposed")
        s_mT = sem("mT_ready")
        s_z = sem("out_psum")
        s_zs = sem("out_rows")
        s_h1 = sem("h_updated")
        s_xl = sem("x_low_ready")
        s_q = sem("query_psum")
        s_qT = sem("query_ready")
        s_scr = sem("scores_psum")
        s_scs = sem("scores_ready")
        s_bv = sem("picks_shifted")
        s_ge = sem("picks_exp")
        s_pk = sem("picks_ready")
        s_pkt = sem("picks_transposed")
        s_hot = sem("onehots")
        s_gmm = sem("gate_products")
        s_gev = sem("gate_read")
        s_gout = sem("gate_stored")
        s_ul = [sem(f"u_loaded{i}") for i in range(2)]
        s_vl = [sem(f"v_loaded{i}") for i in range(2)]
        s_gl = [sem(f"g_loaded{i}") for i in range(2)]
        s_uhi = sem("u_high")
        s_ulo = sem("u_low")
        s_vhi = sem("v_high")
        s_vlo = sem("v_low")
        s_act = sem("expert_act")
        s_gelu = sem("expert_gelu")
        s_w = sem("expert_w")
        s_whi = sem("w_high")
        s_wlo = sem("w_low")
        s_y = sem("y_piece")
        s_yd = sem("y_added")
        s_fin = sem("out_ready")
        s_out = sem("out_stored")
        s_chain = sem("dve_chain")
        s_achain = sem("act_chain")

        freed = []
        halves = 0
        for q in range(ADA_FIRST):
            halves += 1
            freed += [(s_half, halves), (s_ada, q + 1)]
        for s in (s_xp, s_lp):
            halves += 1
            freed += [(s_half, halves), (s, NT)]
        for q in range(ADA_REST):
            halves += 1
            freed += [(s_half, halves), (s_ada, ADA_FIRST + q + 1)]
        for c in range(2):
            for g in range(2):
                halves += 1
                freed += [(s_half, halves), (s_gp, NT * (2 * c + g + 1))]
            freed += [(s_ya, NT * (c + 1)), (s_yb, NT * (c + 1))]
        for c in range(2):
            halves += 1
            freed += [(s_half, halves), (s_z, NT * (c + 1))]
        for n in range(4):
            halves += 1
            freed += [(s_half, halves), (s_q, 4 * (n + 1))]
        assert len(freed) == N_BLOCKS

        block = ctx.enter_context(nc.Block())

        @block.sync
        def _(sp):
            sp.dma_start(csm[:, 0, :], c_col).then_inc(s_c, 16)
            for i in range(NT):
                sp.dma_start(h[:, i, :], x[i * P:(i + 1) * P, :]).then_inc(s_x, 16)
            sp.dma_start(ident[:], ident_in).then_inc(s_x, 16)
            for j in range(N_BLOCKS):
                if j >= RING:
                    sp.wait_ge(*freed[j - RING])
                sp.dma_start(ring[:, j % RING, :, :], wstream[j].rearrange("p (k n) -> p k n", k=4)
                             ).then_inc(s_ring[j % RING], 16)
                if j == RING - 1:
                    for v in ADA_ORDER:
                        sp.dma_start(mod[:, v, :], b_ada[v:v + 1, :].to_broadcast([P, D])).then_inc(s_g1, 16)
                    sp.dma_start(ga[:, 0, :], g_pre1.to_broadcast([P, D])).then_inc(s_g1, 16)
                    sp.dma_start(ga[:, 1, :], g_post1.to_broadcast([P, D])).then_inc(s_g1, 16)
                    for dst, src in ((band, pool_band), (wgr, w_group), (psc, pool_scale)):
                        sp.dma_start(dst[:], src).then_inc(s_pool_in, 16)
                    sp.dma_start(gq[:], g_q.to_broadcast([P, Q_LORA])).then_inc(s_tab, 16)
                    sp.dma_start(gkv[:], g_kv.to_broadcast([P, KV_LORA])).then_inc(s_tab, 16)
                    for dst, src in ((rcos, rope_cos), (rsin, rope_sin), (wkvu, w_kv_up), (wqu, w_q_up),
                                     (mask, mask_in), (iota, iota_in)):
                        sp.dma_start(dst[:], src).then_inc(s_tab, 16)
                    sp.dma_start(key_sb[:], keys).then_inc(s_key, 16)
                if j == B_ADA2 + 2 * RING:
                    sp.wait_ge(s_fold, 2)
                    sp.dma_start(ga[:, 0, :], g_pre2.to_broadcast([P, D])).then_inc(s_g2, 16)
                    sp.dma_start(ga[:, 1, :], g_post2.to_broadcast([P, D])).then_inc(s_g2, 16)
            for i in range(NT):
                sp.wait_ge(s_gev, QUADS + QUADS * TURNS * (i + 1))
                sp.dma_start(g_scratch[:, :, i * P:(i + 1) * P].rearrange("a b t -> b a t"), gate_t[:]
                             ).then_inc(s_gout, 16)
            sp.wait_ge(s_gout, 16 * NT)

            def load(n, s):
                sp.dma_start(raw_u[:, s, :, :], expert_u[n]).then_inc(s_ul[s], 16)
                sp.dma_start(raw_v[:, s, :, :], expert_v[n]).then_inc(s_vl[s], 16)
                sp.dma_start(g_in[:, s, :, :], g_scratch[n * 2:n * 2 + 2, :, :].rearrange("a b t -> b a t")
                             ).then_inc(s_gl[s], 16)

            for n in range(2):
                load(n, n)
            with sp.Fori(0, PAIRS // 2 - 1) as it:
                for s in range(2):
                    sp.wait_ge(s_ulo, it * 4 + (2 * s + 2))
                    sp.wait_ge(s_vlo, it * 4 + (2 * s + 2))
                    sp.wait_ge(s_w, it * 4 + (2 * s + 2))
                    n = it * 2 + (2 + s)
                    sp.dma_start(raw_u[:, s, :, :], expert_u[bass.ds(n, 1)].rearrange("o p e n -> (o p) e n")
                                 ).then_inc(s_ul[s], 16)
                    sp.dma_start(raw_v[:, s, :, :], expert_v[bass.ds(n, 1)].rearrange("o p e n -> (o p) e n")
                                 ).then_inc(s_vl[s], 16)
                    sp.dma_start(g_in[:, s, :, :], g_scratch[bass.ds(n * 2, 2), :, :].rearrange("a b t -> b a t")
                                 ).then_inc(s_gl[s], 16)
            for i in range(NT):
                sp.wait_ge(s_fin, i + 1)
                sp.dma_start(out[i * P:(i + 1) * P, :], h[:, i, :]).then_inc(s_out, 16)
            sp.wait_ge(s_out, 16 * NT)

        @block.scalar
        def _(act):
            a = nc.scalar
            act.wait_ge(s_c, 16)
            a.activation(csm[:, 1, :], csm[:, 0, :], ACT.Sigmoid).then_inc(s_sig_c, 1)

            act.wait_ge(s_x, 16 * (NT + 1))
            for i in range(NT):
                last = a.activation(squares[:, i, :], h[:, i, :], ACT.Square, accum_out=stat[:, SS1 + i:SS1 + i + 1])
            last.then_inc(s_sq, 1)
            act.wait_ge(s_var, 1)
            a.activation(stat[:, SS1:SS1 + 4], stat[:, SS1:SS1 + 4], ACT.Sqrt).then_inc(s_std, 1)

            def read_xT(i, n):
                act.wait_ge(s_xtr, n)
                for b in range(2):
                    last = a.activation(xT[:, 4 * b:4 * b + 4, i * P:(i + 1) * P],
                                        bank[4 + 2 * (i % 2) + b][:].rearrange("p (k t) -> p k t", k=4), ACT.Copy)
                return last

            for i in range(NT):
                read_xT(i, i + 1).then_inc(s_xT, 1)
            act.wait_ge(s_pool_in, 48)
            for i in range(NT):
                act.wait_ge(s_xp, i + 1)
                a.activation(xpool[:, i, :], bank[i][:], ACT.Copy).then_inc(s_xps, 1)
            for i in range(NT):
                act.wait_ge(s_lat, i + 1)
                a.activation(squares[:, i, 0:Q_LORA], lat[:, i, 0:Q_LORA], ACT.Square,
                             accum_out=stat[:, SSL + i:SSL + i + 1])
                last = a.activation(squares[:, i, Q_LORA:Q_LORA + KV_LORA], lat[:, i, Q_LORA:Q_LORA + KV_LORA],
                                    ACT.Square, accum_out=stat[:, SSL + NT + i:SSL + NT + i + 1])
            last.then_inc(s_sq, 1)
            act.wait_ge(s_var, 2)
            a.activation(stat[:, SSL:SSL + 2 * NT], stat[:, SSL:SSL + 2 * NT], ACT.Sqrt).then_inc(s_std, 1)
            for g in range(POOL_G):
                act.wait_ge(s_yp, g + 1)
                a.activation(ypT[:, g, :], bank[2 + g % 2][:], ACT.Copy, scale=psc[:, g:g + 1]).then_inc(s_ypT, 1)
            for i in range(NT):
                act.wait_ge(s_ltr, i + 1)
                a.activation(latT[:, :, i * P:(i + 1) * P],
                             bank[4 + i][:, 0:3 * P].rearrange("p (k t) -> p k t", k=3), ACT.Copy).then_inc(s_latT, 1)

            def q_rows(i):
                act.wait_ge(s_qup, i + 1)
                if i >= 2:
                    act.wait_ge(s_qtr, i - 1)
                for b in range(2):
                    last = a.activation(qs[:, i % 2, 4 * b:4 * b + 4, :],
                                        bank[b][:, 0:4 * QK].rearrange("p (h n) -> p h n", h=4), ACT.Copy,
                                        scale=SM_SCALE)
                last.then_inc(s_qs, 1)

            def read_QT(i):
                act.wait_ge(s_qtr, i + 1)
                for b in range(2):
                    last = a.activation(QT[:, 4 * b:4 * b + 4, i * P:(i + 1) * P],
                                        bank[4 + b][0:QK, :].rearrange("p (h t) -> p h t", h=4), ACT.Copy)
                last.then_inc(s_QT, 1)

            q_rows(0)
            for i in range(NT):
                if i + 1 < NT:
                    q_rows(i + 1)
                read_QT(i)

            for u in range(UNITS + 4):
                if u < UNITS:
                    i = u // HEADS
                    n = (i + 1) * P
                    act.wait_ge(s_max, u + 1)
                    if u >= 2:
                        act.wait_ge(s_ptr, u - 1)
                    a.activation(pr[:, u % 2, 0:n], bank[u % 2][:, 0:n], ACT.Exp, bias=nmax[:, u:u + 1],
                                 accum_out=rsum[:, u:u + 1]).then_inc(s_exp, 1)
                if 1 <= u <= UNITS:
                    v = u - 1
                    n = (v // HEADS + 1)
                    act.wait_ge(s_ptr, v + 1)
                    if v >= 2:
                        act.wait_ge(s_pv, v - 1)
                    a.activation(prT[:, v % 2, 0:n, :], bank[2 + v % 2][:, 0:n * P].rearrange("p (k t) -> p k t", k=n),
                                 ACT.Copy).then_inc(s_prT, 1)
                if u >= HEADS + 2 and (u - HEADS - 2) % HEADS == 0:
                    i = (u - HEADS - 2) // HEADS
                    act.wait_ge(s_otr, i + 1)
                    a.activation(oT[:, :, i * P:(i + 1) * P], bank[5][:].rearrange("p (k t) -> p k t", k=4),
                                 ACT.Copy).then_inc(s_oT, 1)

            for c in range(2):
                for g in range(2):
                    for i in range(NT):
                        act.wait_ge(s_gp, NT * (2 * c + g) + i + 1)
                        if c:
                            act.wait_ge(s_mg, i + 1)
                        a.activation(sg[:, g, i, :], bank[4 * g + i][:], ACT.Sigmoid).then_inc(s_sg, 1)
            for i in range(NT):
                act.wait_ge(s_mtr, i + 1)
                for b in range(2):
                    last = a.activation(mT[:, 4 * b:4 * b + 4, i * P:(i + 1) * P],
                                        bank[2 * (i % 2) + b][:].rearrange("p (k t) -> p k t", k=4), ACT.Copy)
                last.then_inc(s_mT, 1)
            for c in range(2):
                for i in range(NT):
                    act.wait_ge(s_z, NT * c + i + 1)
                    a.activation(zz[:, i, c * HALF:(c + 1) * HALF], bank[4 * c + i][:], ACT.Copy).then_inc(s_zs, 1)
            act.wait_ge(s_zs, 2 * NT)
            for i in range(NT):
                last = a.activation(squares2[:, i, :], zz[:, i, :], ACT.Square, accum_out=stat[:, SSZ + i:SSZ + i + 1])
            last.then_inc(s_sq, 1)
            act.wait_ge(s_var, 3)
            a.activation(stat[:, SSZ:SSZ + 4], stat[:, SSZ:SSZ + 4], ACT.Sqrt).then_inc(s_std, 1)
            for i in range(NT):
                act.wait_ge(s_h1, i + 1)
                last = a.activation(squares2[:, i, :], h[:, i, :], ACT.Square, accum_out=stat[:, SSH + i:SSH + i + 1])
            last.then_inc(s_sq, 1)
            act.wait_ge(s_var, 4)
            a.activation(stat[:, SSH:SSH + 4], stat[:, SSH:SSH + 4], ACT.Sqrt).then_inc(s_std, 1)
            for i in range(NT):
                read_xT(i, NT + i + 1)
                for b in range(2):
                    last = a.activation(xh[:, 4 * b:4 * b + 4, i * P:(i + 1) * P],
                                        bank[4 + 2 * (i % 2) + b][:].rearrange("p (k t) -> p k t", k=4), ACT.Copy)
                last.then_inc(s_xT, 1)
            for n in range(4):
                for m in range(4):
                    act.wait_ge(s_q, 4 * n + m + 1)
                    if n:
                        act.wait_ge(s_scr, 4 * (n - 1) + m + 1)
                    a.activation(qT[:, m, :], bank[m][:], ACT.Copy).then_inc(s_qT, 1)
            for i in range(NT):
                act.wait_ge(s_bv, i + 1)
                a.activation(gexp[:, 1, :, :], gexp[:, 0, :, :], ACT.Exp).then_inc(s_ge, 1)
                if i == 0:
                    a.sem_inc(s_gev, QUADS)
                else:
                    act.wait_ge(s_gout, 16 * i)
                with act.Fori(0, TURNS) as it:
                    for q in range(QUADS):
                        act.wait_ge(s_gmm, it * QUADS + (QUADS + i * TURNS * QUADS + q + 1))
                        a.activation(gate_t[:, :, bass.ds(it * (4 * QUADS) + 4 * q, 4)],
                                     bank[q][:].rearrange("p (t k) -> p k t", t=4), ACT.Copy).then_inc(s_gev, 1)

            def split_u(n_loads, s):
                act.wait_ge(s_ul[s], n_loads)
                for e in range(2):
                    a.activation(u_part[:, e, 0, :, :].rearrange("p k n -> p (k n)"), raw_u[:, s, e, :],
                                 ACT.Copy).then_inc(s_uhi, 1)

            def split_v(n_loads, s):
                act.wait_ge(s_vl[s], n_loads)
                for e in range(2):
                    a.activation(v_part[:, s, e, 0, :], raw_v[:, s, e, :], ACT.Copy).then_inc(s_vhi, 1)

            def gelu(n, s):
                for e in range(2):
                    act.wait_ge(s_act, n * 2 + (e + 1))
                    a.activation(gel[:, e, :], bank[2 * s + e][:], ACT.Gelu_apprx_tanh).then_inc(s_gelu, 1)
                    act.wait_ge(s_w, n * 2 + (e + 1))
                    a.activation(w_part[:, s, e, 0, :], w_full[:, e, :], ACT.Copy).then_inc(s_whi, 1)

            split_u(16, 0)
            split_v(16, 0)
            gelu(0, 0)
            with act.Fori(0, PAIRS // 2 - 1) as it:
                split_u(it * 16 + 16, 1)
                act.wait_ge(s_yd, it * (2 * YJ) + YB)
                split_v(it * 16 + 16, 1)
                gelu(it * 2 + 1, 1)
                split_u(it * 16 + 32, 0)
                act.wait_ge(s_y, it * (2 * YJ) + YJ)
                split_v(it * 16 + 32, 0)
                gelu(it * 2 + 2, 0)
            split_u(8 * PAIRS, 1)
            act.wait_ge(s_y, YJ * (PAIRS - 2))
            split_v(8 * PAIRS, 1)
            gelu(PAIRS - 1, 1)
            act.wait_ge(s_yd, YB + YJ * PAIRS)
            for i in range(NT):
                last = a.activation(squares3[:, i, :], yacc[:, i, :], ACT.Square, accum_out=stat[:, SSY + i:SSY + i + 1])
            last.then_inc(s_sq, 1)
            act.wait_ge(s_var, 5)
            a.activation(stat[:, SSY:SSY + 4], stat[:, SSY:SSY + 4], ACT.Sqrt).then_inc(s_std, 1)

        @block.vector
        def _(dve):
            v = nc.vector
            count = [0]

            def link(ins):
                count[0] += 1
                ins.then_inc(s_chain, 1)
                dve.wait_ge(s_chain, count[0])

            def rstd(col, n, width, stage):
                dve.wait_ge(s_sq, stage)
                for k, w in enumerate(width):
                    last = v.tensor_scalar(stat[:, col + n * k:col + n * (k + 1)], stat[:, col + n * k:col + n * (k + 1)],
                                           1.0 / w, EPS, ALU.mult, ALU.add)
                last.then_inc(s_var, 1)
                dve.wait_ge(s_std, stage)
                m = n * len(width)
                link(v.reciprocal(stat[:, col:col + m], stat[:, col:col + m]))

            def scaled(o, rows, r, g):
                return v.scalar_tensor_tensor(o, rows, r, g, ALU.mult, ALU.mult)

            dve.wait_ge(s_sig_c, 1)
            link(v.tensor_tensor(csm[:, 1, :], csm[:, 0, :], csm[:, 1, :], ALU.mult))
            v.tensor_copy(ccb[:], csm[:, 1, :].unsqueeze(2).to_broadcast([P, ND, P])).then_inc(s_ccb, 1)
            dve.wait_ge(s_g1, 16 * 8)

            def ada(q):
                dve.wait_ge(s_ada, q + 1)
                b = q if q < ADA_FIRST else 6 + q % 2
                m = mod[:, ADA_ORDER[q // 2], (q % 2) * HALF:(q % 2 + 1) * HALF]
                v.tensor_tensor(m, bank[b][:], m, ALU.add).then_inc(s_mod, 1)
                if q % 2 == 0:
                    return
                vec = ADA_ORDER[q // 2]
                if vec in (SCALE1, SCALE2):
                    if vec == SCALE2:
                        dve.wait_ge(s_g2, 32)
                    dve.wait_ge(s_mod, q + 1)
                    v.scalar_tensor_tensor(mod[:, vec, :], mod[:, vec, :], 1.0, ga[:, 0, :], ALU.add,
                                           ALU.mult).then_inc(s_fold, 1)
                if vec in (GATE1, GATE2):
                    dve.wait_ge(s_mod, q + 1)
                    v.tensor_tensor(mod[:, vec, :], mod[:, vec, :], ga[:, 1, :], ALU.mult).then_inc(s_fold, 1)

            for q in range(ADA_FIRST):
                ada(q)
            rstd(SS1, NT, [D], 1)
            dve.wait_ge(s_fold, 1)
            dve.wait_ge(s_mod, ADA_FIRST)
            for i in range(NT):
                if i >= 2:
                    dve.wait_ge(s_xtr, i - 1)
                link(scaled(xrow[:, i % 2, :], h[:, i, :], stat[:, SS1 + i:SS1 + i + 1], mod[:, SCALE1, :]))
                v.tensor_tensor(xrow[:, i % 2, :], xrow[:, i % 2, :], mod[:, SHIFT1, :], ALU.add).then_inc(s_xn, 1)
            for i in range(NT):
                dve.wait_ge(s_lp, i + 1)
                v.tensor_copy(lat[:, i, :], bank[4 + i][:, 0:LAT]).then_inc(s_lat, 1)
            dve.wait_ge(s_tab, 16 * 8)
            v.tensor_copy(iota_b[:], iota[:])
            for g in range(POOL_G):
                dve.wait_ge(s_mxp, g + 1)
                if g >= 2:
                    dve.wait_ge(s_yp, g - 1)
                v.tensor_copy(mx[:, g % 2, :], bank[g % 2][:]).then_inc(s_mx, 1)
            rstd(SSL, NT, [Q_LORA, KV_LORA], 2)
            for i in range(NT):
                scaled(lat[:, i, 0:Q_LORA], lat[:, i, 0:Q_LORA], stat[:, SSL + i:SSL + i + 1], gq[:])
                scaled(lat[:, i, Q_LORA:Q_LORA + KV_LORA], lat[:, i, Q_LORA:Q_LORA + KV_LORA],
                       stat[:, SSL + NT + i:SSL + NT + i + 1], gkv[:]).then_inc(s_ln, 1)
            HR = ROPE // 2

            def rotate(rows, i, nh):
                def tab(t, lo, hi):
                    return t[:, i:i + 1, lo:hi].to_broadcast([P, nh, hi - lo])
                t1, t2 = rtmp[:, 0, 0:nh, :], rtmp[:, 1, 0:nh, :]
                v.tensor_tensor(t1, rows, tab(rcos, 0, ROPE), ALU.mult)
                v.tensor_tensor(t2[:, :, 0:HR], rows[:, :, HR:ROPE], tab(rsin, 0, HR), ALU.mult)
                link(v.tensor_tensor(t2[:, :, HR:ROPE], rows[:, :, 0:HR], tab(rsin, HR, ROPE), ALU.mult))
                return v.tensor_tensor(rows, t1, t2, ALU.add)

            def kv_rows(i):
                dve.wait_ge(s_kvup, i + 1)
                if i >= 2:
                    dve.wait_ge(s_ktr, i - 1)
                for b in range(2):
                    kv = bank[2 + b][:].rearrange("p (h n) -> p h n", h=4)
                    v.tensor_copy(kc[:, i % 2, 4 * b:4 * b + 4, 0:NOPE], kv[:, :, 0:NOPE])
                    last = v.tensor_copy(vv[:, i, 4 * b:4 * b + 4, :], kv[:, :, NOPE:NOPE + VH])
                last.then_inc(s_kc, 1)
                if i:
                    dve.wait_ge(s_rot, i)
                link(rotate(lat[:, i:i + 1, Q_LORA + KV_LORA:LAT], i, 1))
                v.tensor_copy(kc[:, i % 2, :, NOPE:QK],
                              lat[:, i:i + 1, Q_LORA + KV_LORA:LAT].to_broadcast([P, HEADS, ROPE]))
                dve.wait_ge(s_qs, i + 1)
                rotate(qs[:, i % 2, :, NOPE:QK], i, HEADS).then_inc(s_rot, 1)

            def read_KT(i):
                dve.wait_ge(s_ktr, i + 1)
                for b in range(2):
                    last = v.tensor_copy(KT[:, 4 * b:4 * b + 4, i * P:(i + 1) * P],
                                         bank[6 + b][0:QK, :].rearrange("p (h t) -> p h t", h=4))
                last.then_inc(s_KT, 1)

            kv_rows(0)
            for i in range(NT):
                if i + 1 < NT:
                    kv_rows(i + 1)
                read_KT(i)

            for u in range(UNITS + 4):
                if u < UNITS:
                    i = u // HEADS
                    dve.wait_ge(s_sc, u + 1)
                    diag = bank[u % 2][:, i * P:(i + 1) * P]
                    link(v.tensor_tensor(diag, diag, mask[:], ALU.add))
                    v.tensor_reduce(nmax[:, u:u + 1], bank[u % 2][:, 0:(i + 1) * P], AX_X, ALU.max,
                                    negate=True).then_inc(s_max, 1)
                if u >= HEADS + 1 and (u - HEADS - 1) % HEADS == 0:
                    i = (u - HEADS - 1) // HEADS
                    dve.wait_ge(s_exp, HEADS * (i + 1))
                    link(v.reciprocal(rinv[:, 8 * i:8 * i + 8], rsum[:, 8 * i:8 * i + 8]))
                    dve.wait_ge(s_pv, HEADS * (i + 1))
                    if i:
                        dve.wait_ge(s_otr, i)
                    v.tensor_tensor(osb[:], bank[4][:].rearrange("p (h n) -> p h n", h=HEADS),
                                    rinv[:, 8 * i:8 * i + 8].unsqueeze(2).to_broadcast([P, HEADS, VH]),
                                    ALU.mult).then_inc(s_o, 1)
                if u % 4 == 3 and u // 4 < ADA_REST:
                    ada(ADA_FIRST + u // 4)

            for c in range(2):
                for g, s in ((0, s_ya), (1, s_yb)):
                    for i in range(NT):
                        dve.wait_ge(s, NT * c + i + 1)
                        dve.wait_ge(s_sg, 2 * NT * c + NT * g + i + 1)
                        last = v.tensor_tensor(sg[:, g, i, :], bank[4 * g + i][:], sg[:, g, i, :], ALU.mult)
                        if g == 0:
                            last.then_inc(s_yad, 1)
                        else:
                            link(last)
                            dve.wait_ge(s_yad, NT * c + i + 1)
                            v.tensor_tensor(zz[:, i, c * HALF:(c + 1) * HALF], sg[:, 0, i, :], sg[:, 1, i, :],
                                            ALU.add).then_inc(s_mg, 1)
            rstd(SSZ, NT, [D], 3)
            dve.wait_ge(s_fold, 4)
            for i in range(NT):
                link(scaled(zz[:, i, :], zz[:, i, :], stat[:, SSZ + i:SSZ + i + 1], mod[:, GATE1, :]))
                v.tensor_tensor(h[:, i, :], h[:, i, :], zz[:, i, :], ALU.add).then_inc(s_h1, 1)
            dve.wait_ge(s_h1, NT)
            rstd(SSH, NT, [D], 4)
            for i in range(NT):
                link(scaled(zz[:, i, :], h[:, i, :], stat[:, SSH + i:SSH + i + 1], mod[:, SCALE2, :]))
                v.tensor_tensor(zz[:, i, :], zz[:, i, :], mod[:, SHIFT2, :], ALU.add).then_inc(s_xn, 1)
            for i in range(NT):
                dve.wait_ge(s_xT, NT + i + 1)
                v.tensor_tensor(xl[:, :, i * P:(i + 1) * P], xT[:, :, i * P:(i + 1) * P],
                                xh[:, :, i * P:(i + 1) * P].bitcast(F32), ALU.subtract).then_inc(s_xl, 1)
            for n in range(4):
                for m in range(4):
                    dve.wait_ge(s_scr, 4 * n + m + 1)
                    side = (m % 2) * RH + 2 * n + m // 2
                    v.tensor_copy(scores[:, :, side, :], bank[4 + m][:].rearrange("p (i k) -> p i k", i=NT)
                                  ).then_inc(s_scs, 1)
            dve.wait_ge(s_scs, SIDES)

            def top16(vals, idx, src, n):
                for part in range(2):
                    lo, hi = 8 * part, 8 * part + 8
                    for k in range(n):
                        last = v.max(vals(k)[:, lo:hi], src(k))
                    link(last)
                    for k in range(n):
                        last = v.max_index(idx(k)[:, lo:hi], vals(k)[:, lo:hi], src(k))
                    link(last)
                    if part == 0:
                        for k in range(n):
                            last = v.match_replace(src(k), vals(k)[:, lo:hi], src(k), NEG)
                        link(last)

            for i in range(NT):
                top16(lambda k: top_v[:, k, :], lambda k: top_i[:, k, :], lambda k: scores[:, i, k, :], SIDES)
                v.tensor_copy(top_if[:], top_i[:])
                link(v.tensor_tensor(cand[:], top_v[:, 0:RH, :].unsqueeze(3).to_broadcast([P, RH, TOPK, TOPK]),
                                     top_v[:, RH:SIDES, :].unsqueeze(2).to_broadcast([P, RH, TOPK, TOPK]), ALU.add))
                top16(lambda k: best_v[:, k, :], lambda k: best_c[:, k, :],
                      lambda k: cand[:, k, :, :].rearrange("p a b -> p (a b)"), RH)
                v.tensor_tensor(gexp[:, 0, :, :], best_v[:], best_v[:, :, 0:1].to_broadcast([P, RH, TOPK]),
                                ALU.subtract).then_inc(s_bv, 1)
                v.tensor_scalar(best_ab[:, 0, :, :], best_c[:], 4, None, ALU.logical_shift_right)
                link(v.tensor_scalar(best_ab[:, 1, :, :], best_c[:], TOPK - 1, None, ALU.bitwise_and))
                link(v.tensor_copy(best_abf[:], best_ab[:]))
                for s in range(2):
                    link(v.tensor_tensor(cand[:], best_abf[:, s, :, :].unsqueeze(3).to_broadcast([P, RH, TOPK, TOPK]),
                                         iota[:, 0:TOPK].unsqueeze(1).unsqueeze(1).to_broadcast([P, RH, TOPK, TOPK]),
                                         ALU.is_equal))
                    link(v.tensor_tensor(cand[:], cand[:], top_if[:, s * RH:(s + 1) * RH, :].unsqueeze(2)
                                         .to_broadcast([P, RH, TOPK, TOPK]), ALU.mult))
                    link(v.tensor_reduce(picks[:, s, :], cand[:].rearrange("p h k a -> p (h k) a"), AX_X, ALU.add))
                dve.wait_ge(s_ge, i + 1)
                link(v.tensor_reduce(gsum[:, 0, :], gexp[:, 1, :, :], AX_X, ALU.add))
                link(v.reciprocal(gsum[:, 1, :], gsum[:, 0, :]))
                v.tensor_tensor(picks[:, 2, :].rearrange("p (h k) -> p h k", h=RH), gexp[:, 1, :, :],
                                gsum[:, 1, :].unsqueeze(2).to_broadcast([P, RH, TOPK]), ALU.mult).then_inc(s_pk, 1)
                dve.wait_ge(s_pkt, i + 1)
                cols = slice(i * P, (i + 1) * P)
                v.tensor_copy(picksT[:, 0, cols], bank[4][:, 0:P])
                v.tensor_copy(picksT[:, 1, cols], bank[4][:, P:2 * P])
                g = bank[4][:, 2 * P:3 * P]
                link(v.tensor_copy(part_b[:, 0, :], g))
                link(v.tensor_copy(picksT[:, 2, cols], part_b[:, 0, :]))
                link(v.tensor_tensor(rest[:, 0, :], g, picksT[:, 2, cols], ALU.subtract))
                link(v.tensor_copy(part_b[:, 1, :], rest[:, 0, :]))
                link(v.tensor_copy(picksT[:, 3, cols], part_b[:, 1, :]))
                link(v.tensor_tensor(picksT[:, 4, cols], rest[:, 0, :], picksT[:, 3, cols], ALU.subtract))
                with dve.Fori(0, TURNS) as it:
                    for q in range(QUADS):
                        dve.wait_ge(s_gmm, it * QUADS + (i * TURNS * QUADS + q + 1))
                        for t in range(4):
                            def col(r):
                                return picksT[:, r, bass.ds(it * (4 * QUADS) + (i * P + 4 * q + t), 1)]
                            v.tensor_scalar(hot[:, q, t, 0, :], iota_b[:], col(1), None, ALU.is_equal)
                            for part in range(3):
                                last = v.tensor_scalar(hot[:, q, t, 1 + part, :], iota_b[:], col(0), col(2 + part),
                                                       ALU.is_equal, ALU.mult)
                        last.then_inc(s_hot, 1)

            def low(parts, raw, s, e):
                if parts is u_part:
                    hi, lo = (u_part[:, e, k, :, :].rearrange("p k n -> p (k n)") for k in (0, 1))
                else:
                    hi, lo = (v_part[:, s, e, k, :] for k in (0, 1))
                return v.tensor_tensor(lo, raw[:, s, e, :], hi.bitcast(F32), ALU.subtract)

            def split_u(n, s):
                for e in range(2):
                    dve.wait_ge(s_uhi, n * 2 + (e + 1))
                    low(u_part, raw_u, s, e).then_inc(s_ulo, 1)

            def split_v(n, s):
                for e in range(2):
                    dve.wait_ge(s_vhi, n * 2 + (e + 1))
                    low(v_part, raw_v, s, e).then_inc(s_vlo, 1)

            def weigh(n, s, n_loads):
                dve.wait_ge(s_gl[s], n_loads)
                for e in range(2):
                    dve.wait_ge(s_gelu, n * 2 + (e + 1))
                    v.tensor_tensor(w_full[:, e, :], gel[:, e, :], g_in[:, s, e, :], ALU.mult).then_inc(s_w, 1)
                    dve.wait_ge(s_whi, n * 2 + (e + 1))
                    v.tensor_tensor(w_part[:, s, e, 1, :], w_full[:, e, :], w_part[:, s, e, 0, :].bitcast(F32),
                                    ALU.subtract).then_inc(s_wlo, 1)

            def add_y(n):
                for j in range(YJ):
                    dve.wait_ge(s_y, n * YJ + (j + 1))
                    o = yacc[:, j // 2, (j % 2) * HALF:(j % 2 + 1) * HALF]
                    v.tensor_tensor(o, bank[4 + j % YB][:], o, ALU.add).then_inc(s_yd, 1)

            dve.wait_ge(s_gmm, QUADS * (1 + NT * TURNS))
            link(v.memset(yacc[:], 0.0))
            v.sem_inc(s_yd, YB)
            split_u(0, 0)
            split_v(0, 0)
            weigh(0, 0, 16)
            with dve.Fori(0, PAIRS // 2 - 1) as it:
                split_u(it * 2 + 1, 1)
                split_v(it * 2 + 1, 1)
                weigh(it * 2 + 1, 1, it * 16 + 16)
                split_u(it * 2 + 2, 0)
                add_y(it * 2)
                split_v(it * 2 + 2, 0)
                weigh(it * 2 + 2, 0, it * 16 + 32)
                add_y(it * 2 + 1)
            split_u(PAIRS - 1, 1)
            split_v(PAIRS - 1, 1)
            weigh(PAIRS - 1, 1, 8 * PAIRS)
            add_y(PAIRS - 2)
            add_y(PAIRS - 1)
            rstd(SSY, NT, [D], 5)
            for i in range(NT):
                link(scaled(yacc[:, i, :], yacc[:, i, :], stat[:, SSY + i:SSY + i + 1], mod[:, GATE2, :]))
                v.tensor_tensor(h[:, i, :], h[:, i, :], yacc[:, i, :], ALU.add).then_inc(s_fin, 1)

        @block.tensor
        def _(pe):
            def matmul(o, l, r, first, last):
                return nc.tensor.matmul(o, l, r, start=bool(first), stop=bool(last))

            def loaded(j):
                pe.wait_ge(s_ring[j % RING], 16 * (j // RING + 1))

            def ada_piece(q, kh, k):
                j = (KH * q if q < ADA_FIRST else B_ADA2 + KH * (q - ADA_FIRST)) + kh
                b = q if q < ADA_FIRST else 6 + q % 2
                if k == 0:
                    loaded(j)
                    if kh == 0 and q >= ADA_FIRST + 2:
                        pe.wait_ge(s_mod, q - 1)
                last = matmul(bank[b][:], ccb[:, 4 * kh + k, :], ring[:, j % RING, k, :], kh + k == 0, kh and k == 3)
                if k == 3:
                    last.then_inc(s_ada if kh else s_half, 1)

            pe.wait_ge(s_ccb, 1)
            for q in range(ADA_FIRST):
                for kh in range(KH):
                    for k in range(4):
                        ada_piece(q, kh, k)

            def transpose_rows(rows, i, banks):
                for k in range(ND):
                    last = nc.tensor.transpose(bank[banks + k // 4][:, (k % 4) * P:(k % 4 + 1) * P],
                                               rows[:, k * P:(k + 1) * P], ident[:])
                return last

            pe.wait_ge(s_x, 16 * (NT + 1))
            for i in range(NT):
                pe.wait_ge(s_xn, i + 1)
                if i >= 2:
                    pe.wait_ge(s_xT, i - 1)
                transpose_rows(xrow[:, i % 2, :], i, 4 + 2 * (i % 2)).then_inc(s_xtr, 1)

            def project(j0, src, b0, signal, n=HALF):
                for kh in range(KH):
                    loaded(j0 + kh)
                    for i in range(NT):
                        for k in range(4):
                            last = matmul(bank[b0 + i][:, 0:n], src[:, 4 * kh + k, i * P:(i + 1) * P],
                                          ring[:, (j0 + kh) % RING, k, 0:n], kh + k == 0, kh and k == 3)
                        if kh:
                            last.then_inc(signal, 1)
                    if not kh:
                        last.then_inc(s_half, 1)

            pe.wait_ge(s_mod, ADA_FIRST)
            pe.wait_ge(s_xT, NT)
            project(B_IN, xT, 0, s_xp)
            project(B_IN + KH, xT, 4, s_lp, LAT)

            pe.wait_ge(s_xps, NT)
            pe.wait_ge(s_pool_in, 48)

            def pool(g):
                if g >= 2:
                    pe.wait_ge(s_mx, g - 1)
                for i in range(NT):
                    o = bank[g % 2][:, i * P:(i + 1) * P]
                    last = matmul(o, xpool[:, i, g * P:(g + 1) * P], band[:, 0 if i == 0 else 1, g, :], True, i == 0)
                    if i:
                        last = matmul(o, xpool[:, i - 1, g * P:(g + 1) * P], band[:, 2, g, :], False, True)
                last.then_inc(s_mxp, 1)

            def group_map(g):
                pe.wait_ge(s_mx, g + 1)
                if g >= 2:
                    pe.wait_ge(s_ypT, g - 1)
                matmul(bank[2 + g % 2][:], wgr[:, g, :], mx[:, g % 2, :], True, True).then_inc(s_yp, 1)

            pool(0)
            for g in range(POOL_G):
                if g + 1 < POOL_G:
                    pool(g + 1)
                group_map(g)

            for i in range(NT):
                pe.wait_ge(s_ln, i + 1)
                for k in range(3):
                    last = nc.tensor.transpose(bank[4 + i][:, k * P:(k + 1) * P], lat[:, i, k * P:(k + 1) * P], ident[:])
                last.then_inc(s_ltr, 1)
            pe.wait_ge(s_tab, 16 * 8)
            pe.wait_ge(s_ypT, POOL_G)

            def lift(i):
                tok = slice(i * P, (i + 1) * P)
                pe.wait_ge(s_latT, i + 1)
                if i:
                    pe.wait_ge(s_qs, i)
                for b in range(2):
                    for k in range(2):
                        last = matmul(bank[b][:, 0:4 * QK], latT[:, k, tok], wqu[:, k, b * 4 * QK:(b + 1) * 4 * QK],
                                      k == 0, k == 1)
                last.then_inc(s_qup, 1)
                if i:
                    pe.wait_ge(s_kc, i)
                for b in range(2):
                    last = matmul(bank[2 + b][:], latT[:, 2, tok], wkvu[:, b * HALF:(b + 1) * HALF], True, True)
                last.then_inc(s_kvup, 1)

            def turn(i):
                pe.wait_ge(s_rot, i + 1)
                if i:
                    pe.wait_ge(s_QT, i)
                else:
                    pe.wait_ge(s_latT, NT)
                for hd in range(HEADS):
                    last = nc.tensor.transpose(bank[4 + hd // 4][0:QK, (hd % 4) * P:(hd % 4 + 1) * P],
                                               qs[:, i % 2, hd, :], ident[:])
                last.then_inc(s_qtr, 1)
                if i:
                    pe.wait_ge(s_KT, i)
                for hd in range(HEADS):
                    last = nc.tensor.transpose(bank[6 + hd // 4][0:QK, (hd % 4) * P:(hd % 4 + 1) * P],
                                               kc[:, i % 2, hd, :], ident[:])
                last.then_inc(s_ktr, 1)

            lift(0)
            for i in range(NT):
                if i + 1 < NT:
                    lift(i + 1)
                turn(i)

            pe.wait_ge(s_QT, NT)
            pe.wait_ge(s_KT, NT)
            for u in range(UNITS + 4):
                if u < UNITS:
                    i, hd = divmod(u, HEADS)
                    if u >= 2:
                        pe.wait_ge(s_exp, u - 1)
                    matmul(bank[u % 2][:, 0:(i + 1) * P], QT[:, hd, i * P:(i + 1) * P], KT[:, hd, 0:(i + 1) * P],
                           True, True).then_inc(s_sc, 1)
                if 1 <= u <= UNITS:
                    w = u - 1
                    pe.wait_ge(s_exp, w + 1)
                    if w >= 2:
                        pe.wait_ge(s_prT, w - 1)
                    for k in range(w // HEADS + 1):
                        last = nc.tensor.transpose(bank[2 + w % 2][:, k * P:(k + 1) * P],
                                                   pr[:, w % 2, k * P:(k + 1) * P], ident[:])
                    last.then_inc(s_ptr, 1)
                if 2 <= u <= UNITS + 1:
                    w = u - 2
                    i, hd = divmod(w, HEADS)
                    pe.wait_ge(s_prT, w + 1)
                    if hd == 0 and i:
                        pe.wait_ge(s_o, i)
                    for k in range(i + 1):
                        last = matmul(bank[4][:, hd * VH:(hd + 1) * VH], prT[:, w % 2, k, :], vv[:, k, hd, :],
                                      k == 0, k == i)
                    last.then_inc(s_pv, 1)
                if u >= HEADS + 2 and (u - HEADS - 2) % HEADS == 0:
                    i = (u - HEADS - 2) // HEADS
                    pe.wait_ge(s_o, i + 1)
                    if i:
                        pe.wait_ge(s_oT, i)
                    for k in range(4):
                        last = nc.tensor.transpose(bank[5][:, k * P:(k + 1) * P],
                                                   osb[:, 2 * k:2 * k + 2, :].rearrange("p h n -> p (h n)"), ident[:])
                    last.then_inc(s_otr, 1)
                if u < 4 * ADA_REST:
                    for piece in (2 * (u % 4), 2 * (u % 4) + 1):
                        ada_piece(ADA_FIRST + u // 4, piece // 4, piece % 4)

            pe.wait_ge(s_oT, NT)
            pe.wait_ge(s_mod, ADA_FIRST + ADA_REST)
            for c in range(2):
                if c:
                    pe.wait_ge(s_mg, NT)
                project(B_MERGE + 6 * c, xT, 0, s_gp)
                project(B_MERGE + 6 * c + 2, xT, 4, s_gp)
                for g, (src, signal) in enumerate(((ypT, s_ya), (oT, s_yb))):
                    j = B_MERGE + 6 * c + 4 + g
                    loaded(j)
                    for i in range(NT):
                        pe.wait_ge(s_sg, 2 * NT * c + NT * g + i + 1)
                        for k in range(4):
                            last = matmul(bank[4 * g + i][:], src[:, k, i * P:(i + 1) * P], ring[:, j % RING, k, :],
                                          k == 0, k == 3)
                        last.then_inc(signal, 1)
            for i in range(NT):
                pe.wait_ge(s_mg, NT + i + 1)
                if i >= 2:
                    pe.wait_ge(s_mT, i - 1)
                if i == 0:
                    pe.wait_ge(s_yad, 2 * NT)
                transpose_rows(zz[:, i, :], i, 2 * (i % 2)).then_inc(s_mtr, 1)
            pe.wait_ge(s_mT, NT)
            for c in range(2):
                project(B_OUT + KH * c, mT, 4 * c, s_z)
            pe.wait_ge(s_zs, 2 * NT)
            for i in range(NT):
                pe.wait_ge(s_xn, NT + i + 1)
                if i >= 2:
                    pe.wait_ge(s_xT, NT + i - 1)
                transpose_rows(zz[:, i, :], i, 4 + 2 * (i % 2)).then_inc(s_xtr, 1)

            pe.wait_ge(s_xT, 2 * NT)
            pe.wait_ge(s_key, 16)

            def score(n):
                for m in range(4):
                    side = (m % 2) * RH + 2 * n + m // 2
                    pe.wait_ge(s_qT, 4 * n + m + 1)
                    if n:
                        pe.wait_ge(s_scs, 4 * (n - 1) + m + 1)
                    for i in range(NT):
                        last = matmul(bank[4 + m][:, i * P:(i + 1) * P], qT[:, m, i * P:(i + 1) * P],
                                      key_sb[:, side, :], True, True)
                    last.then_inc(s_scr, 1)

            for n in range(4):
                for kh in range(KH):
                    j = B_QUERY + KH * n + kh
                    loaded(j)
                    for m in range(4):
                        if n and not kh:
                            pe.wait_ge(s_qT, 4 * (n - 1) + m + 1)
                        for k in range(4):
                            last = matmul(bank[m][:], ring[:, j % RING, k, m * P:(m + 1) * P], xT[:, 4 * kh + k, :],
                                          kh + k == 0, kh and k == 3)
                        if kh:
                            last.then_inc(s_q, 1)
                    if not kh:
                        last.then_inc(s_half, 1)
                score(n)

            for i in range(NT):
                pe.wait_ge(s_pk, i + 1)
                for r in range(3):
                    last = nc.tensor.transpose(bank[4][:, r * P:(r + 1) * P], picks[:, r, :], ident[:])
                last.then_inc(s_pkt, 1)
                if i == 0:
                    nc.tensor.sem_inc(s_gmm, QUADS)
                with pe.Fori(0, TURNS) as it:
                    for q in range(QUADS):
                        turn_no = it * QUADS + (i * TURNS * QUADS + q + 1)
                        pe.wait_ge(s_hot, turn_no)
                        pe.wait_ge(s_gev, turn_no)
                        for t in range(4):
                            for part in range(3):
                                last = matmul(bank[q][:, t * P:(t + 1) * P], hot[:, q, t, 0, :],
                                              hot[:, q, t, 1 + part, :], part == 0, part == 2)
                        last.then_inc(s_gmm, 1)

            pe.wait_ge(s_xl, NT)
            pe.wait_ge(s_gev, QUADS * (1 + NT * TURNS))

            def activate(n, s):
                for e in range(2):
                    pe.wait_ge(s_ulo, n * 2 + (e + 1))
                    b = bank[2 * s + e]
                    for k in range(ND):
                        matmul(b[:], u_part[:, e, 0, k, :], xh[:, k, :], k == 0, False)
                        matmul(b[:], u_part[:, e, 0, k, :], xl[:, k, :], False, False)
                        last = matmul(b[:], u_part[:, e, 1, k, :], xh[:, k, :], False, k == ND - 1)
                    last.then_inc(s_act, 1)

            def combine(n, s):
                pe.wait_ge(s_wlo, n * 2 + 2)
                pe.wait_ge(s_vlo, n * 2 + 2)
                for j in range(YJ):
                    pe.wait_ge(s_yd, n * YJ + (j + 1))
                    b = bank[4 + j % YB]
                    tok = slice((j // 2) * P, (j // 2 + 1) * P)
                    col = slice((j % 2) * HALF, (j % 2 + 1) * HALF)
                    for e in range(2):
                        matmul(b[:], w_part[:, s, e, 0, tok], v_part[:, s, e, 0, col], e == 0, False)
                        matmul(b[:], w_part[:, s, e, 0, tok], v_part[:, s, e, 1, col], False, False)
                        last = matmul(b[:], w_part[:, s, e, 1, tok], v_part[:, s, e, 0, col], False, e == 1)
                    last.then_inc(s_y, 1)

            activate(0, 0)
            with pe.Fori(0, PAIRS // 2 - 1) as it:
                activate(it * 2 + 1, 1)
                combine(it * 2, 0)
                activate(it * 2 + 2, 0)
                combine(it * 2 + 1, 1)
            activate(PAIRS - 1, 1)
            combine(PAIRS - 2, 0)
            combine(PAIRS - 1, 1)


def kernel(**inputs):
    import numpy as np
    import concourse.bacc as bacc
    from concourse.bass_utils import run_bass_kernel_spmd

    a = {k: np.ascontiguousarray(v) for k, v in inputs.items()}
    f = np.float32

    def blocks(w, n_chunks=None):
        rows, cols = w.shape
        b = w.reshape(rows // HALF, 4, P, cols // HALF, HALF).transpose(3, 0, 2, 1, 4)
        return b.reshape(cols // HALF, rows // HALF, P, 4 * HALF)

    def stream():
        ada = blocks(a["w_ada"][0])
        w_in = a["w_in"][0]
        pool_w = blocks(w_in[:, 0:HALF])
        lat_w = np.zeros((D, HALF), w_in.dtype)
        lat_w[:, 0:LAT] = w_in[:, HALF:HALF + LAT]
        gates = blocks(w_in[:, HALF + LAT:])
        pool_o, mla_o = blocks(a["w_pool_o"][0]), blocks(a["w_mla_o"][0])
        order = [2 * vec + half for vec in ADA_ORDER for half in range(2)]
        parts = [ada[q] for q in order[:ADA_FIRST]] + [pool_w[0], blocks(lat_w)[0]]
        parts += [ada[q] for q in order[ADA_FIRST:]]
        for c in range(2):
            parts += [gates[c], gates[2 + c], pool_o[c], mla_o[c]]
        parts += list(blocks(a["w_out"][0])) + list(blocks(a["w_query"][0]))
        return np.concatenate(parts, axis=0)

    def tables():
        band = np.zeros((P, 3, POOL_G, P), f)
        for g, w in enumerate((2, 4, 8, 16)):
            for t in range(P):
                for s in range(max(0, t - w + 1), t + 1):
                    band[s, 0, g, t] = f(1) / f(min(t + 1, w))
                    band[s, 1, g, t] = f(1) / f(w)
                for s in range(t - w + 1, 0):
                    band[P + s, 2, g, t] = f(1) / f(w)
                band[t, 0:2, g, t] -= f(1)
        inv = f(1) / (f(10000.0) ** (np.arange(0, ROPE, 2, dtype=f) / f(ROPE)))
        ang = np.arange(SEQ, dtype=f)[:, None] * inv[None, :].astype(f)
        cos, sin = np.cos(ang).astype(f), np.sin(ang).astype(f)
        cos = np.concatenate([cos, cos], 1).reshape(NT, P, ROPE).transpose(1, 0, 2)
        sin = np.concatenate([-sin, sin], 1).reshape(NT, P, ROPE).transpose(1, 0, 2)
        mask = np.where(np.arange(P)[None, :] <= np.arange(P)[:, None], f(0), f(-1e30)).astype(f)
        return band, cos, sin, mask

    band, cos, sin, mask = tables()
    k12 = np.concatenate([a["sub_keys1"][0], a["sub_keys2"][0]], axis=0)
    ins = [
        ("x", a["x"][0]),
        ("c_col", a["c"][0].reshape(ND, P).T),
        ("b_ada", a["b_ada"][0].reshape(6, D)),
        ("g_pre1", a["g_pre1"]), ("g_post1", a["g_post1"]), ("g_pre2", a["g_pre2"]), ("g_post2", a["g_post2"]),
        ("g_q", a["g_q_lat"]), ("g_kv", a["g_kv_lat"]),
        ("wstream", stream()),
        ("w_q_up", a["w_q_up"][0].reshape(2, P, HEADS * QK).transpose(1, 0, 2)),
        ("w_kv_up", a["w_kv_up"][0]),
        ("w_group", a["w_pool_group"][0].transpose(1, 0, 2)),
        ("pool_scale", a["pool_scale"][0].reshape(POOL_G, P).T),
        ("keys", k12.transpose(2, 0, 1)),
        ("pool_band", band), ("rope_cos", cos), ("rope_sin", sin),
        ("ident", np.eye(P, dtype=f)), ("mask", mask),
        ("iota", np.broadcast_to(np.arange(P, dtype=f), (P, P))),
        ("expert_u", a["expert_u"][0].reshape(PAIRS, 2, P, ND, P).transpose(0, 4, 1, 3, 2).reshape(PAIRS, P, 2, D)),
        ("expert_v", a["expert_v"][0].reshape(PAIRS, 2, P, D).transpose(0, 2, 1, 3)),
    ]
    nc = bacc.Bacc("TRN2", target_bir_lowering=False, num_devices=1)
    arrays, args = {}, []
    for name, v in ins:
        v = np.ascontiguousarray(v)
        arrays[f"in_{name}"] = v
        args.append(nc.dram_tensor(f"in_{name}", v.shape, mybir.dt.from_np(v.dtype), kind="ExternalInput").ap())
    args.append(nc.dram_tensor("out_0", (SEQ, D), F32, kind="ExternalOutput").ap())
    build(nc, *args)
    r = run_bass_kernel_spmd(nc, [arrays], core_ids=[0])
    return r.results[0]["out_0"].reshape(1, SEQ, D)
```

```python
from contextlib import ExitStack

import concourse.bass as bass
from concourse import mybir

F32 = mybir.dt.float32
F32R = mybir.dt.float32r
BF16 = mybir.dt.bfloat16
U32 = mybir.dt.uint32
ALU = mybir.AluOpType
ACT = mybir.ActivationFunctionType
AX_X = mybir.AxisListType.X

P = 128
SEQ, D = 512, 1024
NT, ND = SEQ // P, D // P
HALF = 512
POOL_G = 4
Q_LORA, KV_LORA, ROPE = 256, 128, 32
LAT = Q_LORA + KV_LORA + ROPE
HEADS, NOPE, VH = 8, 64, 64
QK = NOPE + ROPE
SM_SCALE = float(QK) ** -0.5
EPS = 1e-6
RH, TOPK, KEYS = 8, 16, 128
SIDES = 2 * RH
NEG = -3.0e38

KH = 2
ADA_FIRST, ADA_REST = 4, 8
B_IN = KH * ADA_FIRST
B_ADA2 = B_IN + KH * 2
B_MERGE = B_ADA2 + KH * ADA_REST
B_OUT = B_MERGE + 2 * 6
B_QUERY = B_OUT + 2 * KH
N_BLOCKS = B_QUERY + 4 * KH
RING = 4
SHIFT1, SCALE1, GATE1, SHIFT2, SCALE2, GATE2 = range(6)
ADA_ORDER = [SCALE1, SHIFT1, GATE1, SHIFT2, SCALE2, GATE2]

PAIRS = KEYS // 2
QUADS = 4
TURNS = P // (4 * QUADS)
E_FIRST, E_BETWEEN, E_BESIDE, E_TAIL = 4, 2, TURNS // 2, 4
EARLY = E_FIRST + (NT - 1) * E_BETWEEN + NT * E_BESIDE + E_TAIL
FULL = PAIRS - EARLY
UNITS = NT * HEADS
YJ = NT * 2
YB = 4


def build(nc, x, c_col, b_ada, g_pre1, g_post1, g_pre2, g_post2, g_q, g_kv, wstream, w_q_up, w_kv_up,
          w_group, pool_scale, keys, pool_band, rope_cos, rope_sin, ident_in, mask_in, iota_in,
          expert_u, expert_v, out):
    g_scratch = nc.dram_tensor("g_scratch", (KEYS, KEYS, SEQ), F32, kind="Internal").ap()
    h_scratch = nc.dram_tensor("h_scratch", (P, NT * D), F32, kind="Internal").ap()
    act_scratch = nc.dram_tensor("act_scratch", (EARLY, P, 2 * SEQ), F32, kind="Internal").ap()
    base = (nc.sbuf_base + 31) // 32 * 32

    ctx = ExitStack()
    with ctx:
        def sem(name):
            return ctx.enter_context(nc.semaphore(name))

        def at(name, kb, shape, dt=F32):
            return nc.alloc_sbuf_tensor_at(name, shape, dt, offset=base + int(kb * 1024))

        bank = [ctx.enter_context(nc.psum_tensor(f"bank{i}", [P, HALF], F32)) for i in range(8)]

        h = at("h", 0, [P, NT, D])
        mod = at("mod", 16, [P, 6, D])
        ident = at("ident", 40, [P, P])
        iota = at("iota", 40.5, [P, P])
        stat = at("stat", 41, [P, 96])
        SS1, SSL, SSZ, SSH, SSY = 0, 8, 16, 24, 32
        xh = at("xh", 42, [P, ND, SEQ], F32R)
        xl = at("xl", 58, [P, ND, SEQ], F32R)
        qs = at("qs", 42, [P, 2, HEADS, QK])
        kc = at("kc", 48, [P, 2, HEADS, QK])
        latT = at("latT", 54, [P, 3, SEQ])
        rtmp = at("rtmp", 60, [P, 2, HEADS, ROPE])
        pr = at("pr", 42, [P, 2, HALF])
        prT = at("prT", 46, [P, 2, 4, P])
        mx = at("mx", 50, [P, 2, SEQ])
        sg = at("sg", 42, [P, 2, NT, HALF])
        lat = at("lat", 62, [P, NT, LAT])
        ccb = at("ccb", 68.5, [P, ND, P])
        csm = at("csm", 72.5, [P, 2, ND])
        nmax = at("nmax", 72.75, [P, UNITS])
        rsum = at("rsum", 72.875, [P, UNITS])
        rinv = at("rinv", 73, [P, UNITS])
        psc = at("psc", 73.125, [P, POOL_G])
        mask = at("mask", 73.5, [P, P])
        ring = at("ring", 74, [P, RING, 4, HALF])
        xT = at("xT", 106, [P, ND, SEQ])
        key_sb = at("key_sb", 122, [P, SIDES, KEYS])
        ga = at("ga", 130, [P, 2, D])
        gq = at("gq", 138, [P, Q_LORA])
        gkv = at("gkv", 139, [P, KV_LORA])
        rcos = at("rcos", 139.5, [P, NT, ROPE])
        rsin = at("rsin", 140, [P, NT, ROPE])
        wkvu = at("wkvu", 140.5, [P, HEADS * (NOPE + VH)])
        wqu = at("wqu", 144.5, [P, 2, HEADS * QK])
        oT = at("oT", 144.5, [P, 4, SEQ])
        ypT = at("ypT", 152.5, [P, POOL_G, SEQ])
        band = at("band", 160.5, [P, 3, POOL_G, P])
        wgr = at("wgr", 166.5, [P, POOL_G, P])
        xpool = at("xpool", 168.5, [P, NT, HALF])
        QT = at("QT", 160.5, [QK, HEADS, SEQ])
        KT = at("KT", 176.5, [QK, HEADS, SEQ])
        squares = at("squares", 176.5, [P, 4, D])
        xrow = at("xrow", 192.5, [P, 2, D])
        vv = at("vv", 192.5, [P, NT, HEADS, VH])
        osb = at("osb", 200.5, [P, HEADS, VH])
        zz = at("zz", 160.5, [P, NT, D])
        mT = at("mT", 176.5, [P, ND, SEQ])
        squares2 = at("squares2", 176.5, [P, 4, D])
        qT = at("qT", 130, [P, 4, SEQ])
        scores = at("scores", 138, [P, NT, SIDES, KEYS])
        cand = at("cand", 138, [P, RH, TOPK, TOPK])
        best_v = at("best_v", 146, [P, RH, TOPK])
        best_c = at("best_c", 146.5, [P, RH, TOPK], U32)
        best_ab = at("best_ab", 147, [P, 2, RH, TOPK], U32)
        best_abf = at("best_abf", 148, [P, 2, RH, TOPK])
        picks = at("picks", 149, [P, 3, RH * TOPK])
        gexp = at("gexp", 150.5, [P, 2, RH, TOPK])
        gsum = at("gsum", 151.5, [P, 2, RH])
        picksT = at("picksT", 152, [P, 3, SEQ])
        top_v = at("top_v", 195, [P, NT, SIDES, TOPK])
        top_if = at("top_if", 199, [P, NT, SIDES, TOPK])
        top_i = at("top_i", 203, [P, 2, 4, TOPK], U32)
        hot = at("hot", 16, [P, QUADS, 4, 2, P])
        gate_t = at("gate_t", 74, [P, KEYS, P])
        raw_u = at("raw_u", 0, [P, 2, 2, D])
        u_part = at("u_part", 171, [P, 2, 2, ND, P], F32R)
        gel = at("gel", 187, [P, 2, 2, SEQ])
        raw_v = at("raw_v", 74, [P, 2, 2, D])
        v_part = at("v_part", 90, [P, 2, 2, 2, D], F32R)
        w_part = at("w_part", 122, [P, 2, 2, 2, SEQ], F32R)
        yacc = at("yacc", 138, [P, NT, D])
        g_in = at("g_in", 154, [P, 2, 2, SEQ])
        w_full = at("w_full", 162, [P, 2, SEQ])
        act_in = at("act_in", 195, [P, 2, 2, SEQ])
        squares3 = at("squares3", 74, [P, 4, D])

        s_c = sem("c_loaded")
        s_x = sem("x_loaded")
        s_g1 = sem("gains1_loaded")
        s_g2 = sem("gains2_loaded")
        s_tab = sem("tables_loaded")
        s_pool_in = sem("pool_tables_loaded")
        s_key = sem("keys_loaded")
        s_ring = [sem(f"block_loaded{i}") for i in range(RING)]
        s_half = sem("half_used")
        s_sig_c = sem("sigmoid_c")
        s_ccb = sem("silu_c_spread")
        s_ada = sem("ada_chunk")
        s_mod = sem("mod_chunk")
        s_fold = sem("gains_folded")
        s_sq = sem("squares_summed")
        s_var = sem("variance")
        s_std = sem("std")
        s_xn = sem("x_normed")
        s_xtr = sem("x_transposed")
        s_xT = sem("xT_ready")
        s_xp = sem("xpool_psum")
        s_xps = sem("xpool_ready")
        s_lp = sem("lat_psum")
        s_lat = sem("lat_ready")
        s_mxp = sem("pooled_psum")
        s_mx = sem("pooled_ready")
        s_yp = sem("grouped_psum")
        s_ypT = sem("ypT_ready")
        s_ln = sem("lat_normed")
        s_ltr = sem("lat_transposed")
        s_latT = sem("latT_ready")
        s_qup = sem("q_up_psum")
        s_kvup = sem("kv_up_psum")
        s_qs = sem("q_rows")
        s_kc = sem("k_rows_read")
        s_rot = sem("rows_rotated")
        s_qtr = sem("q_transposed")
        s_ktr = sem("k_transposed")
        s_QT = sem("QT_ready")
        s_KT = sem("KT_ready")
        s_sc = sem("att_scores")
        s_max = sem("att_max")
        s_exp = sem("att_exp")
        s_ptr = sem("att_p_transposed")
        s_prT = sem("att_prT_ready")
        s_pv = sem("att_pv")
        s_o = sem("att_o_rows")
        s_otr = sem("att_o_transposed")
        s_oT = sem("oT_ready")
        s_gp = sem("gates_psum")
        s_sg = sem("sigmoids_ready")
        s_ya = sem("mixer_a_psum")
        s_yb = sem("mixer_b_psum")
        s_yad = sem("mixer_a_read")
        s_mg = sem("merged")
        s_mtr = sem("merged_transposed")
        s_mT = sem("mT_ready")
        s_z = sem("out_psum")
        s_zs = sem("out_rows")
        s_h1 = sem("h_updated")
        s_xl = sem("x_low_ready")
        s_q = sem("query_psum")
        s_qT = sem("query_ready")
        s_scr = sem("scores_psum")
        s_scs = sem("scores_ready")
        s_top = sem("side_searched")
        s_bv = sem("picks_shifted")
        s_ge = sem("picks_exp")
        s_pk = sem("picks_ready")
        s_pkt = sem("picks_transposed")
        s_hot = sem("onehots")
        s_gmm = sem("gate_products")
        s_gev = sem("gate_read")
        s_gout = sem("gate_stored")
        s_hout = sem("h_stored")
        s_hin = sem("h_back")
        s_spill = [sem(f"early_gelu_stored{i}") for i in range(2)]
        s_al = [sem(f"early_gelu_back{i}") for i in range(2)]
        s_ul = [sem(f"u_loaded{i}") for i in range(2)]
        s_vl = [sem(f"v_loaded{i}") for i in range(2)]
        s_gl = [sem(f"g_loaded{i}") for i in range(2)]
        s_uhi = sem("u_high")
        s_ulo = sem("u_low")
        s_vhi = sem("v_high")
        s_vlo = sem("v_low")
        s_act = sem("expert_act")
        s_gelu = sem("expert_gelu")
        s_w = sem("expert_w")
        s_whi = sem("w_high")
        s_wlo = sem("w_low")
        s_y = sem("y_piece")
        s_yd = sem("y_added")
        s_fin = sem("out_ready")
        s_out = sem("out_stored")
        s_chain = sem("dve_chain")
        s_achain = sem("act_chain")

        freed = []
        halves = 0
        for q in range(ADA_FIRST):
            halves += 1
            freed += [(s_half, halves), (s_ada, q + 1)]
        for s in (s_xp, s_lp):
            halves += 1
            freed += [(s_half, halves), (s, NT)]
        for q in range(ADA_REST):
            halves += 1
            freed += [(s_half, halves), (s_ada, ADA_FIRST + q + 1)]
        for c in range(2):
            for g in range(2):
                halves += 1
                freed += [(s_half, halves), (s_gp, NT * (2 * c + g + 1))]
            freed += [(s_ya, NT * (c + 1)), (s_yb, NT * (c + 1))]
        for c in range(2):
            halves += 1
            freed += [(s_half, halves), (s_z, NT * (c + 1))]
        for n in range(4):
            halves += 1
            freed += [(s_half, halves), (s_q, 4 * (n + 1))]
        assert len(freed) == N_BLOCKS

        block = ctx.enter_context(nc.Block())

        @block.sync
        def _(sp):
            sp.dma_start(csm[:, 0, :], c_col).then_inc(s_c, 16)
            for i in range(NT):
                sp.dma_start(h[:, i, :], x[i * P:(i + 1) * P, :]).then_inc(s_x, 16)
            sp.dma_start(ident[:], ident_in).then_inc(s_x, 16)
            for j in range(N_BLOCKS):
                if j >= RING:
                    sp.wait_ge(*freed[j - RING])
                sp.dma_start(ring[:, j % RING, :, :], wstream[j].rearrange("p (k n) -> p k n", k=4)
                             ).then_inc(s_ring[j % RING], 16)
                if j == RING - 1:
                    for v in ADA_ORDER:
                        sp.dma_start(mod[:, v, :], b_ada[v:v + 1, :].to_broadcast([P, D])).then_inc(s_g1, 16)
                    sp.dma_start(ga[:, 0, :], g_pre1.to_broadcast([P, D])).then_inc(s_g1, 16)
                    sp.dma_start(ga[:, 1, :], g_post1.to_broadcast([P, D])).then_inc(s_g1, 16)
                    for dst, src in ((band, pool_band), (wgr, w_group), (psc, pool_scale)):
                        sp.dma_start(dst[:], src).then_inc(s_pool_in, 16)
                    sp.dma_start(gq[:], g_q.to_broadcast([P, Q_LORA])).then_inc(s_tab, 16)
                    sp.dma_start(gkv[:], g_kv.to_broadcast([P, KV_LORA])).then_inc(s_tab, 16)
                    for dst, src in ((rcos, rope_cos), (rsin, rope_sin), (wkvu, w_kv_up), (wqu, w_q_up),
                                     (mask, mask_in), (iota, iota_in)):
                        sp.dma_start(dst[:], src).then_inc(s_tab, 16)
                    sp.dma_start(key_sb[:], keys).then_inc(s_key, 16)
                if j == B_ADA2 + 2 * RING:
                    sp.wait_ge(s_fold, 2)
                    sp.dma_start(ga[:, 0, :], g_pre2.to_broadcast([P, D])).then_inc(s_g2, 16)
                    sp.dma_start(ga[:, 1, :], g_post2.to_broadcast([P, D])).then_inc(s_g2, 16)
            sp.wait_ge(s_h1, NT)
            sp.dma_start(h_scratch, h[:].rearrange("p i n -> p (i n)")).then_inc(s_hout, 16)
            sp.wait_ge(s_hout, 16)
            sp.wait_ge(s_xn, 2 * NT)

            def load_u(n, s):
                sp.dma_start(raw_u[:, s, :, :], expert_u[bass.ds(n, 1)].rearrange("o p e n -> (o p) e n")
                             ).then_inc(s_ul[s], 16)

            def early_pair(n, s):
                sp.wait_ge(s_ulo, n * 2 + 2)
                load_u(n + 2, s)
                sp.wait_ge(s_gelu, n * 2 + 2)
                sp.dma_start(act_scratch[bass.ds(n, 1)].rearrange("o p n -> (o p) n"),
                             gel[:, s, :, :].rearrange("p e n -> p (e n)")).then_inc(s_spill[s], 16)

            def early_pairs(n0, count):
                with sp.Fori(0, count // 2) as it:
                    for s in range(2):
                        early_pair(it * 2 + (n0 + s), s)

            for s in range(2):
                load_u(s, s)
            early_pairs(0, E_FIRST + E_BESIDE)
            n0 = E_FIRST + E_BESIDE
            for i in range(NT):
                sp.wait_ge(s_gev, QUADS + QUADS * TURNS * (i + 1))
                sp.dma_start(g_scratch[:, :, i * P:(i + 1) * P].rearrange("a b t -> b a t"), gate_t[:]
                             ).then_inc(s_gout, 16)
                count = E_BETWEEN + E_BESIDE if i + 1 < NT else E_TAIL
                early_pairs(n0, count)
                n0 += count
            sp.wait_ge(s_gout, 16 * NT)

            def load_v(n, s):
                sp.dma_start(raw_v[:, s, :, :], expert_v[bass.ds(n, 1)].rearrange("o p e n -> (o p) e n")
                             ).then_inc(s_vl[s], 16)

            def load_g(n, s):
                sp.dma_start(g_in[:, s, :, :], g_scratch[bass.ds(n * 2, 2), :, :].rearrange("a b t -> b a t")
                             ).then_inc(s_gl[s], 16)

            def load_act(n, s):
                sp.dma_start(act_in[:, s, :, :].rearrange("p e n -> p (e n)"),
                             act_scratch[bass.ds(n, 1)].rearrange("o p n -> (o p) n")).then_inc(s_al[s], 16)

            def slot_free(j):
                sp.wait_ge(s_vlo, j * 2 + 2)
                sp.wait_ge(s_w, j * 2 + 2)

            for s in range(2):
                load_g(EARLY + s, s)
                load_v(EARLY + s, s)
            with sp.Fori(0, FULL // 2 - 1) as it:
                for s in range(2):
                    sp.wait_ge(s_ulo, it * 4 + (2 * (EARLY + s) + 2))
                    load_u(it * 2 + (EARLY + s + 2), s)
                    slot_free(it * 2 + s)
                    load_g(it * 2 + (EARLY + s + 2), s)
                    load_v(it * 2 + (EARLY + s + 2), s)
            for s in range(2):
                load_act(s, s)
                slot_free(FULL - 2 + s)
                load_g(s, s)
                load_v(s, s)
            sp.wait_ge(s_ulo, 2 * PAIRS)
            sp.wait_ge(s_hout, 16)
            sp.dma_start(h[:].rearrange("p i n -> p (i n)"), h_scratch).then_inc(s_hin, 16)
            with sp.Fori(0, EARLY // 2 - 1) as it:
                for s in range(2):
                    slot_free(it * 2 + (FULL + s))
                    load_act(it * 2 + (s + 2), s)
                    load_g(it * 2 + (s + 2), s)
                    load_v(it * 2 + (s + 2), s)
            for i in range(NT):
                sp.wait_ge(s_fin, i + 1)
                sp.dma_start(out[i * P:(i + 1) * P, :], h[:, i, :]).then_inc(s_out, 16)
            sp.wait_ge(s_out, 16 * NT)

        @block.gpsimd
        def _(pool):
            def low_u(k, s, e):
                pool.wait_ge(s_uhi, k + 1)
                hi, lo = (u_part[:, e, r, :, :].rearrange("p k n -> p (k n)") for r in (0, 1))
                nc.gpsimd.tensor_tensor(lo, raw_u[:, s, e, :], hi.bitcast(F32), ALU.subtract).then_inc(s_ulo, 1)

            def low_v(j, s):
                for e in range(2):
                    pool.wait_ge(s_vhi, j * 2 + (e + 1))
                    nc.gpsimd.tensor_tensor(v_part[:, s, e, 1, :], raw_v[:, s, e, :],
                                            v_part[:, s, e, 0, :].bitcast(F32), ALU.subtract).then_inc(s_vlo, 1)

            with pool.Fori(0, EARLY // 2) as it:
                for s in range(2):
                    for e in range(2):
                        low_u(it * 4 + (2 * s + e), s, e)
            for e in range(2):
                low_u(2 * EARLY + e, 0, e)
            low_v(0, 0)
            with pool.Fori(0, FULL // 2 - 1) as it:
                for s in range(2):
                    for e in range(2):
                        low_u(it * 4 + (2 * EARLY + 2 * s + 2 + e), 1 - s, e)
                    low_v(it * 2 + (s + 1), 1 - s)
            for e in range(2):
                low_u(2 * PAIRS - 2 + e, 1, e)
            low_v(FULL - 1, 1)
            with pool.Fori(0, EARLY // 2) as it:
                for s in range(2):
                    low_v(it * 2 + (FULL + s), s)

        @block.scalar
        def _(act):
            a = nc.scalar
            act.wait_ge(s_c, 16)
            a.activation(csm[:, 1, :], csm[:, 0, :], ACT.Sigmoid).then_inc(s_sig_c, 1)

            act.wait_ge(s_x, 16 * (NT + 1))
            for i in range(NT):
                last = a.activation(squares[:, i, :], h[:, i, :], ACT.Square, accum_out=stat[:, SS1 + i:SS1 + i + 1])
            last.then_inc(s_sq, 1)
            act.wait_ge(s_var, 1)
            a.activation(stat[:, SS1:SS1 + 4], stat[:, SS1:SS1 + 4], ACT.Sqrt).then_inc(s_std, 1)

            def read_xT(i, n):
                act.wait_ge(s_xtr, n)
                for b in range(2):
                    last = a.activation(xT[:, 4 * b:4 * b + 4, i * P:(i + 1) * P],
                                        bank[4 + 2 * (i % 2) + b][:].rearrange("p (k t) -> p k t", k=4), ACT.Copy)
                return last

            for i in range(NT):
                read_xT(i, i + 1).then_inc(s_xT, 1)
            act.wait_ge(s_pool_in, 48)
            for i in range(NT):
                act.wait_ge(s_xp, i + 1)
                a.activation(xpool[:, i, :], bank[i][:], ACT.Copy).then_inc(s_xps, 1)
            for i in range(NT):
                act.wait_ge(s_lat, i + 1)
                a.activation(squares[:, i, 0:Q_LORA], lat[:, i, 0:Q_LORA], ACT.Square,
                             accum_out=stat[:, SSL + i:SSL + i + 1])
                last = a.activation(squares[:, i, Q_LORA:Q_LORA + KV_LORA], lat[:, i, Q_LORA:Q_LORA + KV_LORA],
                                    ACT.Square, accum_out=stat[:, SSL + NT + i:SSL + NT + i + 1])
            last.then_inc(s_sq, 1)
            act.wait_ge(s_var, 2)
            a.activation(stat[:, SSL:SSL + 2 * NT], stat[:, SSL:SSL + 2 * NT], ACT.Sqrt).then_inc(s_std, 1)
            for g in range(POOL_G):
                act.wait_ge(s_yp, g + 1)
                a.activation(ypT[:, g, :], bank[2 + g % 2][:], ACT.Copy, scale=psc[:, g:g + 1]).then_inc(s_ypT, 1)
            for i in range(NT):
                act.wait_ge(s_ltr, i + 1)
                a.activation(latT[:, :, i * P:(i + 1) * P],
                             bank[4 + i][:, 0:3 * P].rearrange("p (k t) -> p k t", k=3), ACT.Copy).then_inc(s_latT, 1)

            def q_rows(i):
                act.wait_ge(s_qup, i + 1)
                if i >= 2:
                    act.wait_ge(s_qtr, i - 1)
                for b in range(2):
                    last = a.activation(qs[:, i % 2, 4 * b:4 * b + 4, :],
                                        bank[b][:, 0:4 * QK].rearrange("p (h n) -> p h n", h=4), ACT.Copy,
                                        scale=SM_SCALE)
                last.then_inc(s_qs, 1)

            def read_QT(i):
                act.wait_ge(s_qtr, i + 1)
                for b in range(2):
                    last = a.activation(QT[:, 4 * b:4 * b + 4, i * P:(i + 1) * P],
                                        bank[4 + b][0:QK, :].rearrange("p (h t) -> p h t", h=4), ACT.Copy)
                last.then_inc(s_QT, 1)

            q_rows(0)
            for i in range(NT):
                if i + 1 < NT:
                    q_rows(i + 1)
                read_QT(i)

            for u in range(UNITS + 4):
                if u < UNITS:
                    i = u // HEADS
                    n = (i + 1) * P
                    act.wait_ge(s_max, u + 1)
                    if u >= 2:
                        act.wait_ge(s_ptr, u - 1)
                    a.activation(pr[:, u % 2, 0:n], bank[u % 2][:, 0:n], ACT.Exp, bias=nmax[:, u:u + 1],
                                 accum_out=rsum[:, u:u + 1]).then_inc(s_exp, 1)
                if 1 <= u <= UNITS:
                    v = u - 1
                    n = (v // HEADS + 1)
                    act.wait_ge(s_ptr, v + 1)
                    if v >= 2:
                        act.wait_ge(s_pv, v - 1)
                    a.activation(prT[:, v % 2, 0:n, :], bank[2 + v % 2][:, 0:n * P].rearrange("p (k t) -> p k t", k=n),
                                 ACT.Copy).then_inc(s_prT, 1)
                if u >= HEADS + 2 and (u - HEADS - 2) % HEADS == 0:
                    i = (u - HEADS - 2) // HEADS
                    act.wait_ge(s_otr, i + 1)
                    a.activation(oT[:, :, i * P:(i + 1) * P], bank[5][:].rearrange("p (k t) -> p k t", k=4),
                                 ACT.Copy).then_inc(s_oT, 1)

            for c in range(2):
                for g in range(2):
                    for i in range(NT):
                        act.wait_ge(s_gp, NT * (2 * c + g) + i + 1)
                        if c:
                            act.wait_ge(s_mg, i + 1)
                        a.activation(sg[:, g, i, :], bank[4 * g + i][:], ACT.Sigmoid).then_inc(s_sg, 1)
            for i in range(NT):
                act.wait_ge(s_mtr, i + 1)
                for b in range(2):
                    last = a.activation(mT[:, 4 * b:4 * b + 4, i * P:(i + 1) * P],
                                        bank[2 * (i % 2) + b][:].rearrange("p (k t) -> p k t", k=4), ACT.Copy)
                last.then_inc(s_mT, 1)
            for c in range(2):
                for i in range(NT):
                    act.wait_ge(s_z, NT * c + i + 1)
                    a.activation(zz[:, i, c * HALF:(c + 1) * HALF], bank[4 * c + i][:], ACT.Copy).then_inc(s_zs, 1)
            act.wait_ge(s_zs, 2 * NT)
            for i in range(NT):
                last = a.activation(squares2[:, i, :], zz[:, i, :], ACT.Square, accum_out=stat[:, SSZ + i:SSZ + i + 1])
            last.then_inc(s_sq, 1)
            act.wait_ge(s_var, 3)
            a.activation(stat[:, SSZ:SSZ + 4], stat[:, SSZ:SSZ + 4], ACT.Sqrt).then_inc(s_std, 1)
            for i in range(NT):
                act.wait_ge(s_h1, i + 1)
                last = a.activation(squares2[:, i, :], h[:, i, :], ACT.Square, accum_out=stat[:, SSH + i:SSH + i + 1])
            last.then_inc(s_sq, 1)
            act.wait_ge(s_var, 4)
            a.activation(stat[:, SSH:SSH + 4], stat[:, SSH:SSH + 4], ACT.Sqrt).then_inc(s_std, 1)
            for i in range(NT):
                read_xT(i, NT + i + 1)
                for b in range(2):
                    last = a.activation(xh[:, 4 * b:4 * b + 4, i * P:(i + 1) * P],
                                        bank[4 + 2 * (i % 2) + b][:].rearrange("p (k t) -> p k t", k=4), ACT.Copy)
                last.then_inc(s_xT, 1)
            for n in range(4):
                for m in range(4):
                    act.wait_ge(s_q, 4 * n + m + 1)
                    if n:
                        act.wait_ge(s_scr, 4 * (n - 1) + m + 1)
                    a.activation(qT[:, m, :], bank[m][:], ACT.Copy).then_inc(s_qT, 1)
            def high_u(k, s, e, loads):
                act.wait_ge(s_ul[s], loads)
                a.activation(u_part[:, e, 0, :, :].rearrange("p k n -> p (k n)"), raw_u[:, s, e, :],
                             ACT.Copy).then_inc(s_uhi, 1)

            def gelu(k, s, e):
                act.wait_ge(s_act, k + 1)
                a.activation(gel[:, s, e, :], bank[4 + e][:], ACT.Gelu_apprx_tanh).then_inc(s_gelu, 1)

            def early_tile(n, s, e, loads, stored):
                if e == 0 and stored is not None:
                    act.wait_ge(s_spill[s], stored)
                gelu(n * 2 + e, s, e)
                high_u(n * 2 + (e + 2), 1 - s, e, loads)

            def early_pair(it16, n, s, n0):
                for e in range(2):
                    early_tile(n, s, e, it16 + 8 * n0 + (16 if s == 0 else 32), it16 + 8 * n0)

            def early_pairs(n0, count):
                with act.Fori(0, count // 2) as it:
                    for s in range(2):
                        early_pair(it * 16, it * 2 + (n0 + s), s, n0)

            act.wait_ge(s_xn, 2 * NT)
            for e in range(2):
                high_u(e, 0, e, 16)
            for n in range(2):
                for e in range(2):
                    early_tile(n, n, e, 16 if n == 0 else 32, None)
            early_pairs(2, E_FIRST - 2)
            n0 = E_FIRST
            for i in range(NT):
                act.wait_ge(s_bv, i + 1)
                a.activation(gexp[:, 1, :, :], gexp[:, 0, :, :], ACT.Exp).then_inc(s_ge, 1)
                if i == 0:
                    a.sem_inc(s_gev, QUADS)
                else:
                    act.wait_ge(s_gout, 16 * i)
                with act.Fori(0, E_BESIDE // 2) as it:
                    for s in range(2):
                        for e in range(2):
                            early_tile(it * 2 + (n0 + s), s, e, it * 16 + (8 * n0 + (16 if s == 0 else 32)),
                                       it * 16 + 8 * n0)
                            turn = 2 * s + e
                            for q in range(QUADS):
                                act.wait_ge(s_gmm, it * (4 * QUADS) +
                                            (QUADS + (i * TURNS + turn) * QUADS + q + 1))
                                a.activation(gate_t[:, :, bass.ds(it * (16 * QUADS) + (turn * 4 * QUADS + 4 * q), 4)],
                                             bank[q][:].rearrange("p (t k) -> p k t", t=4),
                                             ACT.Copy).then_inc(s_gev, 1)
                n0 += E_BESIDE
                count = E_BETWEEN if i + 1 < NT else E_TAIL
                early_pairs(n0, count)
                n0 += count

            def high_v(j, s, loads):
                act.wait_ge(s_vl[s], loads)
                for e in range(2):
                    a.activation(v_part[:, s, e, 0, :], raw_v[:, s, e, :], ACT.Copy).then_inc(s_vhi, 1)

            def high_w(j, s, e):
                act.wait_ge(s_w, j * 2 + (e + 1))
                a.activation(w_part[:, s, e, 0, :], w_full[:, e, :], ACT.Copy).then_inc(s_whi, 1)

            act.wait_ge(s_spill[0], 8 * EARLY)
            act.wait_ge(s_spill[1], 8 * EARLY)
            high_v(0, 0, 16)

            def full_pair(j, s, loads_u, loads_v, passed):
                for e in range(2):
                    gelu(j * 2 + (2 * EARLY + e), s, e)
                    if loads_u is not None:
                        high_u(j * 2 + (2 * EARLY + e + 2), 1 - s, e, loads_u)
                    high_w(j, s, e)
                if passed is not None:
                    act.wait_ge(s_y, passed)
                high_v(j + 1, 1 - s, loads_v)

            full_pair(0, 0, 8 * EARLY + 16, 16, None)
            with act.Fori(0, FULL // 2 - 1) as it:
                full_pair(it * 2 + 1, 1, it * 16 + (8 * EARLY + 32), it * 16 + 32, it * (2 * YJ) + YJ)
                full_pair(it * 2 + 2, 0, it * 16 + (8 * EARLY + 32), it * 16 + 32, it * (2 * YJ) + 2 * YJ)
            full_pair(FULL - 1, 1, None, 8 * FULL + 16, YJ * (FULL - 1))
            with act.Fori(0, EARLY // 2 - 1) as it:
                for s in range(2):
                    j = it * 2 + (FULL + s)
                    for e in range(2):
                        high_w(j, s, e)
                    act.wait_ge(s_y, j * YJ)
                    high_v(j + 1, 1 - s, it * 16 + (8 * FULL + (16 if s == 0 else 32)))
            for e in range(2):
                high_w(PAIRS - 2, 0, e)
            act.wait_ge(s_y, YJ * (PAIRS - 2))
            high_v(PAIRS - 1, 1, 8 * PAIRS)
            for e in range(2):
                high_w(PAIRS - 1, 1, e)
            act.wait_ge(s_yd, YB + YJ * PAIRS)
            for i in range(NT):
                last = a.activation(squares3[:, i, :], yacc[:, i, :], ACT.Square, accum_out=stat[:, SSY + i:SSY + i + 1])
            last.then_inc(s_sq, 1)
            act.wait_ge(s_var, 5)
            a.activation(stat[:, SSY:SSY + 4], stat[:, SSY:SSY + 4], ACT.Sqrt).then_inc(s_std, 1)

        @block.vector
        def _(dve):
            v = nc.vector
            count = [0]

            def link(ins):
                count[0] += 1
                ins.then_inc(s_chain, 1)
                dve.wait_ge(s_chain, count[0])

            def rstd(col, n, width, stage):
                dve.wait_ge(s_sq, stage)
                for k, w in enumerate(width):
                    last = v.tensor_scalar(stat[:, col + n * k:col + n * (k + 1)], stat[:, col + n * k:col + n * (k + 1)],
                                           1.0 / w, EPS, ALU.mult, ALU.add)
                last.then_inc(s_var, 1)
                dve.wait_ge(s_std, stage)
                m = n * len(width)
                link(v.reciprocal(stat[:, col:col + m], stat[:, col:col + m]))

            def scaled(o, rows, r, g):
                return v.scalar_tensor_tensor(o, rows, r, g, ALU.mult, ALU.mult)

            dve.wait_ge(s_sig_c, 1)
            link(v.tensor_tensor(csm[:, 1, :], csm[:, 0, :], csm[:, 1, :], ALU.mult))
            v.tensor_copy(ccb[:], csm[:, 1, :].unsqueeze(2).to_broadcast([P, ND, P])).then_inc(s_ccb, 1)
            dve.wait_ge(s_g1, 16 * 8)

            def ada(q):
                dve.wait_ge(s_ada, q + 1)
                b = q if q < ADA_FIRST else 6 + q % 2
                m = mod[:, ADA_ORDER[q // 2], (q % 2) * HALF:(q % 2 + 1) * HALF]
                v.tensor_tensor(m, bank[b][:], m, ALU.add).then_inc(s_mod, 1)
                if q % 2 == 0:
                    return
                vec = ADA_ORDER[q // 2]
                if vec in (SCALE1, SCALE2):
                    if vec == SCALE2:
                        dve.wait_ge(s_g2, 32)
                    dve.wait_ge(s_mod, q + 1)
                    v.scalar_tensor_tensor(mod[:, vec, :], mod[:, vec, :], 1.0, ga[:, 0, :], ALU.add,
                                           ALU.mult).then_inc(s_fold, 1)
                if vec in (GATE1, GATE2):
                    dve.wait_ge(s_mod, q + 1)
                    v.tensor_tensor(mod[:, vec, :], mod[:, vec, :], ga[:, 1, :], ALU.mult).then_inc(s_fold, 1)

            for q in range(ADA_FIRST):
                ada(q)
            rstd(SS1, NT, [D], 1)
            dve.wait_ge(s_fold, 1)
            dve.wait_ge(s_mod, ADA_FIRST)
            for i in range(NT):
                if i >= 2:
                    dve.wait_ge(s_xtr, i - 1)
                link(scaled(xrow[:, i % 2, :], h[:, i, :], stat[:, SS1 + i:SS1 + i + 1], mod[:, SCALE1, :]))
                v.tensor_tensor(xrow[:, i % 2, :], xrow[:, i % 2, :], mod[:, SHIFT1, :], ALU.add).then_inc(s_xn, 1)
            for i in range(NT):
                dve.wait_ge(s_lp, i + 1)
                v.tensor_copy(lat[:, i, :], bank[4 + i][:, 0:LAT]).then_inc(s_lat, 1)
            dve.wait_ge(s_tab, 16 * 8)
            for g in range(POOL_G):
                dve.wait_ge(s_mxp, g + 1)
                if g >= 2:
                    dve.wait_ge(s_yp, g - 1)
                v.tensor_copy(mx[:, g % 2, :], bank[g % 2][:]).then_inc(s_mx, 1)
            rstd(SSL, NT, [Q_LORA, KV_LORA], 2)
            for i in range(NT):
                scaled(lat[:, i, 0:Q_LORA], lat[:, i, 0:Q_LORA], stat[:, SSL + i:SSL + i + 1], gq[:])
                scaled(lat[:, i, Q_LORA:Q_LORA + KV_LORA], lat[:, i, Q_LORA:Q_LORA + KV_LORA],
                       stat[:, SSL + NT + i:SSL + NT + i + 1], gkv[:]).then_inc(s_ln, 1)
            HR = ROPE // 2

            def rotate(rows, i, nh):
                def tab(t, lo, hi):
                    return t[:, i:i + 1, lo:hi].to_broadcast([P, nh, hi - lo])
                t1, t2 = rtmp[:, 0, 0:nh, :], rtmp[:, 1, 0:nh, :]
                v.tensor_tensor(t1, rows, tab(rcos, 0, ROPE), ALU.mult)
                v.tensor_tensor(t2[:, :, 0:HR], rows[:, :, HR:ROPE], tab(rsin, 0, HR), ALU.mult)
                link(v.tensor_tensor(t2[:, :, HR:ROPE], rows[:, :, 0:HR], tab(rsin, HR, ROPE), ALU.mult))
                return v.tensor_tensor(rows, t1, t2, ALU.add)

            def kv_rows(i):
                dve.wait_ge(s_kvup, i + 1)
                if i >= 2:
                    dve.wait_ge(s_ktr, i - 1)
                for b in range(2):
                    kv = bank[2 + b][:].rearrange("p (h n) -> p h n", h=4)
                    v.tensor_copy(kc[:, i % 2, 4 * b:4 * b + 4, 0:NOPE], kv[:, :, 0:NOPE])
                    last = v.tensor_copy(vv[:, i, 4 * b:4 * b + 4, :], kv[:, :, NOPE:NOPE + VH])
                last.then_inc(s_kc, 1)
                if i:
                    dve.wait_ge(s_rot, i)
                link(rotate(lat[:, i:i + 1, Q_LORA + KV_LORA:LAT], i, 1))
                v.tensor_copy(kc[:, i % 2, :, NOPE:QK],
                              lat[:, i:i + 1, Q_LORA + KV_LORA:LAT].to_broadcast([P, HEADS, ROPE]))
                dve.wait_ge(s_qs, i + 1)
                rotate(qs[:, i % 2, :, NOPE:QK], i, HEADS).then_inc(s_rot, 1)

            def read_KT(i):
                dve.wait_ge(s_ktr, i + 1)
                for b in range(2):
                    last = v.tensor_copy(KT[:, 4 * b:4 * b + 4, i * P:(i + 1) * P],
                                         bank[6 + b][0:QK, :].rearrange("p (h t) -> p h t", h=4))
                last.then_inc(s_KT, 1)

            kv_rows(0)
            for i in range(NT):
                if i + 1 < NT:
                    kv_rows(i + 1)
                read_KT(i)

            for u in range(UNITS + 4):
                if u < UNITS:
                    i = u // HEADS
                    dve.wait_ge(s_sc, u + 1)
                    diag = bank[u % 2][:, i * P:(i + 1) * P]
                    link(v.tensor_tensor(diag, diag, mask[:], ALU.add))
                    v.tensor_reduce(nmax[:, u:u + 1], bank[u % 2][:, 0:(i + 1) * P], AX_X, ALU.max,
                                    negate=True).then_inc(s_max, 1)
                if u >= HEADS + 1 and (u - HEADS - 1) % HEADS == 0:
                    i = (u - HEADS - 1) // HEADS
                    dve.wait_ge(s_exp, HEADS * (i + 1))
                    link(v.reciprocal(rinv[:, 8 * i:8 * i + 8], rsum[:, 8 * i:8 * i + 8]))
                    dve.wait_ge(s_pv, HEADS * (i + 1))
                    if i:
                        dve.wait_ge(s_otr, i)
                    v.tensor_tensor(osb[:], bank[4][:].rearrange("p (h n) -> p h n", h=HEADS),
                                    rinv[:, 8 * i:8 * i + 8].unsqueeze(2).to_broadcast([P, HEADS, VH]),
                                    ALU.mult).then_inc(s_o, 1)
                if u % 4 == 3 and u // 4 < ADA_REST:
                    ada(ADA_FIRST + u // 4)

            for c in range(2):
                for g, s in ((0, s_ya), (1, s_yb)):
                    for i in range(NT):
                        dve.wait_ge(s, NT * c + i + 1)
                        dve.wait_ge(s_sg, 2 * NT * c + NT * g + i + 1)
                        last = v.tensor_tensor(sg[:, g, i, :], bank[4 * g + i][:], sg[:, g, i, :], ALU.mult)
                        if g == 0:
                            last.then_inc(s_yad, 1)
                        else:
                            link(last)
                            dve.wait_ge(s_yad, NT * c + i + 1)
                            v.tensor_tensor(zz[:, i, c * HALF:(c + 1) * HALF], sg[:, 0, i, :], sg[:, 1, i, :],
                                            ALU.add).then_inc(s_mg, 1)
            rstd(SSZ, NT, [D], 3)
            dve.wait_ge(s_fold, 4)
            for i in range(NT):
                link(scaled(zz[:, i, :], zz[:, i, :], stat[:, SSZ + i:SSZ + i + 1], mod[:, GATE1, :]))
                v.tensor_tensor(h[:, i, :], h[:, i, :], zz[:, i, :], ALU.add).then_inc(s_h1, 1)
            dve.wait_ge(s_h1, NT)
            rstd(SSH, NT, [D], 4)
            for i in range(NT):
                link(scaled(zz[:, i, :], h[:, i, :], stat[:, SSH + i:SSH + i + 1], mod[:, SCALE2, :]))
                v.tensor_tensor(zz[:, i, :], zz[:, i, :], mod[:, SHIFT2, :], ALU.add).then_inc(s_xn, 1)
            for i in range(NT):
                dve.wait_ge(s_xT, NT + i + 1)
                v.tensor_tensor(xl[:, :, i * P:(i + 1) * P], xT[:, :, i * P:(i + 1) * P],
                                xh[:, :, i * P:(i + 1) * P].bitcast(F32), ALU.subtract).then_inc(s_xl, 1)
            def top16(vals, idx, src, n):
                for part in range(2):
                    lo, hi = 8 * part, 8 * part + 8
                    for k in range(n):
                        last = v.max(vals(k)[:, lo:hi], src(k))
                    link(last)
                    for k in range(n):
                        last = v.max_index(idx(k)[:, lo:hi], vals(k)[:, lo:hi], src(k))
                    link(last)
                    if part == 0:
                        for k in range(n):
                            last = v.match_replace(src(k), vals(k)[:, lo:hi], src(k), NEG)
                        link(last)

            for n in range(4):
                for m in range(4):
                    dve.wait_ge(s_scr, 4 * n + m + 1)
                    side = (m % 2) * RH + 2 * n + m // 2
                    v.tensor_copy(scores[:, :, side, :], bank[4 + m][:].rearrange("p (i k) -> p i k", i=NT)
                                  ).then_inc(s_scs, 1)
                    dve.wait_ge(s_scs, 4 * n + m + 1)
                    if 4 * n + m >= 2:
                        dve.wait_ge(s_top, 4 * n + m - 1)
                    top16(lambda i: top_v[:, i, side, :], lambda i: top_i[:, m % 2, i, :],
                          lambda i: scores[:, i, side, :], NT)
                    v.tensor_copy(top_if[:, :, side, :], top_i[:, m % 2, :, :]).then_inc(s_top, 1)
            dve.wait_ge(s_top, SIDES)

            def spread(t, dim):
                return t.unsqueeze(dim).to_broadcast([P, RH, TOPK, TOPK])

            for i in range(NT):
                if i:
                    dve.wait_ge(s_ge, i)
                link(v.tensor_tensor(cand[:], spread(top_v[:, i, 0:RH, :], 3), spread(top_v[:, i, RH:SIDES, :], 2),
                                     ALU.add))
                top16(lambda k: best_v[:, k, :], lambda k: best_c[:, k, :],
                      lambda k: cand[:, k, :, :].rearrange("p a b -> p (a b)"), RH)
                v.tensor_tensor(gexp[:, 0, :, :], best_v[:], best_v[:, :, 0:1].to_broadcast([P, RH, TOPK]),
                                ALU.subtract).then_inc(s_bv, 1)
                v.tensor_scalar(best_ab[:, 0, :, :], best_c[:], 4, None, ALU.logical_shift_right)
                link(v.tensor_scalar(best_ab[:, 1, :, :], best_c[:], TOPK - 1, None, ALU.bitwise_and))
                link(v.tensor_copy(best_abf[:], best_ab[:]))
                for s in range(2):
                    link(v.tensor_tensor(cand[:], spread(best_abf[:, s, :, :], 3),
                                         iota[:, 0:TOPK].unsqueeze(1).unsqueeze(1).to_broadcast([P, RH, TOPK, TOPK]),
                                         ALU.is_equal))
                    link(v.tensor_tensor(cand[:], cand[:], spread(top_if[:, i, s * RH:(s + 1) * RH, :], 2), ALU.mult))
                    link(v.tensor_reduce(picks[:, s, :], cand[:].rearrange("p h k a -> p (h k) a"), AX_X, ALU.add))
                dve.wait_ge(s_ge, i + 1)
                link(v.tensor_reduce(gsum[:, 0, :], gexp[:, 1, :, :], AX_X, ALU.add))
                link(v.reciprocal(gsum[:, 1, :], gsum[:, 0, :]))
                v.tensor_tensor(picks[:, 2, :].rearrange("p (h k) -> p h k", h=RH), gexp[:, 1, :, :],
                                gsum[:, 1, :].unsqueeze(2).to_broadcast([P, RH, TOPK]), ALU.mult).then_inc(s_pk, 1)
                dve.wait_ge(s_pkt, i + 1)
                link(v.tensor_copy(picksT[:, :, i * P:(i + 1) * P],
                                   bank[6][:, 0:3 * P].rearrange("p (r t) -> p r t", r=3)))
                with dve.Fori(0, E_BESIDE // 2) as it:
                    for turn in range(4):
                        for q in range(QUADS):
                            dve.wait_ge(s_gmm, it * (4 * QUADS) + ((i * TURNS + turn) * QUADS + q + 1))
                            for t in range(4):
                                def col(r):
                                    return picksT[:, r, bass.ds(it * (16 * QUADS) +
                                                                (i * P + (turn * QUADS + q) * 4 + t), 1)]
                                v.tensor_scalar(hot[:, q, t, 0, :], iota[:], col(1), None, ALU.is_equal)
                                last = v.tensor_scalar(hot[:, q, t, 1, :], iota[:], col(0), col(2),
                                                       ALU.is_equal, ALU.mult)
                            last.then_inc(s_hot, 1)

            def weigh(j, s, act_rows, loads, early_loads=None):
                dve.wait_ge(s_gl[s], loads)
                if early_loads is not None:
                    dve.wait_ge(s_al[s], early_loads)
                for e in range(2):
                    if early_loads is None:
                        dve.wait_ge(s_gelu, j * 2 + (2 * EARLY + e + 1))
                    v.tensor_tensor(w_full[:, e, :], act_rows[:, s, e, :], g_in[:, s, e, :], ALU.mult).then_inc(s_w, 1)
                    dve.wait_ge(s_whi, j * 2 + (e + 1))
                    v.tensor_tensor(w_part[:, s, e, 1, :], w_full[:, e, :], w_part[:, s, e, 0, :].bitcast(F32),
                                    ALU.subtract).then_inc(s_wlo, 1)

            def add_y(j):
                for r in range(YJ):
                    dve.wait_ge(s_y, j * YJ + (r + 1))
                    o = yacc[:, r // 2, (r % 2) * HALF:(r % 2 + 1) * HALF]
                    v.tensor_tensor(o, bank[r % YB][:], o, ALU.add).then_inc(s_yd, 1)

            dve.wait_ge(s_gmm, QUADS * (1 + NT * TURNS))
            link(v.memset(yacc[:], 0.0))
            v.sem_inc(s_yd, YB)
            weigh(0, 0, gel, 16)
            with dve.Fori(0, FULL // 2 - 1) as it:
                weigh(it * 2 + 1, 1, gel, it * 16 + 16)
                add_y(it * 2)
                weigh(it * 2 + 2, 0, gel, it * 16 + 32)
                add_y(it * 2 + 1)
            weigh(FULL - 1, 1, gel, 8 * FULL)
            add_y(FULL - 2)
            with dve.Fori(0, EARLY // 2) as it:
                for s in range(2):
                    weigh(it * 2 + (FULL + s), s, act_in, it * 16 + (8 * FULL + 16), it * 16 + 16)
                    add_y(it * 2 + (FULL + s - 1))
            add_y(PAIRS - 1)
            rstd(SSY, NT, [D], 5)
            dve.wait_ge(s_hin, 16)
            for i in range(NT):
                link(scaled(yacc[:, i, :], yacc[:, i, :], stat[:, SSY + i:SSY + i + 1], mod[:, GATE2, :]))
                v.tensor_tensor(h[:, i, :], h[:, i, :], yacc[:, i, :], ALU.add).then_inc(s_fin, 1)

        @block.tensor
        def _(pe):
            def matmul(o, l, r, first, last):
                return nc.tensor.matmul(o, l, r, start=bool(first), stop=bool(last))

            def loaded(j):
                pe.wait_ge(s_ring[j % RING], 16 * (j // RING + 1))

            def ada_piece(q, kh, k):
                j = (KH * q if q < ADA_FIRST else B_ADA2 + KH * (q - ADA_FIRST)) + kh
                b = q if q < ADA_FIRST else 6 + q % 2
                if k == 0:
                    loaded(j)
                    if kh == 0 and q >= ADA_FIRST + 2:
                        pe.wait_ge(s_mod, q - 1)
                last = matmul(bank[b][:], ccb[:, 4 * kh + k, :], ring[:, j % RING, k, :], kh + k == 0, kh and k == 3)
                if k == 3:
                    last.then_inc(s_ada if kh else s_half, 1)

            pe.wait_ge(s_ccb, 1)
            for q in range(ADA_FIRST):
                for kh in range(KH):
                    for k in range(4):
                        ada_piece(q, kh, k)

            def transpose_rows(rows, i, banks):
                for k in range(ND):
                    last = nc.tensor.transpose(bank[banks + k // 4][:, (k % 4) * P:(k % 4 + 1) * P],
                                               rows[:, k * P:(k + 1) * P], ident[:])
                return last

            pe.wait_ge(s_x, 16 * (NT + 1))
            for i in range(NT):
                pe.wait_ge(s_xn, i + 1)
                if i >= 2:
                    pe.wait_ge(s_xT, i - 1)
                transpose_rows(xrow[:, i % 2, :], i, 4 + 2 * (i % 2)).then_inc(s_xtr, 1)

            def project(j0, src, b0, signal, n=HALF):
                for kh in range(KH):
                    loaded(j0 + kh)
                    for i in range(NT):
                        for k in range(4):
                            last = matmul(bank[b0 + i][:, 0:n], src[:, 4 * kh + k, i * P:(i + 1) * P],
                                          ring[:, (j0 + kh) % RING, k, 0:n], kh + k == 0, kh and k == 3)
                        if kh:
                            last.then_inc(signal, 1)
                    if not kh:
                        last.then_inc(s_half, 1)

            pe.wait_ge(s_mod, ADA_FIRST)
            pe.wait_ge(s_xT, NT)
            project(B_IN, xT, 0, s_xp)
            project(B_IN + KH, xT, 4, s_lp, LAT)

            pe.wait_ge(s_xps, NT)
            pe.wait_ge(s_pool_in, 48)

            def pool(g):
                if g >= 2:
                    pe.wait_ge(s_mx, g - 1)
                for i in range(NT):
                    o = bank[g % 2][:, i * P:(i + 1) * P]
                    last = matmul(o, xpool[:, i, g * P:(g + 1) * P], band[:, 0 if i == 0 else 1, g, :], True, i == 0)
                    if i:
                        last = matmul(o, xpool[:, i - 1, g * P:(g + 1) * P], band[:, 2, g, :], False, True)
                last.then_inc(s_mxp, 1)

            def group_map(g):
                pe.wait_ge(s_mx, g + 1)
                if g >= 2:
                    pe.wait_ge(s_ypT, g - 1)
                matmul(bank[2 + g % 2][:], wgr[:, g, :], mx[:, g % 2, :], True, True).then_inc(s_yp, 1)

            pool(0)
            for g in range(POOL_G):
                if g + 1 < POOL_G:
                    pool(g + 1)
                group_map(g)

            for i in range(NT):
                pe.wait_ge(s_ln, i + 1)
                for k in range(3):
                    last = nc.tensor.transpose(bank[4 + i][:, k * P:(k + 1) * P], lat[:, i, k * P:(k + 1) * P], ident[:])
                last.then_inc(s_ltr, 1)
            pe.wait_ge(s_tab, 16 * 8)
            pe.wait_ge(s_ypT, POOL_G)

            def lift(i):
                tok = slice(i * P, (i + 1) * P)
                pe.wait_ge(s_latT, i + 1)
                if i:
                    pe.wait_ge(s_qs, i)
                for b in range(2):
                    for k in range(2):
                        last = matmul(bank[b][:, 0:4 * QK], latT[:, k, tok], wqu[:, k, b * 4 * QK:(b + 1) * 4 * QK],
                                      k == 0, k == 1)
                last.then_inc(s_qup, 1)
                if i:
                    pe.wait_ge(s_kc, i)
                for b in range(2):
                    last = matmul(bank[2 + b][:], latT[:, 2, tok], wkvu[:, b * HALF:(b + 1) * HALF], True, True)
                last.then_inc(s_kvup, 1)

            def turn(i):
                pe.wait_ge(s_rot, i + 1)
                if i:
                    pe.wait_ge(s_QT, i)
                else:
                    pe.wait_ge(s_latT, NT)
                for hd in range(HEADS):
                    last = nc.tensor.transpose(bank[4 + hd // 4][0:QK, (hd % 4) * P:(hd % 4 + 1) * P],
                                               qs[:, i % 2, hd, :], ident[:])
                last.then_inc(s_qtr, 1)
                if i:
                    pe.wait_ge(s_KT, i)
                for hd in range(HEADS):
                    last = nc.tensor.transpose(bank[6 + hd // 4][0:QK, (hd % 4) * P:(hd % 4 + 1) * P],
                                               kc[:, i % 2, hd, :], ident[:])
                last.then_inc(s_ktr, 1)

            lift(0)
            for i in range(NT):
                if i + 1 < NT:
                    lift(i + 1)
                turn(i)

            pe.wait_ge(s_QT, NT)
            pe.wait_ge(s_KT, NT)
            for u in range(UNITS + 4):
                if u < UNITS:
                    i, hd = divmod(u, HEADS)
                    if u >= 2:
                        pe.wait_ge(s_exp, u - 1)
                    matmul(bank[u % 2][:, 0:(i + 1) * P], QT[:, hd, i * P:(i + 1) * P], KT[:, hd, 0:(i + 1) * P],
                           True, True).then_inc(s_sc, 1)
                if 1 <= u <= UNITS:
                    w = u - 1
                    pe.wait_ge(s_exp, w + 1)
                    if w >= 2:
                        pe.wait_ge(s_prT, w - 1)
                    for k in range(w // HEADS + 1):
                        last = nc.tensor.transpose(bank[2 + w % 2][:, k * P:(k + 1) * P],
                                                   pr[:, w % 2, k * P:(k + 1) * P], ident[:])
                    last.then_inc(s_ptr, 1)
                if 2 <= u <= UNITS + 1:
                    w = u - 2
                    i, hd = divmod(w, HEADS)
                    pe.wait_ge(s_prT, w + 1)
                    if hd == 0 and i:
                        pe.wait_ge(s_o, i)
                    for k in range(i + 1):
                        last = matmul(bank[4][:, hd * VH:(hd + 1) * VH], prT[:, w % 2, k, :], vv[:, k, hd, :],
                                      k == 0, k == i)
                    last.then_inc(s_pv, 1)
                if u >= HEADS + 2 and (u - HEADS - 2) % HEADS == 0:
                    i = (u - HEADS - 2) // HEADS
                    pe.wait_ge(s_o, i + 1)
                    if i:
                        pe.wait_ge(s_oT, i)
                    for k in range(4):
                        last = nc.tensor.transpose(bank[5][:, k * P:(k + 1) * P],
                                                   osb[:, 2 * k:2 * k + 2, :].rearrange("p h n -> p (h n)"), ident[:])
                    last.then_inc(s_otr, 1)
                if u < 4 * ADA_REST:
                    for piece in (2 * (u % 4), 2 * (u % 4) + 1):
                        ada_piece(ADA_FIRST + u // 4, piece // 4, piece % 4)

            pe.wait_ge(s_oT, NT)
            pe.wait_ge(s_mod, ADA_FIRST + ADA_REST)
            for c in range(2):
                if c:
                    pe.wait_ge(s_mg, NT)
                project(B_MERGE + 6 * c, xT, 0, s_gp)
                project(B_MERGE + 6 * c + 2, xT, 4, s_gp)
                for g, (src, signal) in enumerate(((ypT, s_ya), (oT, s_yb))):
                    j = B_MERGE + 6 * c + 4 + g
                    loaded(j)
                    for i in range(NT):
                        pe.wait_ge(s_sg, 2 * NT * c + NT * g + i + 1)
                        for k in range(4):
                            last = matmul(bank[4 * g + i][:], src[:, k, i * P:(i + 1) * P], ring[:, j % RING, k, :],
                                          k == 0, k == 3)
                        last.then_inc(signal, 1)
            for i in range(NT):
                pe.wait_ge(s_mg, NT + i + 1)
                if i >= 2:
                    pe.wait_ge(s_mT, i - 1)
                if i == 0:
                    pe.wait_ge(s_yad, 2 * NT)
                transpose_rows(zz[:, i, :], i, 2 * (i % 2)).then_inc(s_mtr, 1)
            pe.wait_ge(s_mT, NT)
            for c in range(2):
                project(B_OUT + KH * c, mT, 4 * c, s_z)
            pe.wait_ge(s_zs, 2 * NT)
            for i in range(NT):
                pe.wait_ge(s_xn, NT + i + 1)
                if i >= 2:
                    pe.wait_ge(s_xT, NT + i - 1)
                transpose_rows(zz[:, i, :], i, 4 + 2 * (i % 2)).then_inc(s_xtr, 1)

            pe.wait_ge(s_xT, 2 * NT)
            pe.wait_ge(s_key, 16)

            def score(n):
                for m in range(4):
                    side = (m % 2) * RH + 2 * n + m // 2
                    pe.wait_ge(s_qT, 4 * n + m + 1)
                    if n:
                        pe.wait_ge(s_scs, 4 * (n - 1) + m + 1)
                    for i in range(NT):
                        last = matmul(bank[4 + m][:, i * P:(i + 1) * P], qT[:, m, i * P:(i + 1) * P],
                                      key_sb[:, side, :], True, True)
                    last.then_inc(s_scr, 1)

            for n in range(4):
                for kh in range(KH):
                    j = B_QUERY + KH * n + kh
                    loaded(j)
                    for m in range(4):
                        if n and not kh:
                            pe.wait_ge(s_qT, 4 * (n - 1) + m + 1)
                        for k in range(4):
                            last = matmul(bank[m][:], ring[:, j % RING, k, m * P:(m + 1) * P], xT[:, 4 * kh + k, :],
                                          kh + k == 0, kh and k == 3)
                        if kh:
                            last.then_inc(s_q, 1)
                    if not kh:
                        last.then_inc(s_half, 1)
                score(n)

            def activate(k, e):
                pe.wait_ge(s_ulo, k + 1)
                b = bank[4 + e]
                for d in range(ND):
                    matmul(b[:], u_part[:, e, 0, d, :], xh[:, d, :], d == 0, False)
                    matmul(b[:], u_part[:, e, 0, d, :], xl[:, d, :], False, False)
                    last = matmul(b[:], u_part[:, e, 1, d, :], xh[:, d, :], False, d == ND - 1)
                last.then_inc(s_act, 1)

            def early_pairs(n0, count):
                with pe.Fori(0, count // 2) as it:
                    for t in range(4):
                        activate(it * 4 + (2 * n0 + t), t % 2)

            pe.wait_ge(s_xl, NT)
            pe.wait_ge(s_scs, SIDES)
            early_pairs(0, E_FIRST)
            n0 = E_FIRST
            for i in range(NT):
                pe.wait_ge(s_pk, i + 1)
                for r in range(3):
                    last = nc.tensor.transpose(bank[6][:, r * P:(r + 1) * P], picks[:, r, :], ident[:])
                last.then_inc(s_pkt, 1)
                if i == 0:
                    nc.tensor.sem_inc(s_gmm, QUADS)
                with pe.Fori(0, E_BESIDE // 2) as it:
                    for turn in range(4):
                        activate(it * 4 + (2 * n0 + turn), turn % 2)
                        for q in range(QUADS):
                            done = it * (4 * QUADS) + ((i * TURNS + turn) * QUADS + q + 1)
                            pe.wait_ge(s_hot, done)
                            pe.wait_ge(s_gev, done)
                            for t in range(4):
                                last = matmul(bank[q][:, t * P:(t + 1) * P], hot[:, q, t, 0, :], hot[:, q, t, 1, :],
                                              True, True)
                            last.then_inc(s_gmm, 1)
                n0 += E_BESIDE
                count = E_BETWEEN if i + 1 < NT else E_TAIL
                early_pairs(n0, count)
                n0 += count
            pe.wait_ge(s_gev, QUADS * (1 + NT * TURNS))

            def combine(j, s):
                pe.wait_ge(s_wlo, j * 2 + 2)
                pe.wait_ge(s_vlo, j * 2 + 2)
                for r in range(YJ):
                    pe.wait_ge(s_yd, j * YJ + (r + 1))
                    b = bank[r % YB]
                    tok = slice((r // 2) * P, (r // 2 + 1) * P)
                    col = slice((r % 2) * HALF, (r % 2 + 1) * HALF)
                    for e in range(2):
                        matmul(b[:], w_part[:, s, e, 0, tok], v_part[:, s, e, 0, col], e == 0, False)
                        matmul(b[:], w_part[:, s, e, 0, tok], v_part[:, s, e, 1, col], False, False)
                        last = matmul(b[:], w_part[:, s, e, 1, tok], v_part[:, s, e, 0, col], False, e == 1)
                    last.then_inc(s_y, 1)

            def activate_pair(j):
                for e in range(2):
                    activate(j * 2 + (2 * EARLY + e), e)

            activate_pair(0)
            with pe.Fori(0, FULL // 2 - 1) as it:
                activate_pair(it * 2 + 1)
                combine(it * 2, 0)
                activate_pair(it * 2 + 2)
                combine(it * 2 + 1, 1)
            activate_pair(FULL - 1)
            combine(FULL - 2, 0)
            combine(FULL - 1, 1)
            with pe.Fori(0, EARLY // 2) as it:
                for s in range(2):
                    combine(it * 2 + (FULL + s), s)


def kernel(**inputs):
    import numpy as np
    import concourse.bacc as bacc
    from concourse.bass_utils import run_bass_kernel_spmd

    a = {k: np.ascontiguousarray(v) for k, v in inputs.items()}
    f = np.float32

    def blocks(w, n_chunks=None):
        rows, cols = w.shape
        b = w.reshape(rows // HALF, 4, P, cols // HALF, HALF).transpose(3, 0, 2, 1, 4)
        return b.reshape(cols // HALF, rows // HALF, P, 4 * HALF)

    def stream():
        ada = blocks(a["w_ada"][0])
        w_in = a["w_in"][0]
        pool_w = blocks(w_in[:, 0:HALF])
        lat_w = np.zeros((D, HALF), w_in.dtype)
        lat_w[:, 0:LAT] = w_in[:, HALF:HALF + LAT]
        gates = blocks(w_in[:, HALF + LAT:])
        pool_o, mla_o = blocks(a["w_pool_o"][0]), blocks(a["w_mla_o"][0])
        order = [2 * vec + half for vec in ADA_ORDER for half in range(2)]
        parts = [ada[q] for q in order[:ADA_FIRST]] + [pool_w[0], blocks(lat_w)[0]]
        parts += [ada[q] for q in order[ADA_FIRST:]]
        for c in range(2):
            parts += [gates[c], gates[2 + c], pool_o[c], mla_o[c]]
        parts += list(blocks(a["w_out"][0])) + list(blocks(a["w_query"][0]))
        return np.concatenate(parts, axis=0)

    def tables():
        band = np.zeros((P, 3, POOL_G, P), f)
        for g, w in enumerate((2, 4, 8, 16)):
            for t in range(P):
                for s in range(max(0, t - w + 1), t + 1):
                    band[s, 0, g, t] = f(1) / f(min(t + 1, w))
                    band[s, 1, g, t] = f(1) / f(w)
                for s in range(t - w + 1, 0):
                    band[P + s, 2, g, t] = f(1) / f(w)
                band[t, 0:2, g, t] -= f(1)
        inv = f(1) / (f(10000.0) ** (np.arange(0, ROPE, 2, dtype=f) / f(ROPE)))
        ang = np.arange(SEQ, dtype=f)[:, None] * inv[None, :].astype(f)
        cos, sin = np.cos(ang).astype(f), np.sin(ang).astype(f)
        cos = np.concatenate([cos, cos], 1).reshape(NT, P, ROPE).transpose(1, 0, 2)
        sin = np.concatenate([-sin, sin], 1).reshape(NT, P, ROPE).transpose(1, 0, 2)
        mask = np.where(np.arange(P)[None, :] <= np.arange(P)[:, None], f(0), f(-1e30)).astype(f)
        return band, cos, sin, mask

    band, cos, sin, mask = tables()
    k12 = np.concatenate([a["sub_keys1"][0], a["sub_keys2"][0]], axis=0)
    ins = [
        ("x", a["x"][0]),
        ("c_col", a["c"][0].reshape(ND, P).T),
        ("b_ada", a["b_ada"][0].reshape(6, D)),
        ("g_pre1", a["g_pre1"]), ("g_post1", a["g_post1"]), ("g_pre2", a["g_pre2"]), ("g_post2", a["g_post2"]),
        ("g_q", a["g_q_lat"]), ("g_kv", a["g_kv_lat"]),
        ("wstream", stream()),
        ("w_q_up", a["w_q_up"][0].reshape(2, P, HEADS * QK).transpose(1, 0, 2)),
        ("w_kv_up", a["w_kv_up"][0]),
        ("w_group", a["w_pool_group"][0].transpose(1, 0, 2)),
        ("pool_scale", a["pool_scale"][0].reshape(POOL_G, P).T),
        ("keys", k12.transpose(2, 0, 1)),
        ("pool_band", band), ("rope_cos", cos), ("rope_sin", sin),
        ("ident", np.eye(P, dtype=f)), ("mask", mask),
        ("iota", np.broadcast_to(np.arange(P, dtype=f), (P, P))),
        ("expert_u", a["expert_u"][0].reshape(PAIRS, 2, P, ND, P).transpose(0, 4, 1, 3, 2).reshape(PAIRS, P, 2, D)),
        ("expert_v", a["expert_v"][0].reshape(PAIRS, 2, P, D).transpose(0, 2, 1, 3)),
    ]
    nc = bacc.Bacc("TRN2", target_bir_lowering=False, num_devices=1)
    arrays, args = {}, []
    for name, v in ins:
        v = np.ascontiguousarray(v)
        arrays[f"in_{name}"] = v
        args.append(nc.dram_tensor(f"in_{name}", v.shape, mybir.dt.from_np(v.dtype), kind="ExternalInput").ap())
    args.append(nc.dram_tensor("out_0", (SEQ, D), F32, kind="ExternalOutput").ap())
    build(nc, *args)
    r = run_bass_kernel_spmd(nc, [arrays], core_ids=[0])
    return r.results[0]["out_0"].reshape(1, SEQ, D)
```

```python
from contextlib import ExitStack

import concourse.bass as bass
from concourse import mybir

F32 = mybir.dt.float32
F32R = mybir.dt.float32r
U32 = mybir.dt.uint32
ALU = mybir.AluOpType
ACT = mybir.ActivationFunctionType
AX_X = mybir.AxisListType.X

P = 128
SEQ, D = 512, 1024
NT, ND = SEQ // P, D // P
HALF = 512
POOL_G = 4
Q_LORA, KV_LORA, ROPE = 256, 128, 32
LAT = Q_LORA + KV_LORA + ROPE
HEADS, NOPE, VH = 8, 64, 64
QK = NOPE + ROPE
SM_SCALE = float(QK) ** -0.5
EPS = 1e-6
RH, TOPK, KEYS = 8, 16, 128
SIDES = 2 * RH
NEG = -3.0e38

KH = 2
ADA_FIRST, ADA_ATT, ADA_MERGE = 4, 4, 4
W_IN = 0
W_MERGE = W_IN + 2 * KH
W_OUT = W_MERGE + 2 * 6
W_QUERY = W_OUT + 2 * KH
N_W = W_QUERY + 4 * KH
RING = 3
STREAM = [("A", 0), ("A", 1), ("W", W_IN), ("A", 2), ("A", 3), ("A", 4), ("A", 5), ("A", 6), ("W", W_IN + 1), ("A", 7)]
STREAM += [("W", i) for i in range(W_IN + KH, W_MERGE)]
STREAM += [("A", KH * ADA_FIRST + i) for i in range(KH * ADA_ATT)]
STREAM += [("W", W_MERGE), ("W", W_MERGE + 1)]
for _t in range(KH * ADA_MERGE):
    STREAM += [("A", KH * (ADA_FIRST + ADA_ATT) + _t), ("W", W_MERGE + 2 + _t)]
STREAM += [("W", i) for i in range(W_MERGE + 2 + KH * ADA_MERGE, N_W)]
PLACE = {block: j for j, block in enumerate(STREAM)}
SHIFT1, SCALE1, GATE1, SHIFT2, SCALE2, GATE2 = range(6)
CHUNKS = [(SCALE1, 0), (SHIFT1, 0), (SCALE1, 1), (SHIFT1, 1)]
CHUNKS += [(vec, half) for vec in (GATE1, SHIFT2, SCALE2, GATE2) for half in range(2)]

PAIRS = KEYS // 2
QUADS = 4
TURNS = P // (4 * QUADS)
E_FIRST, E_BETWEEN, E_BESIDE, E_TAIL = 6, 4, TURNS // 2, 6
GOUT = 8
EARLY = E_FIRST + (NT - 1) * E_BETWEEN + NT * E_BESIDE + E_TAIL
FULL = PAIRS - EARLY
OUT_ORDER = [(0, 0), (1, 0), (0, 1), (2, 0), (1, 1), (3, 0), (2, 1), (3, 1)]
OUT_DONE = [max(OUT_ORDER.index((i, c)) for c in range(2)) + 1 for i in range(NT)]
UNITS = NT * HEADS
YJ = NT * 2
YB = 4


def build(nc, x, c_col, b_ada, g_pre1, g_post1, g_pre2, g_post2, g_q, g_kv, wstream, w_q_up, w_kv_up,
          w_group, pool_scale, keys, pool_band, rope_cos, rope_sin, ident_in, mask_in, iota_in,
          expert_u, expert_v, out):
    g_scratch = nc.dram_tensor("g_scratch", (KEYS, KEYS, SEQ), F32, kind="Internal").ap()
    h_scratch = nc.dram_tensor("h_scratch", (P, NT * D), F32, kind="Internal").ap()
    act_scratch = nc.dram_tensor("act_scratch", (EARLY, P, 2 * SEQ), F32, kind="Internal").ap()
    base = (nc.sbuf_base + 31) // 32 * 32

    ctx = ExitStack()
    with ctx:
        def sem(name):
            return ctx.enter_context(nc.semaphore(name))

        def at(name, kb, shape, dt=F32):
            return nc.alloc_sbuf_tensor_at(name, shape, dt, offset=base + int(kb * 1024))

        bank = [ctx.enter_context(nc.psum_tensor(f"bank{i}", [P, HALF], F32)) for i in range(8)]

        h = at("h", 0, [P, NT, D])
        mod = at("mod", 16, [P, 6, D])
        ident = at("ident", 40, [P, P])
        iota = at("iota", 40.5, [P, P])
        stat = at("stat", 41, [P, 96])
        SS1, SSL, SSZ, SSH, SSY = 0, 8, 16, 24, 32
        ones = at("ones", 41.5, [P, P])
        band = at("band", 24, [P, 3, POOL_G, P])
        wgr = at("wgr", 30, [P, POOL_G, P])
        xpool = at("xpool", 32, [P, NT, HALF])
        kc = at("kc", 32, [P, 2, HEADS, QK])
        xh = at("xh", 42, [P, ND, SEQ], F32R)
        xl = at("xl", 58, [P, ND, SEQ], F32R)
        ring = at("ring", 74, [P, RING, 4, HALF])
        w2 = at("w2", 98, [P, 2, 2, 4, HALF], F32R)
        QT = at("QT", 98, [QK, HEADS, SEQ])
        KT = at("KT", 114, [QK, HEADS, SEQ])
        ga = at("ga", 130, [P, 2, D])
        key_sb = at("key_sb", 130, [P, SIDES, KEYS])
        gq = at("gq", 138, [P, Q_LORA])
        gkv = at("gkv", 139, [P, KV_LORA])
        rcos = at("rcos", 139.5, [P, NT, ROPE])
        rsin = at("rsin", 140, [P, NT, ROPE])
        mask = at("mask", 140.5, [P, P])
        csm = at("csm", 141, [P, 2, ND])
        nmax = at("nmax", 141.125, [P, UNITS])
        rsum = at("rsum", 141.25, [P, UNITS])
        rinv = at("rinv", 141.375, [P, UNITS])
        psc = at("psc", 141.5, [P, POOL_G])
        gcol = at("gcol", 142, [P, ND])
        mcol = at("mcol", 142.125, [P, 2, ND])
        xT = at("xT", 186.5, [P, ND, SEQ])
        squares = at("squares", 146.5, [P, 4, D])
        ypT = at("ypT", 146.5, [P, 2, POOL_G, SEQ], F32R)
        oT = at("oT", 162.5, [P, 2, 4, SEQ], F32R)
        wkvu = at("wkvu", 162.5, [P, HEADS * (NOPE + VH)])
        wqu = at("wqu", 166.5, [P, 2, HEADS * QK])
        latT = at("latT", 172.5, [P, 3, SEQ])
        xrow = at("xrow", 178.5, [P, 2, D])
        vv = at("vv", 178.5, [P, NT, HEADS, VH])
        osb = at("osb", 186.5, [P, HEADS, VH])
        mx = at("mx", 188.5, [P, 2, SEQ])
        qs = at("qs", 188.5, [P, 2, HEADS, QK])
        rtmp = at("rtmp", 194.5, [P, 2, HEADS, ROPE])
        pr = at("pr", 188.5, [P, 2, HALF])
        prT = at("prT", 192.5, [P, 2, 4, P])
        lat = at("lat", 196.5, [P, NT, LAT])
        sg = at("sg", 178.5, [P, 3, NT, HALF])
        zz = at("zz", 146.5, [P, NT, D])
        squares2 = at("squares2", 162.5, [P, 4, D])
        qT = at("qT", 16, [P, 4, SEQ])
        scores = at("scores", 138, [P, NT, SIDES, KEYS])
        cand = at("cand", 138, [P, RH, TOPK, TOPK])
        best_v = at("best_v", 146, [P, RH, TOPK])
        best_c = at("best_c", 146.5, [P, RH, TOPK], U32)
        best_ab = at("best_ab", 147, [P, 2, RH, TOPK], U32)
        best_abf = at("best_abf", 148, [P, 2, RH, TOPK])
        picks = at("picks", 149, [P, 3, RH * TOPK])
        gexp = at("gexp", 150.5, [P, 2, RH, TOPK])
        gsum = at("gsum", 151.5, [P, 2, RH])
        picksT = at("picksT", 152, [P, 3, SEQ])
        top_v = at("top_v", 195, [P, NT, SIDES, TOPK])
        top_if = at("top_if", 199, [P, NT, SIDES, TOPK])
        top_i = at("top_i", 203, [P, 2, 4, TOPK], U32)
        hot = at("hot", 16, [P, QUADS, 4, 2, P])
        gate_t = at("gate_t", 74, [P, KEYS, P])
        raw_u = at("raw_u", 0, [P, 2, 2, D])
        u_part = at("u_part", 171, [P, 2, 2, ND, P], F32R)
        gel = at("gel", 187, [P, 2, 2, SEQ])
        raw_v = at("raw_v", 74, [P, 2, 2, D])
        v_part = at("v_part", 90, [P, 2, 2, 2, D], F32R)
        w_part = at("w_part", 122, [P, 2, 2, 2, SEQ], F32R)
        yacc = at("yacc", 138, [P, NT, D])
        g_in = at("g_in", 154, [P, 2, 2, SEQ])
        w_full = at("w_full", 162, [P, 2, SEQ])
        act_in = at("act_in", 195, [P, 2, 2, SEQ])
        squares3 = at("squares3", 74, [P, 4, D])

        s_c = sem("c_loaded")
        s_x = sem("x_loaded")
        s_gc = sem("gain_column_loaded")
        s_g1 = sem("gains1_loaded")
        s_g2 = sem("gain2_loaded")
        s_zero = sem("modulation_zeroed")
        s_bias = sem("bias_loaded")
        s_tab = sem("tables_loaded")
        s_pool_in = sem("pool_tables_loaded")
        s_key = sem("keys_loaded")
        s_ring = [sem(f"block_loaded{i}") for i in range(RING)]
        s_half = sem("half_used")
        s_sig_c = sem("sigmoid_c")
        s_ada = sem("ada_block_used")
        s_adp = sem("ada_psum")
        s_mod = sem("mod_chunk")
        s_whi2 = sem("weight_high")
        s_wlo2 = sem("weight_low")
        s_sq = sem("squares_summed")
        s_var = sem("variance")
        s_std = sem("std")
        s_r1 = sem("rstd1")
        s_xs = sem("x_scaled")
        s_x1tr = sem("x_rows_transposed")
        s_xraw = sem("xT_read")
        s_xm = sem("xT_modulated")
        s_x1h = sem("x1_high")
        s_x1l = sem("x1_low")
        s_x2 = sem("h_scaled")
        s_xn = [sem(f"x_normed{i}") for i in range(2)]
        s_xtr = sem("x_transposed")
        s_xT = sem("xT_high_ready")
        s_xp = sem("xpool_psum")
        s_xps = sem("xpool_ready")
        s_lp = sem("lat_psum")
        s_lat = sem("lat_ready")
        s_mxp = sem("pooled_psum")
        s_mx = sem("pooled_ready")
        s_yp = sem("grouped_psum")
        s_yph = sem("ypT_high")
        s_ypT = sem("ypT_ready")
        s_ln = sem("lat_normed")
        s_ltr = sem("lat_transposed")
        s_latT = sem("latT_ready")
        s_qup = sem("q_up_psum")
        s_kvup = sem("kv_up_psum")
        s_qs = sem("q_rows")
        s_kc = sem("k_rows_read")
        s_rot = sem("rows_rotated")
        s_qtr = sem("q_transposed")
        s_ktr = sem("k_transposed")
        s_QT = sem("QT_ready")
        s_KT = sem("KT_ready")
        s_sc = sem("att_scores")
        s_max = sem("att_max")
        s_exp = sem("att_exp")
        s_ptr = sem("att_p_transposed")
        s_prT = sem("att_prT_ready")
        s_pv = sem("att_pv")
        s_o = sem("att_o_rows")
        s_otr = sem("att_o_transposed")
        s_oTh = sem("oT_high")
        s_oT = sem("oT_ready")
        s_gp = sem("gates_psum")
        s_sg = sem("sigmoids_ready")
        s_ya = sem("mixer_a_psum")
        s_yb = sem("mixer_b_psum")
        s_yad = sem("mixer_a_read")
        s_mg = sem("merged")
        s_z = sem("out_psum")
        s_zs = sem("out_rows")
        s_h1 = sem("h_updated")
        s_xl = sem("x_low_ready")
        s_q = sem("query_psum")
        s_qT = sem("query_ready")
        s_scr = sem("scores_psum")
        s_scs = sem("scores_ready")
        s_top = sem("side_searched")
        s_bv = sem("picks_shifted")
        s_ge = sem("picks_exp")
        s_pk = sem("picks_ready")
        s_pkt = sem("picks_transposed")
        s_hot = sem("onehots")
        s_gmm = sem("gate_products")
        s_gev = sem("gate_read")
        s_gout = sem("gate_stored")
        s_hout = sem("h_stored")
        s_hin = sem("h_back")
        s_spill = [sem(f"early_gelu_stored{i}") for i in range(2)]
        s_al = [sem(f"early_gelu_back{i}") for i in range(2)]
        s_ul = [sem(f"u_loaded{i}") for i in range(2)]
        s_vl = [sem(f"v_loaded{i}") for i in range(2)]
        s_gl = [sem(f"g_loaded{i}") for i in range(2)]
        s_uhi = sem("u_high")
        s_ulo = sem("u_low")
        s_vhi = sem("v_high")
        s_vlo = sem("v_low")
        s_act = sem("expert_act")
        s_gelu = sem("expert_gelu")
        s_w = sem("expert_w")
        s_whi = sem("w_high")
        s_wlo = sem("w_low")
        s_y = sem("y_piece")
        s_yd = sem("y_added")
        s_ys = sem("y_scaled")
        s_fin = sem("out_ready")
        s_fin3 = sem("last_out_ready")
        s_out = sem("out_stored")
        s_chain = sem("dve_chain")

        freed = []

        def two(signal, value):
            halves = sum(1 for x in freed if x[0] is s_half)
            freed.extend([(s_half, halves + 1), (signal, value)])

        two(s_xp, NT)
        two(s_lp, NT)
        for c in range(2):
            two(s_gp, NT * (2 * c + 1))
            two(s_gp, NT * (2 * c + 2))
            freed += [(s_ya, NT * (c + 1)), (s_yb, NT * (c + 1))]
        for _ in range(2):
            freed.append((s_half, sum(1 for x in freed if x[0] is s_half) + 1))
        freed += [(s_z, OUT_ORDER.index((NT - 1, c)) + 1) for c in range(2)]
        for n in range(4):
            two(s_q, 4 * (n + 1))
        assert len(freed) == N_W

        SCORE_BANK = (0, 1, 6)
        ADA_BANK = [4, 5, 6, 7] + [7] * ADA_ATT + [4, 5, 6, 7]
        ATT_ADA = 4 * KH + 1
        STEPS = UNITS + 6

        block = ctx.enter_context(nc.Block())

        @block.sync
        def _(sp):
            sp.dma_start(csm[:, 0, :], c_col).then_inc(s_c, 16)

            sp.dma_start(ident[:], ident_in).then_inc(s_x, 16)
            for i in range(NT):
                sp.dma_start(h[:, i, :], x[i * P:(i + 1) * P, :]).then_inc(s_x, 16)
            sp.wait_ge(s_zero, 1)
            sp.dma_start(mod[0:1, 0:2, :], b_ada[0:2, :].unsqueeze(0)).then_inc(s_bias, 16)
            sp.dma_start(gcol[:], g_pre1).then_inc(s_gc, 16)

            def tables():
                for dst, src in ((band, pool_band), (wgr, w_group), (psc, pool_scale)):
                    sp.dma_start(dst[:], src).then_inc(s_pool_in, 16)
                sp.dma_start(gq[:], g_q.to_broadcast([P, Q_LORA])).then_inc(s_tab, 16)
                sp.dma_start(gkv[:], g_kv.to_broadcast([P, KV_LORA])).then_inc(s_tab, 16)
                for dst, src in ((rcos, rope_cos), (rsin, rope_sin), (wkvu, w_kv_up), (wqu, w_q_up),
                                 (mask, mask_in), (iota, iota_in)):
                    sp.dma_start(dst[:], src).then_inc(s_tab, 16)
                sp.dma_start(ga[:, 0, :], g_pre2.to_broadcast([P, D])).then_inc(s_g1, 16)
                sp.dma_start(ga[:, 1, :], g_post1.to_broadcast([P, D])).then_inc(s_g1, 16)

            for j, (kind, b) in enumerate(STREAM):
                if j >= RING:
                    k0, b0 = STREAM[j - RING]
                    sp.wait_ge(s_ada if k0 == "A" else s_wlo2, b0 + 1)
                sp.dma_start(ring[:, j % RING, :, :], wstream[j].rearrange("p (k n) -> p k n", k=4)
                             ).then_inc(s_ring[j % RING], 16)
                if (kind, b) == ("W", W_IN + KH):
                    tables()
                if (kind, b) == ("A", KH * ADA_FIRST + RING - 1):
                    sp.wait_ge(s_zero, 2)
                    sp.dma_start(mod[0:1, 2:4, :], b_ada[2:4, :].unsqueeze(0)).then_inc(s_bias, 16)
                if (kind, b) == ("W", W_MERGE):
                    sp.wait_ge(s_zero, 3)
                    sp.dma_start(mod[0:1, 4:6, :], b_ada[4:6, :].unsqueeze(0)).then_inc(s_bias, 16)
                if (kind, b) == ("W", W_MERGE + 2):
                    sp.wait_ge(s_mod, ADA_FIRST + 2)
                    sp.dma_start(ga[:, 1, :], g_post2.to_broadcast([P, D])).then_inc(s_g2, 16)
                if (kind, b) == ("W", W_QUERY + 1):
                    sp.wait_ge(s_mod, len(CHUNKS))
                    sp.dma_start(key_sb[:], keys).then_inc(s_key, 16)
            sp.wait_ge(s_h1, NT)
            sp.dma_start(h_scratch, h[:].rearrange("p i n -> p (i n)")).then_inc(s_hout, 16)
            sp.wait_ge(s_hout, 16)
            for i in range(2):
                sp.wait_ge(s_xn[i], 2)

            def load_u(n, s):
                sp.dma_start(raw_u[:, s, :, :], expert_u[bass.ds(n, 1)].rearrange("o p e n -> (o p) e n")
                             ).then_inc(s_ul[s], 16)

            def early_pair(n, s):
                sp.wait_ge(s_ulo, n * 2 + 2)
                load_u(n + 2, s)
                sp.wait_ge(s_gelu, n * 2 + 2)
                sp.dma_start(act_scratch[bass.ds(n, 1)].rearrange("o p n -> (o p) n"),
                             gel[:, s, :, :].rearrange("p e n -> p (e n)")).then_inc(s_spill[s], 16)

            def early_pairs(n0, count, tokens=None):
                with sp.Fori(0, count // 2) as it:
                    for s in range(2):
                        early_pair(it * 2 + (n0 + s), s)
                        if tokens is not None:
                            for r in range(2):
                                i1 = it * (4 * KEYS // GOUT) + (2 * s + r) * (KEYS // GOUT)
                                sp.dma_start(g_scratch[bass.ds(i1, KEYS // GOUT), :, tokens].rearrange("a b t -> b a t"),
                                             gate_t[:, bass.ds(i1, KEYS // GOUT), :]).then_inc(s_gout, 16)

            for s in range(2):
                load_u(s, s)
            early_pairs(0, E_FIRST + E_BESIDE)
            n0 = E_FIRST + E_BESIDE
            for i in range(NT):
                sp.wait_ge(s_gev, QUADS + QUADS * TURNS * (i + 1))
                early_pairs(n0, GOUT // 2, slice(i * P, (i + 1) * P))
                n0 += GOUT // 2
                rest = (E_BETWEEN + E_BESIDE if i + 1 < NT else E_TAIL) - GOUT // 2
                early_pairs(n0, rest)
                n0 += rest
            sp.wait_ge(s_gout, 16 * GOUT * NT)

            def load_v(n, s):
                sp.dma_start(raw_v[:, s, :, :], expert_v[bass.ds(n, 1)].rearrange("o p e n -> (o p) e n")
                             ).then_inc(s_vl[s], 16)

            def load_g(n, s):
                sp.dma_start(g_in[:, s, :, :], g_scratch[bass.ds(n * 2, 2), :, :].rearrange("a b t -> b a t")
                             ).then_inc(s_gl[s], 16)

            def load_act(n, s):
                sp.dma_start(act_in[:, s, :, :].rearrange("p e n -> p (e n)"),
                             act_scratch[bass.ds(n, 1)].rearrange("o p n -> (o p) n")).then_inc(s_al[s], 16)

            def slot_free(j):
                sp.wait_ge(s_vlo, j * 2 + 2)
                sp.wait_ge(s_w, j * 2 + 2)

            for s in range(2):
                load_g(EARLY + s, s)
                load_v(EARLY + s, s)
            with sp.Fori(0, FULL // 2 - 1) as it:
                for s in range(2):
                    sp.wait_ge(s_ulo, it * 4 + (2 * (EARLY + s) + 2))
                    load_u(it * 2 + (EARLY + s + 2), s)
                    slot_free(it * 2 + s)
                    load_g(it * 2 + (EARLY + s + 2), s)
                    load_v(it * 2 + (EARLY + s + 2), s)
            for s in range(2):
                load_act(s, s)
                slot_free(FULL - 2 + s)
                load_g(s, s)
                load_v(s, s)
            sp.wait_ge(s_ulo, 2 * PAIRS)
            sp.wait_ge(s_hout, 16)
            sp.dma_start(h[:].rearrange("p i n -> p (i n)"), h_scratch).then_inc(s_hin, 16)
            with sp.Fori(0, EARLY // 2 - 1) as it:
                for s in range(2):
                    slot_free(it * 2 + (FULL + s))
                    load_act(it * 2 + (s + 2), s)
                    load_g(it * 2 + (s + 2), s)
                    load_v(it * 2 + (s + 2), s)
            for i in range(NT - 1):
                sp.wait_ge(s_fin, i + 1)
                sp.dma_start(out[i * P:(i + 1) * P, :], h[:, i, :]).then_inc(s_out, 16)
            for c in range(2):
                sp.wait_ge(s_fin3, c + 1)
                cols = slice(c * HALF, (c + 1) * HALF)
                sp.dma_start(out[(NT - 1) * P:, cols], h[:, NT - 1, cols]).then_inc(s_out, 16)
            sp.wait_ge(s_out, 16 * (NT + 1))

        @block.gpsimd
        def _(pool):
            nc.gpsimd.memset(ones[:], 1.0)
            nc.gpsimd.memset(mod[:, 0:2, :], 0.0).then_inc(s_zero, 1)

            def low_weight(b):
                pool.wait_ge(s_whi2, b + 1)
                nc.gpsimd.tensor_tensor(w2[:, b % 2, 1, :, :], ring[:, PLACE["W", b] % RING, :, :],
                                        w2[:, b % 2, 0, :, :].bitcast(F32), ALU.subtract).then_inc(s_wlo2, 1)

            for b in range(N_W):
                if b == W_MERGE:
                    pool.wait_ge(s_yp, POOL_G)
                    nc.gpsimd.memset(mod[:, 2:4, :], 0.0).then_inc(s_zero, 1)
                    pool.wait_ge(s_ktr, NT)
                    nc.gpsimd.memset(mod[:, 4:6, :], 0.0).then_inc(s_zero, 1)
                if b == W_QUERY:
                    for i in range(2):
                        pool.wait_ge(s_x2, i + 1)
                        nc.gpsimd.tensor_tensor(zz[:, i, :], zz[:, i, :], mod[:, SHIFT2, :], ALU.add).then_inc(s_xn[0], 1)
                low_weight(b)
                if b == 0:
                    for d in range(ND // 2):
                        pool.wait_ge(s_x1h, d + 1)
                        nc.gpsimd.tensor_tensor(xl[:, d, :], xT[:, d, :], xh[:, d, :].bitcast(F32), ALU.subtract
                                                ).then_inc(s_x1l, 1)

            def low_u(k, s, e):
                pool.wait_ge(s_uhi, k + 1)
                hi, lo = (u_part[:, e, r, :, :].rearrange("p k n -> p (k n)") for r in (0, 1))
                nc.gpsimd.tensor_tensor(lo, raw_u[:, s, e, :], hi.bitcast(F32), ALU.subtract).then_inc(s_ulo, 1)

            def low_v(j, s):
                for e in range(2):
                    pool.wait_ge(s_vhi, j * 2 + (e + 1))
                    nc.gpsimd.tensor_tensor(v_part[:, s, e, 1, :], raw_v[:, s, e, :],
                                            v_part[:, s, e, 0, :].bitcast(F32), ALU.subtract).then_inc(s_vlo, 1)

            with pool.Fori(0, EARLY // 2) as it:
                for s in range(2):
                    for e in range(2):
                        low_u(it * 4 + (2 * s + e), s, e)
            def low_pair(p, s):
                for e in range(2):
                    low_u(p * 2 + (2 * EARLY + e), s, e)

            low_pair(0, 0)
            low_pair(1, 1)
            low_v(0, 0)
            with pool.Fori(0, FULL // 2 - 1) as it:
                for s in range(2):
                    low_v(it * 2 + (s + 1), 1 - s)
                    low_pair(it * 2 + (s + 2), s)
            low_v(FULL - 1, 1)
            with pool.Fori(0, EARLY // 2) as it:
                for s in range(2):
                    low_v(it * 2 + (FULL + s), s)
            pool.wait_ge(s_hin, 16)
            for i in range(NT - 1):
                pool.wait_ge(s_ys, i + 1)
                nc.gpsimd.tensor_tensor(h[:, i, :], h[:, i, :], yacc[:, i, :], ALU.add).then_inc(s_fin, 1)

        @block.scalar
        def _(act):
            a = nc.scalar
            act.wait_ge(s_c, 16)
            a.activation(csm[:, 1, :], csm[:, 0, :], ACT.Sigmoid).then_inc(s_sig_c, 1)

            def high_weight(b):
                j = PLACE["W", b]
                act.wait_ge(s_ring[j % RING], 16 * (j // RING + 1))
                if b >= 2:
                    act.wait_ge(*freed[b - 2])
                a.activation(w2[:, b % 2, 0, :, :], ring[:, j % RING, :, :], ACT.Copy).then_inc(s_whi2, 1)

            def high_x(i, n, b0):
                act.wait_ge(s_xtr, n)
                for b in range(2):
                    last = a.activation(xh[:, 4 * b:4 * b + 4, i * P:(i + 1) * P],
                                        bank[b0 + b][:].rearrange("p (k t) -> p k t", k=4), ACT.Copy)
                last.then_inc(s_xT, 1)

            act.wait_ge(s_x, 16 * (NT + 1))
            for i in range(NT):
                last = a.activation(squares[:, i, :], h[:, i, :], ACT.Square, accum_out=stat[:, SS1 + i:SS1 + i + 1])
            last.then_inc(s_sq, 1)
            act.wait_ge(s_var, 1)
            a.activation(stat[:, SS1:SS1 + 4], stat[:, SS1:SS1 + 4], ACT.Sqrt).then_inc(s_std, 1)

            def scale_x(i):
                if i >= 2:
                    act.wait_ge(s_x1tr, i - 1)
                a.activation(xrow[:, i % 2, :], h[:, i, :], ACT.Copy, scale=stat[:, SS1 + i:SS1 + i + 1]
                             ).then_inc(s_xs, 1)

            def read_xT(i):
                act.wait_ge(s_x1tr, i + 1)
                for b in range(2):
                    last = a.activation(xT[:, 4 * b:4 * b + 4, i * P:(i + 1) * P],
                                        bank[2 * i + b][:].rearrange("p (k t) -> p k t", k=4), ACT.Copy)
                last.then_inc(s_xraw, 1)

            def high_x1(d):
                act.wait_ge(s_xm, d + 1)
                a.activation(xh[:, d, :], xT[:, d, :], ACT.Copy).then_inc(s_x1h, 1)

            act.wait_ge(s_r1, 1)
            scale_x(0)
            scale_x(1)
            high_weight(0)
            read_xT(0)
            scale_x(2)
            read_xT(1)
            scale_x(3)
            read_xT(2)
            read_xT(3)
            for d in range(ND // 2):
                high_x1(d)
            high_weight(1)
            for d in range(ND // 2, ND):
                high_x1(d)
            high_weight(2)
            act.wait_ge(s_pool_in, 48)
            for i in range(NT):
                act.wait_ge(s_xp, i + 1)
                a.activation(xpool[:, i, :], bank[i][:], ACT.Copy).then_inc(s_xps, 1)
            high_weight(3)
            for i in range(NT):
                act.wait_ge(s_lat, i + 1)
                a.activation(squares[:, i, 0:Q_LORA], lat[:, i, 0:Q_LORA], ACT.Square,
                             accum_out=stat[:, SSL + i:SSL + i + 1])
                last = a.activation(squares[:, i, Q_LORA:Q_LORA + KV_LORA], lat[:, i, Q_LORA:Q_LORA + KV_LORA],
                                    ACT.Square, accum_out=stat[:, SSL + NT + i:SSL + NT + i + 1])
            last.then_inc(s_sq, 1)
            act.wait_ge(s_var, 2)
            a.activation(stat[:, SSL:SSL + 2 * NT], stat[:, SSL:SSL + 2 * NT], ACT.Sqrt).then_inc(s_std, 1)
            for g in range(POOL_G):
                act.wait_ge(s_yp, g + 1)
                a.activation(ypT[:, 0, g, :], bank[2 + g % 2][:], ACT.Copy, scale=psc[:, g:g + 1]).then_inc(s_yph, 1)
            for i in range(NT):
                act.wait_ge(s_ltr, i + 1)
                a.activation(latT[:, :, i * P:(i + 1) * P],
                             bank[4 + i][:, 0:3 * P].rearrange("p (k t) -> p k t", k=3), ACT.Copy).then_inc(s_latT, 1)

            def q_rows(i):
                act.wait_ge(s_qup, i + 1)
                if i >= 2:
                    act.wait_ge(s_qtr, i - 1)
                for b in range(2):
                    last = a.activation(qs[:, i % 2, 4 * b:4 * b + 4, :],
                                        bank[b][:, 0:4 * QK].rearrange("p (h n) -> p h n", h=4), ACT.Copy,
                                        scale=SM_SCALE)
                last.then_inc(s_qs, 1)

            def read_QT(i):
                act.wait_ge(s_qtr, i + 1)
                for b in range(2):
                    last = a.activation(QT[:, 4 * b:4 * b + 4, i * P:(i + 1) * P],
                                        bank[4 + b][0:QK, :].rearrange("p (h t) -> p h t", h=4), ACT.Copy)
                last.then_inc(s_QT, 1)

            act.wait_ge(s_mx, POOL_G)
            q_rows(0)
            for i in range(NT):
                if i + 1 < NT:
                    q_rows(i + 1)
                read_QT(i)

            for u in range(STEPS):
                w = u - 2
                if 0 <= w < UNITS:
                    n = w // HEADS + 1
                    act.wait_ge(s_ptr, w + 1)
                    if w >= 2:
                        act.wait_ge(s_pv, w - 1)
                    a.activation(prT[:, w % 2, 0:n, :], bank[2 + w % 2][:, 0:n * P].rearrange("p (k t) -> p k t", k=n),
                                 ACT.Copy).then_inc(s_prT, 1)
                if u < UNITS:
                    n = (u // HEADS + 1) * P
                    act.wait_ge(s_max, u + 1)
                    if u >= 2:
                        act.wait_ge(s_ptr, u - 1)
                    a.activation(pr[:, u % 2, 0:n], bank[SCORE_BANK[u % 3]][:, 0:n], ACT.Exp,
                                 bias=nmax[:, u:u + 1], accum_out=rsum[:, u:u + 1]).then_inc(s_exp, 1)
                if u >= HEADS + 3 and (u - HEADS - 3) % HEADS == 0:
                    i = (u - HEADS - 3) // HEADS
                    act.wait_ge(s_otr, i + 1)
                    a.activation(oT[:, 0, :, i * P:(i + 1) * P], bank[4 + i % 2][:].rearrange("p (k t) -> p k t", k=4),
                                 ACT.Copy).then_inc(s_oTh, 1)
                if u == UNITS + 1:
                    act.wait_ge(s_sc, UNITS)
                    high_weight(W_MERGE)
            high_weight(W_MERGE + 1)

            b = W_MERGE + 2
            for c in range(2):
                for g in range(2):
                    high_weight(b)
                    for i in range(NT):
                        act.wait_ge(s_gp, NT * (2 * c + g) + i + 1)
                        if c and g == 0:
                            act.wait_ge(s_mg, i + 1)
                        a.activation(sg[:, c + g, i, :], bank[4 * g + i][:], ACT.Sigmoid).then_inc(s_sg, 1)
                    high_weight(b + 1)
                    b += 2
                high_weight(b)
                high_weight(b + 1)
                b += 2
            for i in range(NT):
                high_x(i, i + 1, 2 * (i % 2))
            for _ in range(2):
                high_weight(b)
                b += 1
            stage = [2]

            def root(col):
                stage[0] += 1
                act.wait_ge(s_var, stage[0])
                a.activation(stat[:, col:col + 1], stat[:, col:col + 1], ACT.Sqrt).then_inc(s_std, 1)

            def out_rows(i):
                act.wait_ge(s_z, OUT_DONE[i])
                for c in range(2):
                    last = a.activation(zz[:, i, c * HALF:(c + 1) * HALF], bank[4 * c + i][:], ACT.Copy)
                last.then_inc(s_zs, 1)
                act.wait_ge(s_zs, i + 1)
                a.activation(squares2[:, i, :], zz[:, i, :], ACT.Square,
                             accum_out=stat[:, SSZ + i:SSZ + i + 1]).then_inc(s_sq, 1)
                root(SSZ + i)

            def new_rows(i):
                act.wait_ge(s_h1, i + 1)
                a.activation(squares2[:, i, :], h[:, i, :], ACT.Square,
                             accum_out=stat[:, SSH + i:SSH + i + 1]).then_inc(s_sq, 1)
                root(SSH + i)

            out_rows(0)
            out_rows(1)
            new_rows(0)
            out_rows(2)
            out_rows(3)
            new_rows(1)
            new_rows(2)
            high_weight(b)
            new_rows(3)
            for i in range(NT):
                high_x(i, NT + i + 1, 2 * i)
            high_weight(b + 1)
            b += 2
            def high_u(k, s, e, loads):
                act.wait_ge(s_ul[s], loads)
                a.activation(u_part[:, e, 0, :, :].rearrange("p k n -> p (k n)"), raw_u[:, s, e, :],
                             ACT.Copy).then_inc(s_uhi, 1)

            for n in range(4):
                if b < N_W:
                    high_weight(b)
                if n == 3:
                    for e in range(2):
                        high_u(e, 0, e, 16)
                for m in range(4):
                    act.wait_ge(s_q, 4 * n + m + 1)
                    if n:
                        act.wait_ge(s_scr, 4 * (n - 1) + m + 1)
                    a.activation(qT[:, m, :], bank[m][:], ACT.Copy).then_inc(s_qT, 1)
                if b < N_W:
                    high_weight(b + 1)
                b += 2
            def gelu(k, s, e):
                act.wait_ge(s_act, k + 1)
                a.activation(gel[:, s, e, :], bank[4 + e][:], ACT.Gelu_apprx_tanh).then_inc(s_gelu, 1)

            def early_tile(n, s, e, loads, stored):
                if e == 0 and stored is not None:
                    act.wait_ge(s_spill[s], stored)
                gelu(n * 2 + e, s, e)
                high_u(n * 2 + (e + 2), 1 - s, e, loads)

            def early_pair(it16, n, s, n0):
                for e in range(2):
                    early_tile(n, s, e, it16 + 8 * n0 + (16 if s == 0 else 32), it16 + 8 * n0)

            def early_pairs(n0, count):
                with act.Fori(0, count // 2) as it:
                    for s in range(2):
                        early_pair(it * 16, it * 2 + (n0 + s), s, n0)

            for n in range(2):
                for e in range(2):
                    early_tile(n, n, e, 16 if n == 0 else 32, None)
            def picks_exp(i):
                act.wait_ge(s_bv, i + 1)
                a.activation(gexp[:, 1, :, :], gexp[:, 0, :, :], ACT.Exp).then_inc(s_ge, 1)

            early_pairs(2, E_FIRST - 4)
            picks_exp(0)
            early_pairs(E_FIRST - 2, 2)
            n0 = E_FIRST
            for i in range(NT):
                if i == 0:
                    a.sem_inc(s_gev, QUADS)
                else:
                    act.wait_ge(s_gout, 16 * GOUT * i)
                with act.Fori(0, E_BESIDE // 2) as it:
                    for s in range(2):
                        for e in range(2):
                            early_tile(it * 2 + (n0 + s), s, e, it * 16 + (8 * n0 + (16 if s == 0 else 32)),
                                       it * 16 + 8 * n0)
                            turn = 2 * s + e
                            for q in range(QUADS):
                                act.wait_ge(s_gmm, it * (4 * QUADS) +
                                            (QUADS + (i * TURNS + turn) * QUADS + q + 1))
                                a.activation(gate_t[:, :, bass.ds(it * (16 * QUADS) + (turn * 4 * QUADS + 4 * q), 4)],
                                             bank[q][:].rearrange("p (t k) -> p k t", t=4),
                                             ACT.Copy).then_inc(s_gev, 1)
                n0 += E_BESIDE
                if i + 1 < NT:
                    early_pairs(n0, E_BETWEEN - 2)
                    picks_exp(i + 1)
                    early_pairs(n0 + E_BETWEEN - 2, 2)
                    n0 += E_BETWEEN
                else:
                    early_pairs(n0, E_TAIL)

            def high_v(j, s, loads):
                act.wait_ge(s_vl[s], loads)
                for e in range(2):
                    a.activation(v_part[:, s, e, 0, :], raw_v[:, s, e, :], ACT.Copy).then_inc(s_vhi, 1)

            def high_w(j, s, e):
                act.wait_ge(s_w, j * 2 + (e + 1))
                a.activation(w_part[:, s, e, 0, :], w_full[:, e, :], ACT.Copy).then_inc(s_whi, 1)

            def full_pair(j, s, loads_u, loads_v, passed):
                for e in range(2):
                    gelu(j * 2 + (2 * EARLY + e), s, e)
                    if loads_u is not None:
                        high_u(j * 2 + (2 * EARLY + e + 2), 1 - s, e, loads_u)
                    high_w(j, s, e)
                if passed is None:
                    high_v(0, 0, 16)
                else:
                    act.wait_ge(s_y, passed)
                high_v(j + 1, 1 - s, loads_v)

            act.wait_ge(s_spill[0], 8 * EARLY)
            act.wait_ge(s_spill[1], 8 * EARLY)
            full_pair(0, 0, 8 * EARLY + 16, 16, None)
            with act.Fori(0, FULL // 2 - 1) as it:
                full_pair(it * 2 + 1, 1, it * 16 + (8 * EARLY + 32), it * 16 + 32, it * (2 * YJ) + YJ)
                full_pair(it * 2 + 2, 0, it * 16 + (8 * EARLY + 32), it * 16 + 32, it * (2 * YJ) + 2 * YJ)
            full_pair(FULL - 1, 1, None, 8 * FULL + 16, YJ * (FULL - 1))
            with act.Fori(0, EARLY // 2 - 1) as it:
                for s in range(2):
                    j = it * 2 + (FULL + s)
                    for e in range(2):
                        high_w(j, s, e)
                    act.wait_ge(s_y, j * YJ)
                    high_v(j + 1, 1 - s, it * 16 + (8 * FULL + (16 if s == 0 else 32)))
            for e in range(2):
                high_w(PAIRS - 2, 0, e)
            act.wait_ge(s_y, YJ * (PAIRS - 2))
            high_v(PAIRS - 1, 1, 8 * PAIRS)
            for e in range(2):
                high_w(PAIRS - 1, 1, e)
            for i in range(NT):
                act.wait_ge(s_yd, YB + YJ * (PAIRS - 1) + 2 * (i + 1))
                a.activation(squares3[:, i, :], yacc[:, i, :], ACT.Square,
                             accum_out=stat[:, SSY + i:SSY + i + 1]).then_inc(s_sq, 1)
                root(SSY + i)

        @block.vector
        def _(dve):
            v = nc.vector
            count = [0]

            def link(ins):
                count[0] += 1
                ins.then_inc(s_chain, 1)
                dve.wait_ge(s_chain, count[0])

            def rstd(col, n, width, stage, signal=None):
                dve.wait_ge(s_sq, stage)
                for k, w in enumerate(width):
                    last = v.tensor_scalar(stat[:, col + n * k:col + n * (k + 1)], stat[:, col + n * k:col + n * (k + 1)],
                                           1.0 / w, EPS, ALU.mult, ALU.add)
                last.then_inc(s_var, 1)
                dve.wait_ge(s_std, stage)
                m = n * len(width)
                last = v.reciprocal(stat[:, col:col + m], stat[:, col:col + m])
                if signal is None:
                    link(last)
                else:
                    last.then_inc(signal, 1)

            def scaled(o, rows, r, g):
                return v.scalar_tensor_tensor(o, rows, r, g, ALU.mult, ALU.mult)

            dve.wait_ge(s_sig_c, 1)
            link(v.tensor_tensor(csm[:, 1, :], csm[:, 0, :], csm[:, 1, :], ALU.mult))

            before = []

            def ada_piece(i, k):
                q, kh = divmod(i, KH)
                vec, half = CHUNKS[q]
                j = PLACE["A", i]
                m = mod[:, vec, half * HALF:(half + 1) * HALF]
                if k == 0:
                    dve.wait_ge(s_ring[j % RING], 16 * (j // RING + 1))
                if before:
                    dve.wait_ge(*before.pop())
                last = v.scalar_tensor_tensor(m, ring[:, j % RING, k, :],
                                              csm[:, 1, 4 * kh + k:4 * kh + k + 1], m, ALU.mult, ALU.add)
                if k < 3:
                    count[0] += 1
                    last.then_inc(s_chain, 1)
                    before.append((s_chain, count[0]))
                else:
                    last.then_inc(s_ada, 1)
                    before.append((s_ada, i + 1))

            def ada_block(i):
                for k in range(4):
                    ada_piece(i, k)

            def ada_column(q):
                dve.wait_ge(s_adp, q + 1)
                vec, half = CHUNKS[q]
                cols = slice(4 * half, 4 * half + 4)
                p = bank[ADA_BANK[q]][:, 4 * q:4 * q + 4]
                if vec == SCALE1:
                    v.scalar_tensor_tensor(mcol[:, 0, cols], p, 1.0, gcol[:, cols], ALU.add, ALU.mult
                                           ).then_inc(s_mod, 1)
                else:
                    v.tensor_copy(mcol[:, 1, cols], p).then_inc(s_mod, 1)

            def ada_back(q):
                dve.wait_ge(s_adp, q + 1)
                vec, half = CHUNKS[q]
                cols = slice(half * HALF, (half + 1) * HALF)
                m, p = mod[:, vec, cols], bank[ADA_BANK[q]][:]
                if vec == SCALE2:
                    last = v.scalar_tensor_tensor(m, p, 1.0, ga[:, 0, cols], ALU.add, ALU.mult)
                elif vec in (GATE1, GATE2):
                    last = v.tensor_tensor(m, p, ga[:, 1, cols], ALU.mult)
                else:
                    last = v.tensor_copy(m, p)
                last.then_inc(s_mod, 1)

            def low_x(i, n, b0):
                dve.wait_ge(s_xT, n)
                for b in range(2):
                    k = slice(4 * b, 4 * b + 4)
                    last = v.tensor_tensor(xl[:, k, i * P:(i + 1) * P],
                                           bank[b0 + b][:].rearrange("p (k t) -> p k t", k=4),
                                           xh[:, k, i * P:(i + 1) * P].bitcast(F32), ALU.subtract)
                last.then_inc(s_xl, 1)

            def low_x1(d):
                dve.wait_ge(s_x1h, d + 1)
                v.tensor_tensor(xl[:, d, :], xT[:, d, :], xh[:, d, :].bitcast(F32), ALU.subtract).then_inc(s_x1l, 1)

            dve.wait_ge(s_bias, 16)
            ada_block(0)
            rstd(SS1, NT, [D], 1, s_r1)
            for c in range(2):
                for i in range(1 if c == 0 else 2 * KH + 2, 2 * KH * (c + 1)):
                    ada_block(i)
                if c == 0:
                    dve.wait_ge(s_gc, 16)
                for q in range(2 * c, 2 * c + 2):
                    ada_column(q)
                dve.wait_ge(s_mod, 2 * c + 2)
                if c == 0:
                    dve.wait_ge(s_xraw, NT)
                else:
                    dve.wait_ge(s_x1l, ND // 2)
                for d in range(4 * c, 4 * c + 4):
                    v.tensor_scalar(xT[:, d, :], xT[:, d, :], mcol[:, 0, d:d + 1], mcol[:, 1, d:d + 1],
                                    ALU.mult, ALU.add).then_inc(s_xm, 1)
                    if c == 0:
                        for n in range(2 * d, 2 * d + 2):
                            ada_piece(2 * KH + n // 4, n % 4)
                    elif d > 4:
                        low_x1(d - 1)
            low_x1(ND - 1)
            for i in range(NT):
                dve.wait_ge(s_lp, i + 1)
                v.tensor_copy(lat[:, i, :], bank[4 + i][:, 0:LAT]).then_inc(s_lat, 1)
            dve.wait_ge(s_tab, 16 * 8)

            def low_yp(g):
                dve.wait_ge(s_yph, g + 1)
                v.scalar_tensor_tensor(ypT[:, 1, g, :], bank[2 + g % 2][:], psc[:, g:g + 1],
                                       ypT[:, 0, g, :].bitcast(F32), ALU.mult, ALU.subtract).then_inc(s_ypT, 1)

            for g in range(2):
                dve.wait_ge(s_mxp, g + 1)
                v.tensor_copy(mx[:, g % 2, :], bank[g % 2][:]).then_inc(s_mx, 1)
            rstd(SSL, NT, [Q_LORA, KV_LORA], 2)
            for g in range(2, POOL_G):
                dve.wait_ge(s_mxp, g + 1)
                dve.wait_ge(s_yp, g - 1)
                v.tensor_copy(mx[:, g % 2, :], bank[g % 2][:]).then_inc(s_mx, 1)
                low_yp(g - 2)
            for i in range(NT):
                scaled(lat[:, i, 0:Q_LORA], lat[:, i, 0:Q_LORA], stat[:, SSL + i:SSL + i + 1], gq[:])
                scaled(lat[:, i, Q_LORA:Q_LORA + KV_LORA], lat[:, i, Q_LORA:Q_LORA + KV_LORA],
                       stat[:, SSL + NT + i:SSL + NT + i + 1], gkv[:]).then_inc(s_ln, 1)
            for g in range(2, POOL_G):
                low_yp(g)
            HR = ROPE // 2

            def rotate(rows, i, nh):
                def tab(t, lo, hi):
                    return t[:, i:i + 1, lo:hi].to_broadcast([P, nh, hi - lo])
                t1, t2 = rtmp[:, 0, 0:nh, :], rtmp[:, 1, 0:nh, :]
                v.tensor_tensor(t1, rows, tab(rcos, 0, ROPE), ALU.mult)
                v.tensor_tensor(t2[:, :, 0:HR], rows[:, :, HR:ROPE], tab(rsin, 0, HR), ALU.mult)
                link(v.tensor_tensor(t2[:, :, HR:ROPE], rows[:, :, 0:HR], tab(rsin, HR, ROPE), ALU.mult))
                return v.tensor_tensor(rows, t1, t2, ALU.add)

            def kv_rows(i):
                dve.wait_ge(s_kvup, i + 1)
                if i >= 2:
                    dve.wait_ge(s_ktr, i - 1)
                for b in range(2):
                    kv = bank[2 + b][:].rearrange("p (h n) -> p h n", h=4)
                    v.tensor_copy(kc[:, i % 2, 4 * b:4 * b + 4, 0:NOPE], kv[:, :, 0:NOPE])
                    last = v.tensor_copy(vv[:, i, 4 * b:4 * b + 4, :], kv[:, :, NOPE:NOPE + VH])
                last.then_inc(s_kc, 1)
                if i:
                    dve.wait_ge(s_rot, i)
                link(rotate(lat[:, i:i + 1, Q_LORA + KV_LORA:LAT], i, 1))
                v.tensor_copy(kc[:, i % 2, :, NOPE:QK],
                              lat[:, i:i + 1, Q_LORA + KV_LORA:LAT].to_broadcast([P, HEADS, ROPE]))
                dve.wait_ge(s_qs, i + 1)
                rotate(qs[:, i % 2, :, NOPE:QK], i, HEADS).then_inc(s_rot, 1)

            def read_KT(i):
                dve.wait_ge(s_ktr, i + 1)
                for b in range(2):
                    last = v.tensor_copy(KT[:, 4 * b:4 * b + 4, i * P:(i + 1) * P],
                                         bank[6 + b][0:QK, :].rearrange("p (h t) -> p h t", h=4))
                last.then_inc(s_KT, 1)

            kv_rows(0)
            for i in range(NT):
                if i + 1 < NT:
                    kv_rows(i + 1)
                read_KT(i)

            dve.wait_ge(s_bias, 32)
            dve.wait_ge(s_g1, 32)
            for u in range(STEPS):
                if u < UNITS:
                    i = u // HEADS
                    dve.wait_ge(s_sc, u + 1)
                    b = bank[SCORE_BANK[u % 3]]
                    diag = b[:, i * P:(i + 1) * P]
                    link(v.tensor_tensor(diag, diag, mask[:], ALU.add))
                    v.tensor_reduce(nmax[:, u:u + 1], b[:, 0:(i + 1) * P], AX_X, ALU.max,
                                    negate=True).then_inc(s_max, 1)
                if u < 4 * KH * ADA_ATT:
                    ada_piece(KH * ADA_FIRST + u // 4, u % 4)
                if u >= ATT_ADA + 2 and (u - ATT_ADA - 2) % (4 * KH) == 0:
                    ada_back(ADA_FIRST + (u - ATT_ADA - 2) // (4 * KH))
                if u >= HEADS + 2 and (u - HEADS - 2) % HEADS == 0:
                    i = (u - HEADS - 2) // HEADS
                    dve.wait_ge(s_exp, HEADS * (i + 1))
                    link(v.reciprocal(rinv[:, 8 * i:8 * i + 8], rsum[:, 8 * i:8 * i + 8]))
                    dve.wait_ge(s_pv, HEADS * (i + 1))
                    if i:
                        dve.wait_ge(s_otr, i)
                    v.tensor_tensor(osb[:], bank[4 + i % 2][:].rearrange("p (h n) -> p h n", h=HEADS),
                                    rinv[:, 8 * i:8 * i + 8].unsqueeze(2).to_broadcast([P, HEADS, VH]),
                                    ALU.mult).then_inc(s_o, 1)
                if u >= HEADS + 4 and (u - HEADS - 4) % HEADS == 0:
                    i = (u - HEADS - 4) // HEADS
                    dve.wait_ge(s_oTh, i + 1)
                    v.tensor_tensor(oT[:, 1, :, i * P:(i + 1) * P], bank[4 + i % 2][:].rearrange("p (k t) -> p k t", k=4),
                                    oT[:, 0, :, i * P:(i + 1) * P].bitcast(F32), ALU.subtract).then_inc(s_oT, 1)

            dve.wait_ge(s_bias, 48)
            a0 = KH * (ADA_FIRST + ADA_ATT)
            for c in range(2):
                for _ in range(4 - c):
                    ada_block(a0)
                    a0 += 1
                for g, s in ((0, s_ya), (1, s_yb)):
                    for i in range(NT):
                        dve.wait_ge(s, NT * c + i + 1)
                        dve.wait_ge(s_sg, 2 * NT * c + NT * g + i + 1)
                        r = sg[:, c + g, i, :]
                        last = v.tensor_tensor(r, bank[4 * g + i][:], r, ALU.mult)
                        if g == 0:
                            last.then_inc(s_yad, 1)
                        else:
                            link(last)
                            dve.wait_ge(s_yad, NT * c + i + 1)
                            v.tensor_tensor(sg[:, c, i, :], sg[:, c, i, :], r, ALU.add).then_inc(s_mg, 1)
                    if c == 0 and g == 0:
                        ada_block(a0)
                        a0 += 1
            for i in range(NT):
                low_x(i, i + 1, 2 * (i % 2))
            dve.wait_ge(s_g2, 16)
            for q in range(ADA_FIRST + ADA_ATT, len(CHUNKS)):
                ada_back(q)
            dve.wait_ge(s_mod, len(CHUNKS))
            stage = [2]

            def rstd_row(col):
                stage[0] += 1
                rstd(col, 1, [D], stage[0])

            def residual(i):
                rstd_row(SSZ + i)
                link(scaled(zz[:, i, :], zz[:, i, :], stat[:, SSZ + i:SSZ + i + 1], mod[:, GATE1, :]))
                v.tensor_tensor(h[:, i, :], h[:, i, :], zz[:, i, :], ALU.add).then_inc(s_h1, 1)

            def norm2(i):
                rstd_row(SSH + i)
                scaled(zz[:, i, :], h[:, i, :], stat[:, SSH + i:SSH + i + 1], mod[:, SCALE2, :]).then_inc(s_x2, 1)
                if i >= 2:
                    dve.wait_ge(s_x2, i + 1)
                    v.tensor_tensor(zz[:, i, :], zz[:, i, :], mod[:, SHIFT2, :], ALU.add).then_inc(s_xn[1], 1)

            residual(0)
            residual(1)
            norm2(0)
            residual(2)
            residual(3)
            for i in range(1, NT):
                norm2(i)
            for i in range(NT):
                low_x(i, NT + i + 1, 2 * i)

            def top16(vals, idx, src, n):
                for part in range(2):
                    lo, hi = 8 * part, 8 * part + 8
                    for k in range(n):
                        last = v.max(vals(k)[:, lo:hi], src(k))
                    link(last)
                    for k in range(n):
                        last = v.max_index(idx(k)[:, lo:hi], vals(k)[:, lo:hi], src(k))
                    link(last)
                    if part == 0:
                        for k in range(n):
                            last = v.match_replace(src(k), vals(k)[:, lo:hi], src(k), NEG)
                        link(last)

            for n in range(4):
                sides = [(m % 2) * RH + 2 * n + m // 2 for m in range(4)]
                for m in range(4):
                    dve.wait_ge(s_scr, 4 * n + m + 1)
                    v.tensor_copy(scores[:, :, sides[m], :], bank[4 + m][:].rearrange("p (i k) -> p i k", i=NT)
                                  ).then_inc(s_scs, 1)
                for m in range(4):
                    dve.wait_ge(s_scs, 4 * n + m + 1)
                    if 4 * n + m >= 2:
                        dve.wait_ge(s_top, 4 * n + m - 1)
                    top16(lambda i: top_v[:, i, sides[m], :], lambda i: top_i[:, m % 2, i, :],
                          lambda i: scores[:, i, sides[m], :], NT)
                    v.tensor_copy(top_if[:, :, sides[m], :], top_i[:, m % 2, :, :]).then_inc(s_top, 1)
            dve.wait_ge(s_top, SIDES)

            def spread(t, dim):
                return t.unsqueeze(dim).to_broadcast([P, RH, TOPK, TOPK])

            for i in range(NT):
                if i:
                    dve.wait_ge(s_ge, i)
                link(v.tensor_tensor(cand[:], spread(top_v[:, i, 0:RH, :], 3), spread(top_v[:, i, RH:SIDES, :], 2),
                                     ALU.add))
                top16(lambda k: best_v[:, k, :], lambda k: best_c[:, k, :],
                      lambda k: cand[:, k, :, :].rearrange("p a b -> p (a b)"), RH)
                v.tensor_tensor(gexp[:, 0, :, :], best_v[:], best_v[:, :, 0:1].to_broadcast([P, RH, TOPK]),
                                ALU.subtract).then_inc(s_bv, 1)
                v.tensor_scalar(best_ab[:, 0, :, :], best_c[:], 4, None, ALU.logical_shift_right)
                link(v.tensor_scalar(best_ab[:, 1, :, :], best_c[:], TOPK - 1, None, ALU.bitwise_and))
                link(v.tensor_copy(best_abf[:], best_ab[:]))
                for s in range(2):
                    link(v.tensor_tensor(cand[:], spread(best_abf[:, s, :, :], 3),
                                         iota[:, 0:TOPK].unsqueeze(1).unsqueeze(1).to_broadcast([P, RH, TOPK, TOPK]),
                                         ALU.is_equal))
                    link(v.tensor_tensor(cand[:], cand[:], spread(top_if[:, i, s * RH:(s + 1) * RH, :], 2), ALU.mult))
                    link(v.tensor_reduce(picks[:, s, :], cand[:].rearrange("p h k a -> p (h k) a"), AX_X, ALU.add))
                dve.wait_ge(s_ge, i + 1)
                link(v.tensor_reduce(gsum[:, 0, :], gexp[:, 1, :, :], AX_X, ALU.add))
                link(v.reciprocal(gsum[:, 1, :], gsum[:, 0, :]))
                v.tensor_tensor(picks[:, 2, :].rearrange("p (h k) -> p h k", h=RH), gexp[:, 1, :, :],
                                gsum[:, 1, :].unsqueeze(2).to_broadcast([P, RH, TOPK]), ALU.mult).then_inc(s_pk, 1)
                dve.wait_ge(s_pkt, i + 1)
                link(v.tensor_copy(picksT[:, :, i * P:(i + 1) * P],
                                   bank[6][:, 0:3 * P].rearrange("p (r t) -> p r t", r=3)))
                with dve.Fori(0, E_BESIDE // 2) as it:
                    for turn in range(4):
                        for q in range(QUADS):
                            dve.wait_ge(s_gmm, it * (4 * QUADS) + ((i * TURNS + turn) * QUADS + q + 1))
                            def col(r, t, n=1):
                                return picksT[:, r, bass.ds(it * (16 * QUADS) +
                                                            (i * P + (turn * QUADS + q) * 4 + t), n)]
                            v.tensor_tensor(hot[:, q, :, 0, :], iota[:].unsqueeze(1).to_broadcast([P, 4, P]),
                                            col(1, 0, 4).unsqueeze(2).to_broadcast([P, 4, P]), ALU.is_equal)
                            for t in range(4):
                                last = v.tensor_scalar(hot[:, q, t, 1, :], iota[:], col(0, t), col(2, t),
                                                       ALU.is_equal, ALU.mult)
                            last.then_inc(s_hot, 1)

            def weigh(j, s, act_rows, loads, early_loads=None, add=None):
                dve.wait_ge(s_gl[s], loads)
                if early_loads is not None:
                    dve.wait_ge(s_al[s], early_loads)
                for e in range(2):
                    if early_loads is None:
                        dve.wait_ge(s_gelu, j * 2 + (2 * EARLY + e + 1))
                    v.tensor_tensor(w_full[:, e, :], act_rows[:, s, e, :], g_in[:, s, e, :], ALU.mult).then_inc(s_w, 1)
                    if add:
                        add(2 * e)
                    dve.wait_ge(s_whi, j * 2 + (e + 1))
                    v.tensor_tensor(w_part[:, s, e, 1, :], w_full[:, e, :], w_part[:, s, e, 0, :].bitcast(F32),
                                    ALU.subtract).then_inc(s_wlo, 1)
                    if add:
                        add(2 * e + 1)
                if add:
                    for r in range(4, YJ):
                        add(r)

            def adder(j):
                def add(r):
                    dve.wait_ge(s_y, j * YJ + (r + 1))
                    o = yacc[:, r // 2, (r % 2) * HALF:(r % 2 + 1) * HALF]
                    v.tensor_tensor(o, bank[r % YB][:], o, ALU.add).then_inc(s_yd, 1)
                return add

            dve.wait_ge(s_gmm, QUADS * (1 + NT * TURNS))
            link(v.memset(yacc[:], 0.0))
            v.sem_inc(s_yd, YB)
            weigh(0, 0, gel, 16)
            with dve.Fori(0, FULL // 2 - 1) as it:
                weigh(it * 2 + 1, 1, gel, it * 16 + 16, add=adder(it * 2))
                weigh(it * 2 + 2, 0, gel, it * 16 + 32, add=adder(it * 2 + 1))
            weigh(FULL - 1, 1, gel, 8 * FULL, add=adder(FULL - 2))
            with dve.Fori(0, EARLY // 2) as it:
                for s in range(2):
                    weigh(it * 2 + (FULL + s), s, act_in, it * 16 + (8 * FULL + 16), it * 16 + 16,
                          adder(it * 2 + (FULL + s - 1)))

            def scale_y(i, cols=slice(0, D)):
                return scaled(yacc[:, i, cols], yacc[:, i, cols], stat[:, SSY + i:SSY + i + 1], mod[:, GATE2, cols])

            for i in range(NT):
                for r in range(2 * i, 2 * i + 2):
                    adder(PAIRS - 1)(r)
                if i:
                    rstd_row(SSY + i - 1)
                    scale_y(i - 1).then_inc(s_ys, 1)
            rstd_row(SSY + NT - 1)
            dve.wait_ge(s_hin, 16)
            for c in range(2):
                cols = slice(c * HALF, (c + 1) * HALF)
                link(scale_y(NT - 1, cols))
                v.tensor_tensor(h[:, NT - 1, cols], h[:, NT - 1, cols], yacc[:, NT - 1, cols], ALU.add
                                ).then_inc(s_fin3, 1)

        @block.tensor
        def _(pe):
            def matmul(o, l, r, first, last):
                return nc.tensor.matmul(o, l, r, start=bool(first), stop=bool(last))

            def split(b):
                pe.wait_ge(s_wlo2, b + 1)

            PASSES = ((0, 0), (0, 1), (1, 0))

            def ada_sum(q):
                pe.wait_ge(s_ada, KH * (q + 1))
                vec, half = CHUNKS[q]
                m = mod[:, vec, half * HALF:(half + 1) * HALF]
                matmul(bank[ADA_BANK[q]][:], ones[:], m, True, True).then_inc(s_adp, 1)

            def ada_sum_columns(q):
                pe.wait_ge(s_ada, KH * (q + 1))
                vec, half = CHUNKS[q]
                for k in range(4):
                    col = half * HALF + k * P
                    last = matmul(bank[ADA_BANK[q]][:, 4 * q + k:4 * q + k + 1], mod[:, vec, col:col + P],
                                  ones[:, 0:1], True, True)
                last.then_inc(s_adp, 1)

            def transpose_rows(rows, banks):
                for k in range(ND):
                    last = nc.tensor.transpose(bank[banks + k // 4][:, (k % 4) * P:(k % 4 + 1) * P], rows(k), ident[:])
                return last

            def row_blocks(rows):
                return lambda k: rows[:, k * P:(k + 1) * P]

            pe.wait_ge(s_x, 16 * (NT + 1))
            for i in range(NT):
                pe.wait_ge(s_xs, i + 1)
                transpose_rows(row_blocks(xrow[:, i % 2, :]), 2 * i).then_inc(s_x1tr, 1)

            def project(b0, banks, signal, n=HALF, low_later=False):
                def product(kh, i, k, r, last):
                    xp, wp = PASSES[r]
                    return matmul(bank[banks + i][:, 0:n], (xl if xp else xh)[:, 4 * kh + k, i * P:(i + 1) * P],
                                  w2[:, (b0 + kh) % 2, wp, k, 0:n], kh + k + r == 0, last)

                if low_later:
                    pe.wait_ge(s_whi2, b0 + 1)
                    for i in range(NT):
                        for k in range(4):
                            for r in (0, 2):
                                product(0, i, k, r, False)
                    split(b0)
                    for i in range(NT):
                        for k in range(4):
                            last = product(0, i, k, 1, False)
                    last.then_inc(s_half, 1)
                for kh in range(1 if low_later else 0, KH):
                    split(b0 + kh)
                    for i in range(NT):
                        for k in range(4):
                            for r in range(3):
                                last = product(kh, i, k, r, kh and k == 3 and r == 2)
                        if kh:
                            last.then_inc(signal, 1)
                    if not kh:
                        last.then_inc(s_half, 1)

            pe.wait_ge(s_zero, 1)
            pe.wait_ge(s_xraw, NT)
            for kh in range(KH):
                for q in range(2 * kh, 2 * kh + 2):
                    ada_sum_columns(q)
                split(W_IN + kh)
                for k in range(4):
                    for passes, ready in (((0, 1), s_x1h), ((2,), s_x1l)):
                        pe.wait_ge(ready, 4 * kh + k + 1)
                        for i in range(NT):
                            for r in passes:
                                xp, wp = PASSES[r]
                                last = matmul(bank[i][:], (xl if xp else xh)[:, 4 * kh + k, i * P:(i + 1) * P],
                                              w2[:, kh, wp, k, :], kh + k + r == 0, kh and k == 3 and r == 2)
                            if kh and k == 3 and passes == (2,):
                                last.then_inc(s_xp, 1)
                if not kh:
                    last.then_inc(s_half, 1)
            project(W_IN + KH, 4, s_lp, LAT)

            pe.wait_ge(s_xps, NT)
            pe.wait_ge(s_pool_in, 48)

            def pool(g):
                if g >= 2:
                    pe.wait_ge(s_mx, g - 1)
                for i in range(NT):
                    o = bank[g % 2][:, i * P:(i + 1) * P]
                    last = matmul(o, xpool[:, i, g * P:(g + 1) * P], band[:, 0 if i == 0 else 1, g, :], True, i == 0)
                    if i:
                        last = matmul(o, xpool[:, i - 1, g * P:(g + 1) * P], band[:, 2, g, :], False, True)
                last.then_inc(s_mxp, 1)

            def group_map(g):
                pe.wait_ge(s_mx, g + 1)
                if g >= 2:
                    pe.wait_ge(s_ypT, g - 1)
                matmul(bank[2 + g % 2][:], wgr[:, g, :], mx[:, g % 2, :], True, True).then_inc(s_yp, 1)

            pool(0)
            for g in range(POOL_G):
                if g + 1 < POOL_G:
                    pool(g + 1)
                group_map(g)

            for i in range(NT):
                pe.wait_ge(s_ln, i + 1)
                for k in range(3):
                    last = nc.tensor.transpose(bank[4 + i][:, k * P:(k + 1) * P], lat[:, i, k * P:(k + 1) * P], ident[:])
                last.then_inc(s_ltr, 1)
            pe.wait_ge(s_tab, 16 * 8)
            pe.wait_ge(s_ypT, POOL_G)

            def lift(i):
                tok = slice(i * P, (i + 1) * P)
                pe.wait_ge(s_latT, i + 1)
                if i:
                    pe.wait_ge(s_qs, i)
                for b in range(2):
                    for k in range(2):
                        last = matmul(bank[b][:, 0:4 * QK], latT[:, k, tok], wqu[:, k, b * 4 * QK:(b + 1) * 4 * QK],
                                      k == 0, k == 1)
                last.then_inc(s_qup, 1)
                if i:
                    pe.wait_ge(s_kc, i)
                for b in range(2):
                    last = matmul(bank[2 + b][:], latT[:, 2, tok], wkvu[:, b * HALF:(b + 1) * HALF], True, True)
                last.then_inc(s_kvup, 1)

            def turn(i):
                pe.wait_ge(s_rot, i + 1)
                if i:
                    pe.wait_ge(s_QT, i)
                else:
                    pe.wait_ge(s_latT, NT)
                for hd in range(HEADS):
                    last = nc.tensor.transpose(bank[4 + hd // 4][0:QK, (hd % 4) * P:(hd % 4 + 1) * P],
                                               qs[:, i % 2, hd, :], ident[:])
                last.then_inc(s_qtr, 1)
                if i:
                    pe.wait_ge(s_KT, i)
                for hd in range(HEADS):
                    last = nc.tensor.transpose(bank[6 + hd // 4][0:QK, (hd % 4) * P:(hd % 4 + 1) * P],
                                               kc[:, i % 2, hd, :], ident[:])
                last.then_inc(s_ktr, 1)

            lift(0)
            for i in range(NT):
                if i + 1 < NT:
                    lift(i + 1)
                turn(i)

            pe.wait_ge(s_QT, NT)
            pe.wait_ge(s_KT, NT)
            for u in range(STEPS):
                if u >= ATT_ADA and (u - ATT_ADA) % (4 * KH) == 0:
                    q = ADA_FIRST + (u - ATT_ADA) // (4 * KH)
                    if q > ADA_FIRST:
                        pe.wait_ge(s_mod, q)
                    ada_sum(q)
                if u < UNITS:
                    i, hd = divmod(u, HEADS)
                    if u >= 3:
                        pe.wait_ge(s_exp, u - 2)
                    matmul(bank[SCORE_BANK[u % 3]][:, 0:(i + 1) * P], QT[:, hd, i * P:(i + 1) * P],
                           KT[:, hd, 0:(i + 1) * P], True, True).then_inc(s_sc, 1)
                w = u - 2
                if 0 <= w < UNITS:
                    pe.wait_ge(s_exp, w + 1)
                    if w >= 2:
                        pe.wait_ge(s_prT, w - 1)
                    for k in range(w // HEADS + 1):
                        last = nc.tensor.transpose(bank[2 + w % 2][:, k * P:(k + 1) * P],
                                                   pr[:, w % 2, k * P:(k + 1) * P], ident[:])
                    last.then_inc(s_ptr, 1)
                w = u - 3
                if 0 <= w < UNITS:
                    i, hd = divmod(w, HEADS)
                    pe.wait_ge(s_prT, w + 1)
                    if hd == 0 and i >= 2:
                        pe.wait_ge(s_oT, i - 1)
                    for k in range(i + 1):
                        last = matmul(bank[4 + i % 2][:, hd * VH:(hd + 1) * VH], prT[:, w % 2, k, :], vv[:, k, hd, :],
                                      k == 0, k == i)
                    last.then_inc(s_pv, 1)
                if u >= HEADS + 3 and (u - HEADS - 3) % HEADS == 0:
                    i = (u - HEADS - 3) // HEADS
                    pe.wait_ge(s_o, i + 1)
                    for k in range(4):
                        last = nc.tensor.transpose(bank[4 + i % 2][:, k * P:(k + 1) * P],
                                                   osb[:, 2 * k:2 * k + 2, :].rearrange("p h n -> p (h n)"), ident[:])
                    last.then_inc(s_otr, 1)

            for c in range(2):
                if c:
                    pe.wait_ge(s_yad, NT)
                project(W_MERGE + 6 * c, 0, s_gp, low_later=c == 0)
                if c:
                    pe.wait_ge(s_mg, NT)
                else:
                    pe.wait_ge(s_oT, NT)
                    pe.wait_ge(s_mod, ADA_FIRST + ADA_ATT)
                project(W_MERGE + 6 * c + 2, 4, s_gp)
                for g, (src, signal) in enumerate(((ypT, s_ya), (oT, s_yb))):
                    b = W_MERGE + 6 * c + 4 + g
                    split(b)
                    for i in range(NT):
                        pe.wait_ge(s_sg, 2 * NT * c + NT * g + i + 1)
                        for k in range(4):
                            for r, (xp, wp) in enumerate(PASSES):
                                last = matmul(bank[4 * g + i][:], src[:, xp, k, i * P:(i + 1) * P],
                                              w2[:, b % 2, wp, k, :], k + r == 0, k == 3 and r == 2)
                        last.then_inc(signal, 1)
            for i in range(NT):
                pe.wait_ge(s_mg, NT + i + 1)
                if i >= 2:
                    pe.wait_ge(s_xl, i - 1)
                if i == 0:
                    pe.wait_ge(s_yad, 2 * NT)
                transpose_rows(lambda k: sg[:, k // 4, i, (k % 4) * P:(k % 4 + 1) * P], 2 * (i % 2)).then_inc(s_xtr, 1)
            for q in range(ADA_FIRST + ADA_ATT, len(CHUNKS)):
                ada_sum(q)
            pe.wait_ge(s_xl, NT)

            def out_piece(i, c, kh):
                for k in range(4):
                    for r, (xp, wp) in enumerate(PASSES):
                        last = matmul(bank[4 * c + i][:], (xl if xp else xh)[:, 4 * kh + k, i * P:(i + 1) * P],
                                      w2[:, c, wp, k, :], kh + k + r == 0, kh and k == 3 and r == 2)
                return last

            for c in range(2):
                split(W_OUT + c)
                if c:
                    pe.wait_ge(s_mod, len(CHUNKS))
                for i in range(NT):
                    last = out_piece(i, c, 0)
                last.then_inc(s_half, 1)
            for i, c in OUT_ORDER:
                if i == 0:
                    split(W_OUT + 2 + c)
                out_piece(i, c, 1).then_inc(s_z, 1)
            pe.wait_ge(s_zs, NT)
            for i in range(NT):
                pe.wait_ge(s_xn[i // 2], i % 2 + 1)
                transpose_rows(row_blocks(zz[:, i, :]), 2 * i).then_inc(s_xtr, 1)

            pe.wait_ge(s_xT, 2 * NT)

            def score(n):
                for m in range(4):
                    side = (m % 2) * RH + 2 * n + m // 2
                    pe.wait_ge(s_qT, 4 * n + m + 1)
                    if n:
                        pe.wait_ge(s_scs, 4 * (n - 1) + m + 1)
                    for i in range(NT):
                        last = matmul(bank[4 + m][:, i * P:(i + 1) * P], qT[:, m, i * P:(i + 1) * P],
                                      key_sb[:, side, :], True, True)
                    last.then_inc(s_scr, 1)

            def query(n, kh, m, passes):
                for k in range(4):
                    for r in passes:
                        xp, wp = PASSES[r]
                        last = matmul(bank[m][:], w2[:, (W_QUERY + KH * n + kh) % 2, wp, k, m * P:(m + 1) * P],
                                      (xl if xp else xh)[:, 4 * kh + k, :], kh + k + r == 0,
                                      kh and k == 3 and r == 2)
                return last

            for n in range(4):
                for kh in range(KH):
                    split(W_QUERY + KH * n + kh)
                    if n + kh == 0:
                        for m in range(4):
                            pe.wait_ge(s_xl, NT + m // 2 + 1)
                            query(0, 0, m, (0, 1))
                        pe.wait_ge(s_xl, 2 * NT)
                    for m in range(4):
                        if n and not kh:
                            pe.wait_ge(s_qT, 4 * (n - 1) + m + 1)
                        last = query(n, kh, m, range(3) if n + kh else (2,))
                        if kh:
                            last.then_inc(s_q, 1)
                    if not kh:
                        last.then_inc(s_half, 1)
                if n == 0:
                    pe.wait_ge(s_key, 16)
                score(n)

            def activate(k, e):
                pe.wait_ge(s_ulo, k + 1)
                b = bank[4 + e]
                for d in range(ND):
                    matmul(b[:], u_part[:, e, 0, d, :], xh[:, d, :], d == 0, False)
                    matmul(b[:], u_part[:, e, 0, d, :], xl[:, d, :], False, False)
                    last = matmul(b[:], u_part[:, e, 1, d, :], xh[:, d, :], False, d == ND - 1)
                last.then_inc(s_act, 1)

            def early_pairs(n0, count):
                with pe.Fori(0, count // 2) as it:
                    for t in range(4):
                        activate(it * 4 + (2 * n0 + t), t % 2)

            pe.wait_ge(s_scs, SIDES)
            early_pairs(0, E_FIRST)
            n0 = E_FIRST
            for i in range(NT):
                pe.wait_ge(s_pk, i + 1)
                for r in range(3):
                    last = nc.tensor.transpose(bank[6][:, r * P:(r + 1) * P], picks[:, r, :], ident[:])
                last.then_inc(s_pkt, 1)
                if i == 0:
                    nc.tensor.sem_inc(s_gmm, QUADS)
                with pe.Fori(0, E_BESIDE // 2) as it:
                    for turn in range(4):
                        activate(it * 4 + (2 * n0 + turn), turn % 2)
                        for q in range(QUADS):
                            done = it * (4 * QUADS) + ((i * TURNS + turn) * QUADS + q + 1)
                            pe.wait_ge(s_hot, done)
                            pe.wait_ge(s_gev, done)
                            for t in range(4):
                                last = matmul(bank[q][:, t * P:(t + 1) * P], hot[:, q, t, 0, :], hot[:, q, t, 1, :],
                                              True, True)
                            last.then_inc(s_gmm, 1)
                n0 += E_BESIDE
                count = E_BETWEEN if i + 1 < NT else E_TAIL
                early_pairs(n0, count)
                n0 += count
            pe.wait_ge(s_gev, QUADS * (1 + NT * TURNS))

            def combine(j, s):
                pe.wait_ge(s_wlo, j * 2 + 2)
                pe.wait_ge(s_vlo, j * 2 + 2)
                for r in range(YJ):
                    pe.wait_ge(s_yd, j * YJ + (r + 1))
                    b = bank[r % YB]
                    tok = slice((r // 2) * P, (r // 2 + 1) * P)
                    col = slice((r % 2) * HALF, (r % 2 + 1) * HALF)
                    for e in range(2):
                        matmul(b[:], w_part[:, s, e, 0, tok], v_part[:, s, e, 0, col], e == 0, False)
                        matmul(b[:], w_part[:, s, e, 0, tok], v_part[:, s, e, 1, col], False, False)
                        last = matmul(b[:], w_part[:, s, e, 1, tok], v_part[:, s, e, 0, col], False, e == 1)
                    last.then_inc(s_y, 1)

            def activate_pair(j):
                for e in range(2):
                    activate(j * 2 + (2 * EARLY + e), e)

            activate_pair(0)
            with pe.Fori(0, FULL // 2 - 1) as it:
                activate_pair(it * 2 + 1)
                combine(it * 2, 0)
                activate_pair(it * 2 + 2)
                combine(it * 2 + 1, 1)
            activate_pair(FULL - 1)
            combine(FULL - 2, 0)
            combine(FULL - 1, 1)
            with pe.Fori(0, EARLY // 2) as it:
                for s in range(2):
                    combine(it * 2 + (FULL + s), s)


def kernel(**inputs):
    import numpy as np
    import concourse.bacc as bacc
    from concourse.bass_utils import run_bass_kernel_spmd

    a = {k: np.ascontiguousarray(v) for k, v in inputs.items()}
    f = np.float32

    def blocks(w, n_chunks=None):
        rows, cols = w.shape
        b = w.reshape(rows // HALF, 4, P, cols // HALF, HALF).transpose(3, 0, 2, 1, 4)
        return b.reshape(cols // HALF, rows // HALF, P, 4 * HALF)

    def stream():
        ada = blocks(a["w_ada"][0])
        w_in = a["w_in"][0]
        pool_w = blocks(w_in[:, 0:HALF])
        lat_w = np.zeros((D, HALF), w_in.dtype)
        lat_w[:, 0:LAT] = w_in[:, HALF:HALF + LAT]
        gates = blocks(w_in[:, HALF + LAT:])
        pool_o, mla_o = blocks(a["w_pool_o"][0]), blocks(a["w_mla_o"][0])
        modulation = np.concatenate([ada[2 * vec + half] for vec, half in CHUNKS])
        parts = [pool_w[0], blocks(lat_w)[0]]
        for c in range(2):
            parts += [gates[c], gates[2 + c], pool_o[c], mla_o[c]]
        parts += list(blocks(a["w_out"][0]).transpose(1, 0, 2, 3)) + list(blocks(a["w_query"][0]))
        weights = np.concatenate(parts)
        return np.stack([(modulation if kind == "A" else weights)[i] for kind, i in STREAM])

    def tables():
        band = np.zeros((P, 3, POOL_G, P), f)
        for g, w in enumerate((2, 4, 8, 16)):
            for t in range(P):
                for s in range(max(0, t - w + 1), t + 1):
                    band[s, 0, g, t] = f(1) / f(min(t + 1, w))
                    band[s, 1, g, t] = f(1) / f(w)
                for s in range(t - w + 1, 0):
                    band[P + s, 2, g, t] = f(1) / f(w)
                band[t, 0:2, g, t] -= f(1)
        inv = f(1) / (f(10000.0) ** (np.arange(0, ROPE, 2, dtype=f) / f(ROPE)))
        ang = np.arange(SEQ, dtype=f)[:, None] * inv[None, :].astype(f)
        cos, sin = np.cos(ang).astype(f), np.sin(ang).astype(f)
        cos = np.concatenate([cos, cos], 1).reshape(NT, P, ROPE).transpose(1, 0, 2)
        sin = np.concatenate([-sin, sin], 1).reshape(NT, P, ROPE).transpose(1, 0, 2)
        mask = np.where(np.arange(P)[None, :] <= np.arange(P)[:, None], f(0), f(-1e30)).astype(f)
        return band, cos, sin, mask

    band, cos, sin, mask = tables()
    k12 = np.concatenate([a["sub_keys1"][0], a["sub_keys2"][0]], axis=0)
    ins = [
        ("x", a["x"][0]),
        ("c_col", a["c"][0].reshape(ND, P).T),
        ("b_ada", a["b_ada"][0].reshape(6, D)),
        ("g_pre1", a["g_pre1"][0].reshape(ND, P).T), ("g_post1", a["g_post1"]), ("g_pre2", a["g_pre2"]), ("g_post2", a["g_post2"]),
        ("g_q", a["g_q_lat"]), ("g_kv", a["g_kv_lat"]),
        ("wstream", stream()),
        ("w_q_up", a["w_q_up"][0].reshape(2, P, HEADS * QK).transpose(1, 0, 2)),
        ("w_kv_up", a["w_kv_up"][0]),
        ("w_group", a["w_pool_group"][0].transpose(1, 0, 2)),
        ("pool_scale", a["pool_scale"][0].reshape(POOL_G, P).T),
        ("keys", k12.transpose(2, 0, 1)),
        ("pool_band", band), ("rope_cos", cos), ("rope_sin", sin),
        ("ident", np.eye(P, dtype=f)), ("mask", mask),
        ("iota", np.broadcast_to(np.arange(P, dtype=f), (P, P))),
        ("expert_u", a["expert_u"][0].reshape(PAIRS, 2, P, ND, P).transpose(0, 4, 1, 3, 2).reshape(PAIRS, P, 2, D)),
        ("expert_v", a["expert_v"][0].reshape(PAIRS, 2, P, D).transpose(0, 2, 1, 3)),
    ]
    nc = bacc.Bacc("TRN2", target_bir_lowering=False, num_devices=1)
    arrays, args = {}, []
    for name, v in ins:
        v = np.ascontiguousarray(v)
        arrays[f"in_{name}"] = v
        args.append(nc.dram_tensor(f"in_{name}", v.shape, mybir.dt.from_np(v.dtype), kind="ExternalInput").ap())
    args.append(nc.dram_tensor("out_0", (SEQ, D), F32, kind="ExternalOutput").ap())
    build(nc, *args)
    r = run_bass_kernel_spmd(nc, [arrays], core_ids=[0])
    return r.results[0]["out_0"].reshape(1, SEQ, D)
```
